# Optimizing a Trainium2 kernel written in Bass

```python
import jax, jax.numpy as jnp
from jax import lax
import numpy as np

D_MODEL = 1024
BATCH = 1
SEQ = 256
DEPTH = 2
DEC_BATCH = 8
DEC_SEQ = 4
PAST_LEN = 1024
PAGE_SIZE = 128

HEAD_DIM = 64
DIL_PAIRS = ((128, 1), (512, 4), (2048, 16))
N_DIL = len(DIL_PAIRS)
H_A = D_MODEL // 2 // HEAD_DIM
H_B = D_MODEL // 2 // HEAD_DIM
H_BKV = 2
G_B = H_B // H_BKV
SWA_WINDOW = 128
H_R = 4
DK_R = D_MODEL // H_R
DV_R = 2 * DK_R
RET_CHUNK = 128
D_FF = 4 * D_MODEL
ROPE_THETA = 10000.0
BLOCK = 128
NORM_EPS = 1e-6
GN_EPS = 1e-5
NEG_INF = -1e30
N_EVEN = (DEPTH + 1) // 2
N_ODD = DEPTH // 2
A_COLS = N_DIL * 3 * H_A * HEAD_DIM
B_Q = H_B * HEAD_DIM
B_KV = H_BKV * HEAD_DIM
MIX_IN = A_COLS + B_Q + 2 * B_KV
MIX_OUT = (H_A + H_B) * HEAD_DIM
RET_QK = H_R * DK_R
RET_V = H_R * DV_R
RET_IN = 2 * RET_QK + 2 * RET_V

kernel_name = 'hybrid_dilated_swa_retention_decoder_step'

def _rmsnorm(x, g):
    xf = x.astype(jnp.float32)
    y = xf * lax.rsqrt(jnp.mean(xf * xf, axis=-1, keepdims=True) + NORM_EPS)
    return (y * g.astype(jnp.float32)).astype(x.dtype)

def _rope(x, pos):
    dh = x.shape[-1]
    half = dh // 2
    inv = ROPE_THETA ** (-jnp.arange(half, dtype=jnp.float32) * (2.0 / dh))
    ang = jnp.asarray(pos, jnp.float32)[:, None] * inv[None, :]
    ang = ang.reshape((x.shape[1],) + (1,) * (x.ndim - 3) + (half,))
    c, s = jnp.cos(ang), jnp.sin(ang)
    xf = x.astype(jnp.float32)
    x1, x2 = xf[..., :half], xf[..., half:]
    return jnp.concatenate([x1 * c - x2 * s, x2 * c + x1 * s], axis=-1).astype(x.dtype)

def _attend(q, k, v, mask, sink=None):
    qf = q.astype(jnp.float32) * (q.shape[-1] ** -0.5)
    s = jnp.einsum('...qhgd,...khd->...hgqk', qf, k.astype(jnp.float32))
    s = jnp.where(mask, s, NEG_INF)
    m = jnp.max(s, axis=-1)
    if sink is not None:
        sk = sink.astype(jnp.float32)[:, :, None]
        m = jnp.maximum(m, sk)
    p = jnp.exp(s - m[..., None])
    l = jnp.sum(p, axis=-1)
    if sink is not None:
        l = l + jnp.exp(sk - m)
    o = jnp.einsum('...hgqk,...khd->...qhgd', p, v.astype(jnp.float32))
    l_q = jnp.moveaxis(l, -1, -3)
    o = o / l_q[..., None]
    lse = jnp.moveaxis(m, -1, -3) + jnp.log(l_q)
    return o.astype(q.dtype), lse

def _banded(q, k, v, window_back, sink=None):
    N, L, Hk, G, Dh = q.shape
    nb = -(-L // BLOCK)
    Lp = nb * BLOCK
    qb = jnp.pad(q, ((0, 0), (0, Lp - L), (0, 0), (0, 0), (0, 0))).reshape(N, nb, BLOCK, Hk, G, Dh)

    def blocks(x):
        xp = jnp.pad(x, ((0, 0), (BLOCK, Lp - L), (0, 0), (0, 0)))
        return jnp.concatenate([xp[:, :Lp].reshape(N, nb, BLOCK, Hk, Dh),
                                xp[:, BLOCK:].reshape(N, nb, BLOCK, Hk, Dh)], axis=2)

    kb, vb = blocks(k), blocks(v)
    blk = np.arange(nb)[:, None, None]
    i = np.arange(BLOCK)[None, :, None]
    j = np.arange(2 * BLOCK)[None, None, :]
    diff = i + BLOCK - j
    mask = (diff >= 0) & (diff <= window_back) & (blk * BLOCK - BLOCK + j >= 0)
    mask = mask[None, :, None, None]
    o, lse = _attend(qb, kb, vb, mask, sink)
    return o.reshape(N, Lp, Hk, G, Dh)[:, :L], lse.reshape(N, Lp, Hk, G)[:, :L]

def _dilated_prompt(q, k, v, dil, span):
    N, S, H, Dh = q.shape
    Ls = S // dil

    def to_res(x):
        return x.reshape(N, Ls, dil, H, Dh).swapaxes(1, 2).reshape(N * dil, Ls, H, Dh)

    o, lse = _banded(to_res(q)[:, :, :, None], to_res(k), to_res(v), span)
    o = o[:, :, :, 0].reshape(N, dil, Ls, H, Dh).swapaxes(1, 2).reshape(N, S, H, Dh)
    lse = lse[:, :, :, 0].reshape(N, dil, Ls, H).swapaxes(1, 2).reshape(N, S, H)
    return o, lse

def _ab_project(h, w_in, pos):
    N, L, _ = h.shape
    z = h @ w_in
    za = z[..., :A_COLS].reshape(N, L, N_DIL, 3, H_A, HEAD_DIM)
    qa = _rope(za[:, :, :, 0], pos)
    ka = _rope(za[:, :, :, 1], pos)
    va = za[:, :, :, 2]
    zb = z[..., A_COLS:]
    qb = _rope(zb[..., :B_Q].reshape(N, L, H_BKV, G_B, HEAD_DIM), pos)
    kb = _rope(zb[..., B_Q:B_Q + B_KV].reshape(N, L, H_BKV, HEAD_DIM), pos)
    vb = zb[..., B_Q + B_KV:].reshape(N, L, H_BKV, HEAD_DIM)
    return qa, ka, va, qb, kb, vb

def _ab_merge(oa_list, lse_list, ob, w_out):
    lse = jnp.stack(lse_list, axis=2)
    wts = jax.nn.softmax(lse, axis=2)
    oa = jnp.sum(wts[..., None] * jnp.stack(oa_list, axis=2).astype(jnp.float32), axis=2).astype(ob.dtype)
    N, L = oa.shape[:2]
    y = jnp.concatenate([oa.reshape(N, L, H_A * HEAD_DIM), ob.reshape(N, L, H_B * HEAD_DIM)], axis=-1)
    return y @ w_out

def _ab_prompt(h, pos, w_in, w_out, sinks):
    S = h.shape[1]
    qa, ka, va, qb, kb, vb = _ab_project(h, w_in, pos)
    oa_list, lse_list, rows = [], [], []
    for g, (win, dil) in enumerate(DIL_PAIRS):
        o, lse = _dilated_prompt(qa[:, :, g], ka[:, :, g], va[:, :, g], dil, win // dil)
        oa_list.append(o)
        lse_list.append(lse)
        wb = min(win, S)
        rows.append(jnp.stack([ka[:, S - wb:, g], va[:, S - wb:, g]], axis=2))
    ob, _ = _banded(qb, kb, vb, SWA_WINDOW - 1, sinks.reshape(H_BKV, G_B))
    wb = min(SWA_WINDOW, S)
    swa_rows = jnp.stack([kb[:, S - wb:], vb[:, S - wb:]], axis=2)
    return _ab_merge(oa_list, lse_list, ob, w_out), rows, swa_rows

def _ab_sample(h, pos, dil_caches, cache_swa, w_in, w_out, sinks):
    T = h.shape[1]
    qa, ka, va, qb, kb, vb = _ab_project(h, w_in, pos)
    oa_list, lse_list, rows = [], [], []
    for g, (win, dil) in enumerate(DIL_PAIRS):
        cache = dil_caches[g]
        wb = cache.shape[1]
        m = np.arange(win // dil + 1)
        idx = wb + np.arange(T)[:, None] - dil * m[None, :]
        from_new = idx >= wb
        valid = idx >= 0
        kv_new = jnp.stack([ka[:, :, g], va[:, :, g]], axis=2)
        g_cache = cache[:, np.clip(idx, 0, wb - 1)]
        g_new = kv_new[:, np.clip(idx - wb, 0, T - 1)]
        kv = jnp.where(from_new[None, :, :, None, None, None], g_new, g_cache)
        mask = valid.reshape(1, T, 1, 1, 1, -1)
        o, lse = _attend(qa[:, :, g][:, :, None, :, None, :], kv[:, :, :, 0], kv[:, :, :, 1], mask)
        oa_list.append(o[:, :, 0, :, 0])
        lse_list.append(lse[:, :, 0, :, 0])
        rows.append(kv_new)
    wb = cache_swa.shape[1]
    kc = jnp.concatenate([cache_swa[:, :, 0], kb], axis=1)
    vc = jnp.concatenate([cache_swa[:, :, 1], vb], axis=1)
    kpos = PAST_LEN - wb + np.arange(wb + T)
    diff = np.asarray(pos)[:, None] - kpos[None, :]
    mask = ((diff >= 0) & (diff <= SWA_WINDOW - 1))[None, None, None]
    ob, _ = _attend(qb, kc, vc, mask, sinks.reshape(H_BKV, G_B))
    swa_rows = jnp.stack([kb, vb], axis=2)
    return _ab_merge(oa_list, lse_list, ob, w_out), rows, swa_rows

def _retention(q, k, v, state):
    N, L, H, Dk = q.shape
    Dv = v.shape[-1]
    C = RET_CHUNK if L % RET_CHUNK == 0 else L
    nc = L // C
    log_g = jnp.log(1.0 - 2.0 ** (-5.0 - jnp.arange(H, dtype=jnp.float32)))
    ii = jnp.arange(C, dtype=jnp.float32)
    diff = ii[:, None] - ii[None, :]
    decay = jnp.where(diff >= 0, jnp.exp(jnp.maximum(diff, 0.0)[None] * log_g[:, None, None]), 0.0)
    q_dec = jnp.exp((ii + 1.0)[:, None] * log_g[None, :])
    k_dec = jnp.exp((C - 1.0 - ii)[:, None] * log_g[None, :])
    c_dec = jnp.exp(C * log_g)

    def to_chunks(x):
        return x.astype(jnp.float32).reshape(N, nc, C, H, x.shape[-1]).swapaxes(0, 1)

    def step(S, xs):
        qc, kc, vc = xs
        a = jnp.einsum('nihd,njhd->nhij', qc, kc) * decay[None]
        o = (jnp.einsum('nhij,njhe->nihe', a, vc)
             + jnp.einsum('nihd,nhde->nihe', qc * q_dec[None, :, :, None], S))
        S = c_dec[None, :, None, None] * S + jnp.einsum('njhd,njhe->nhde', kc * k_dec[None, :, :, None], vc)
        return S, o

    S, o = lax.scan(step, state.astype(jnp.float32), (to_chunks(q), to_chunks(k), to_chunks(v)))
    return o.swapaxes(0, 1).reshape(N, L, H, Dv), S

def _ret_mixer(h, pos, state, w_in, w_out):
    N, L, _ = h.shape
    z = h @ w_in
    q = _rope(z[..., :RET_QK].reshape(N, L, H_R, DK_R), pos)
    k = _rope(z[..., RET_QK:2 * RET_QK].reshape(N, L, H_R, DK_R), pos) * (DK_R ** -0.5)
    v = z[..., 2 * RET_QK:2 * RET_QK + RET_V].reshape(N, L, H_R, DV_R)
    gate = z[..., 2 * RET_QK + RET_V:]
    o, S = _retention(q, k, v, state)
    mu = jnp.mean(o, axis=-1, keepdims=True)
    var = jnp.mean(jnp.square(o - mu), axis=-1, keepdims=True)
    o = (o - mu) * lax.rsqrt(var + GN_EPS)
    y = (jax.nn.silu(gate.astype(jnp.float32)) * o.reshape(N, L, RET_V)).astype(h.dtype)
    return y @ w_out, S

def _mlp(h, w1, w2):
    a = jax.nn.relu(h @ w1)
    return (a * a) @ w2

def setup_inputs(seed: int = 0) -> dict:
    key = jax.random.key(seed)
    ks = jax.random.split(key, 15)

    def nrm(k, shape, scale):
        return jax.random.normal(k, shape, jnp.float32) * scale

    return {
        'x_prompt': nrm(ks[0], (BATCH, SEQ, D_MODEL), 1.0),
        'x_sample': nrm(ks[1], (DEC_BATCH, DEC_SEQ, D_MODEL), 1.0),
        'cache_dil_w128': nrm(ks[2], (N_EVEN, DEC_BATCH, min(DIL_PAIRS[0][0], PAST_LEN), 2, H_A, HEAD_DIM), 1.0),
        'cache_dil_w512': nrm(ks[3], (N_EVEN, DEC_BATCH, min(DIL_PAIRS[1][0], PAST_LEN), 2, H_A, HEAD_DIM), 1.0),
        'cache_dil_w2048': nrm(ks[4], (N_EVEN, DEC_BATCH, min(DIL_PAIRS[2][0], PAST_LEN), 2, H_A, HEAD_DIM), 1.0),
        'cache_swa': nrm(ks[5], (N_EVEN, DEC_BATCH, min(SWA_WINDOW, PAST_LEN), 2, H_BKV, HEAD_DIM), 1.0),
        'state_ret': nrm(ks[6], (N_ODD, DEC_BATCH, H_R, DK_R, DV_R), 0.5),
        'norm_gains': 1.0 + nrm(ks[7], (DEPTH, 4, D_MODEL), 0.05),
        'w_in_mix': nrm(ks[8], (N_EVEN, D_MODEL, MIX_IN), D_MODEL ** -0.5),
        'w_out_mix': nrm(ks[9], (N_EVEN, MIX_OUT, D_MODEL), MIX_OUT ** -0.5),
        'attn_sinks': nrm(ks[10], (N_EVEN, H_B), 1.0),
        'w_in_ret': nrm(ks[11], (N_ODD, D_MODEL, RET_IN), D_MODEL ** -0.5),
        'w_out_ret': nrm(ks[12], (N_ODD, RET_V, D_MODEL), RET_V ** -0.5),
        'w_ff1': nrm(ks[13], (DEPTH, D_MODEL, D_FF), D_MODEL ** -0.5),
        'w_ff2': nrm(ks[14], (DEPTH, D_FF, D_MODEL), D_FF ** -0.5),
    }

def reference(x_prompt, x_sample, cache_dil_w128, cache_dil_w512, cache_dil_w2048, cache_swa, state_ret,
              norm_gains, w_in_mix, w_out_mix, attn_sinks, w_in_ret, w_out_ret, w_ff1, w_ff2):
    xp, xs = x_prompt, x_sample
    dil_caches = (cache_dil_w128, cache_dil_w512, cache_dil_w2048)
    dil_p = [[] for _ in DIL_PAIRS]
    dil_s = [[] for _ in DIL_PAIRS]
    swa_p, swa_s, ret_p, ret_s = [], [], [], []
    pos_p = np.arange(xp.shape[1])
    pos_s = PAST_LEN + np.arange(xs.shape[1])
    for layer in range(DEPTH):
        gn = norm_gains[layer]
        hp = _rmsnorm(xp, gn[0])
        hs = _rmsnorm(xs, gn[0])
        if layer % 2 == 0:
            e = layer // 2
            mp, rows_p, sw_p = _ab_prompt(hp, pos_p, w_in_mix[e], w_out_mix[e], attn_sinks[e])
            ms, rows_s, sw_s = _ab_sample(hs, pos_s, [c[e] for c in dil_caches], cache_swa[e],
                                          w_in_mix[e], w_out_mix[e], attn_sinks[e])
            for g in range(N_DIL):
                dil_p[g].append(rows_p[g])
                dil_s[g].append(rows_s[g])
            swa_p.append(sw_p)
            swa_s.append(sw_s)
        else:
            o = layer // 2
            zero_state = jnp.zeros((xp.shape[0], H_R, DK_R, DV_R), jnp.float32)
            mp, st_p = _ret_mixer(hp, pos_p, zero_state, w_in_ret[o], w_out_ret[o])
            ms, st_s = _ret_mixer(hs, pos_s, state_ret[o], w_in_ret[o], w_out_ret[o])
            ret_p.append(st_p.astype(state_ret.dtype))
            ret_s.append(st_s.astype(state_ret.dtype))
        xp = xp + _rmsnorm(mp, gn[1])
        xs = xs + _rmsnorm(ms, gn[1])
        xp = xp + _rmsnorm(_mlp(_rmsnorm(xp, gn[2]), w_ff1[layer], w_ff2[layer]), gn[3])
        xs = xs + _rmsnorm(_mlp(_rmsnorm(xs, gn[2]), w_ff1[layer], w_ff2[layer]), gn[3])
    return (xp, xs,
            jnp.stack(dil_p[0]), jnp.stack(dil_s[0]),
            jnp.stack(dil_p[1]), jnp.stack(dil_s[1]),
            jnp.stack(dil_p[2]), jnp.stack(dil_s[2]),
            jnp.stack(swa_p), jnp.stack(swa_s),
            jnp.stack(ret_p), jnp.stack(ret_s))


_drawn_inputs = setup_inputs


def setup_inputs(seed=0):
    import zlib

    import numpy as np

    out = dict(_drawn_inputs(seed))
    spreads = {}
    factors = {}
    for name, (base, spread) in spreads.items():
        noise = np.random.default_rng([zlib.crc32(name.encode()), seed]).standard_normal(out[name].shape)
        drawn = base * np.exp(spread * noise) if base else spread * noise
        out[name] = __import__('jax').numpy.asarray(drawn.astype(out[name].dtype))
    for name, factor in factors.items():
        out[name] = (out[name] * factor).astype(out[name].dtype)
    return out
```

```python
from contextlib import ExitStack

import numpy as np

import concourse.bass as bass
from concourse import mybir

F32 = mybir.dt.float32
F32R = mybir.dt.float32r
ALU = mybir.AluOpType
ACT = mybir.ActivationFunctionType
AX = mybir.AxisListType
ds = bass.ds

P = 128
D = 1024
KT = D // P
SEQ = 256
NB, NT = 8, 4
NS = NB * NT
T = SEQ + NS
PAST = 1024
HD = 64
HALF = HD // 2
NH = 8
NG = 3
DILS = (1, 4, 16)
WINS = (128, 512, 2048)
NBR = NG + 1
NHR, DK, DV = 4, 256, 512
DFF = 4 * D
SC = 256
RAWS = 4
SPL = 2
EPS = 1e-6
GN_EPS = 1e-5
NEG = -1e30
SCALE = HD ** -0.5
CT = 2
CSLOTS = 4

N_Q, N_KV, N_BKV, N_MIXOUT, N_FF, N_RETIN, N_RETOUT = 8, 12, 1, 4, 16, 24, 8
S_Q = 0
S_KV = S_Q + N_Q
S_BKV = S_KV + N_KV
S_MIXOUT = S_BKV + N_BKV
S_FF1A = S_MIXOUT + N_MIXOUT
S_FF2A = S_FF1A + N_FF
S_RETIN = S_FF2A + N_FF
S_RETOUT = S_RETIN + N_RETIN
S_FF1B = S_RETOUT + N_RETOUT
S_FF2B = S_FF1B + N_FF
N_STRIPS = S_FF2B + N_FF

C_GAIN = 0
C_SINKP = C_GAIN + 64
C_SINKD = C_SINKP + 16
C_KDEC = C_SINKD + 4
C_EPS = C_KDEC + 8
C_GNEPS = C_EPS + 1
N_COL = C_GNEPS + 1
GAMMA = [1.0 - 2.0 ** (-5.0 - h) for h in range(NHR)]




def build_program(nc, wst, x_in, cols, trig, mats, pmask, dmask, rmask, qkdec, kcache, vcache, state,
                  x_out, k_out, v_out, pstate_out, sstate_out):
    with ExitStack() as ctx:
        def sem(name):
            return ctx.enter_context(nc.semaphore(name))

        def sb(name, shape, dt=F32, scope=ctx):
            return scope.enter_context(nc.sbuf_tensor(name, shape, dt))

        raw = sb("raw", [P, RAWS, KT * SC])
        wH = sb("wH", [P, SPL, KT * SC], F32R)
        wL = sb("wL", [P, SPL, KT * SC], F32R)
        x = sb("x", [P, KT, T])
        hH = sb("hH", [P, KT, T], F32R)
        hL = sb("hL", [P, KT, T], F32R)
        y = sb("y", [P, KT, T])
        sq = sb("sq", [P, 2, T])
        acc = sb("acc", [P, 2, T])
        sumsq = sb("sumsq", [P, T])
        rms = sb("rms", [P, T])
        rs_post = sb("rs_post", [P, T])
        rs_pre = sb("rs_pre", [P, T])
        tmp = sb("tmp", [P, 2, T])
        trig_sb = sb("trig_sb", [P, 2, T])
        trigR = sb("trigR", [P, 2, T])
        col = sb("col", [P, N_COL])
        mat = sb("mat", [P, 7, P])

        NVT = 4 * NG + 1
        with ExitStack() as mix:
            qT = sb("qT", [P, 4 * NBR, T], F32, mix)
            kT = sb("kT", [P, 4 * NBR, T], F32, mix)
            vtok = sb("vtok", [P, 2, NVT * P], F32, mix)
            vnew = [a.rearrange("p a t -> p (a t)") for a in (sq[:, :, :], acc[:, :, :], tmp[:, :, :])] + [rms[:, :]]
            pm = sb("pm", [P, NBR, 2 * P], F32, mix)
            dm = sb("dm", [P, 640], F32, mix)
            cslot = sb("cslot", [P, CSLOTS, CT * 512], F32, mix)
            with ExitStack() as s1:
                vT = sb("vT", [P, NVT, T], F32, s1)
                kz = sb("kz", [P, T], F32, s1)
            with ExitStack() as s2:
                p_sb = sb("p_sb", [P, 2, 9 * P], F32, s2)
                pt_sb = sb("pt_sb", [P, 3, 3 * P], F32, s2)
                small = sb("small", [P, 2, 10], F32, s2)
            with ExitStack() as s3:
                st_sb = sb("st_sb", [P, 2, 512], F32, s3)
                sp_sb = sb("sp_sb", [P, 2, 640], F32, s3)
                ptn_sb = sb("ptn_sb", [NS, 2, 512], F32, s3)
                dsm = sb("dsm", [P, 24], F32, s3)
            qbd = y[:, :, :].rearrange("p k t -> p (k t)")[:, 0:16 * P].rearrange("p (a c) -> p a c", c=P)
        with ExitStack() as ffs:
            aH = sb("aH", [P, 4 * KT, T], F32R, ffs)
            aL = sb("aL", [P, 4 * KT, T], F32R, ffs)
            relu_sb = sb("relu_sb", [P, 2, 2, T], F32, ffs)
            a_sb = sb("a_sb", [P, 2, T], F32, ffs)
        with ExitStack() as ret:
            with ExitStack() as r1:
                vTr = sb("vTr", [P, 4 * NHR, T], F32, r1)
                gate = sb("gate", [P, 4 * NHR, T], F32, r1)
            with ExitStack() as r2:
                yH = sb("yH", [P, 4 * NHR, T], F32R, r2)
                yL = sb("yL", [P, 4 * NHR, T], F32R, r2)
                qr = sb("qr", [P, 2 * NHR, T], F32, r2)
                kr = sb("kr", [P, 2 * NHR, T], F32, r2)
                sslot = sb("sslot", [P, 4, 2 * DV], F32, r2)
                vtok_r = sb("vtok_r", [P, 2, DV], F32, r2)
                ktok_r = sb("ktok_r", [P, 2, DK], F32, r2)
                vpad = sb("vpad", [P, 4, 8, NS], F32, r2)
                kpad = sb("kpad", [P, 2, 8, NS], F32, r2)
                rm = sb("rm", [P, NHR, T], F32, r2)
                dec = sb("dec", [P, 2, NHR, NS], F32, r2)
            vtok_s = sq[0:NS, :, :].rearrange("p a t -> p (a t)")[:, 0:DV]
            at_sb = trig_sb[:, :, :].rearrange("p a t -> p (a t)")[:, 0:13 * NS]
            qkd = trigR[:, :, :].rearrange("p a t -> p (a t)")[:, 0:16 * NS].rearrange("p (a h c) -> p a h c", a=2, h=8)
            kst = hH[:, :, :].rearrange("p k t -> p (k t)")[:, 0:2 * DK].rearrange("p (a c) -> p a c", c=DK)
            vst = hL[:, :, :].rearrange("p k t -> p (k t)")[:, 0:2 * DV].rearrange("p (a c) -> p a c", c=DV)
            o_sb = y[:, 0:4, :]
            oc_sb = y[:, 4:8, :]
            ps_sb = [a[:, :, :].rearrange("p a t -> p (a t)")[:, 0:DV] for a in (tmp, acc)]

        banks = ctx.enter_context(nc.psum_tensor("banks", [P, 8, 512], F32))

        def G(j):
            return banks[:, 2 * (j % 2):2 * (j % 2) + 2, 0:T]

        def both(a):
            return a.unsqueeze(1).broadcast_to([P, 2, T])

        ident, mean_d, mean_v = mat[:, 0, :], mat[:, 1, :], mat[:, 2, :]
        MS = banks[:, 7, 0:T]
        S45 = banks[:, 4:6, :].rearrange("p a c -> p (a c)")
        eps, gn_eps = col[:, C_EPS:C_EPS + 1], col[:, C_GNEPS:C_GNEPS + 1]

        def gain(layer, norm, k):
            c = C_GAIN + (4 * layer + norm) * KT + k
            return col[:, c:c + 1]

        const_in, x_landed, trig_in, mask_in, rmask_in = map(
            sem, ("const_in", "x_landed", "trig_in", "mask_in", "rmask_in"))
        w_landed = [sem(f"w_landed{i}") for i in range(RAWS)]
        h_round, l_split, strip_used = map(sem, ("h_round", "l_split", "strip_used"))
        g_dve, y_copied, g_act = map(sem, ("g_dve", "y_copied", "g_act"))
        hx_round, hx_split = map(sem, ("hx_round", "hx_split"))
        sq_sum, ms_done, rms_done, rs_done = map(sem, ("sq_sum", "ms_done", "rms_done", "rs_done"))
        t_done, x_done, xsq_done, xacc = map(sem, ("t_done", "x_done", "xsq_done", "xacc"))
        rope_mul, rope_out, trigR_done, kz_done, sel_done = map(
            sem, ("rope_mul", "rope_out", "trigR_done", "kz_done", "sel_done"))
        v_turned, v_tok, kv_stored = map(sem, ("v_turned", "v_tok", "kv_stored"))
        scored, masked, max_scaled, negmax, exp_done, l_done, p_norm, p_turned, pt_copied, pv_done = map(sem, (
            "scored", "masked", "max_scaled", "negmax", "exp_done", "l_done", "p_norm", "p_turned", "pt_copied",
            "pv_done"))
        o_round, o_split, q_zero, q_spread = map(sem, ("o_round", "o_split", "q_zero", "q_spread"))
        c_landed = [sem(f"c_landed{i}") for i in range(CSLOTS)]
        c_used = sem("c_used")
        d_scored, d_scopied, d_turned, d_masked, d_max, d_max2, d_negmax, d_exp, d_l, d_norm, d_pturned, d_ptcopied = map(
            sem, ("d_scored", "d_scopied", "d_turned", "d_masked", "d_max", "d_max2", "d_negmax", "d_exp", "d_l",
                  "d_norm", "d_pturned", "d_ptcopied"))
        relu_sq, a_round, a_split = map(sem, ("relu_sq", "a_round", "a_split"))
        fin = sem("fin")
        z_scaled, e_done, e_plus, e_inv, gated = map(sem, ("z_scaled", "e_done", "e_plus", "e_inv", "gated"))
        s_landed = [sem(f"s_landed{i}") for i in range(4)]
        s_stored = [sem(f"s_stored{i}") for i in range(4)]
        r_dec, r_zero, r_padH, r_padL, r_turned, r_tok, r_pturned, r_stack = map(
            sem, ("r_dec", "r_zero", "r_padH", "r_padL", "r_turned", "r_tok", "r_pturned", "r_stack"))
        r_scored, r_decayed, r_state, r_scopied, r_out, r_sread, r_outer, r_updated = map(
            sem, ("r_scored", "r_decayed", "r_state", "r_scopied", "r_out", "r_sread", "r_outer", "r_updated"))
        gn_o, gn_mean, gn_sq, gn_rms, gn_rs, yr_round, yr_split, ps_stored = map(
            sem, ("gn_o", "gn_mean", "gn_sq", "gn_rms", "gn_rs", "yr_round", "yr_split", "ps_stored"))

        block = ctx.enter_context(nc.Block())

        NU = 2 * NH
        CL = 8 // CT
        GD_MIX, GD_FF1A, GD_RET, GD_FF1B = 0, 23, 39, 63
        TILES = ([(0, 0, 16)] + [(1, 4 * t, 4) for t in range(NT)] + [(2, 8 * p, 8) for p in range(2)] + [(3, 0, 16)])

        def loop(eng, first, count, body):
            assert count % RAWS == 0
            with eng.Fori(0, count // RAWS) as i:
                for u in range(RAWS):
                    body(RAWS * i + (first + u), u, i)

        @block.sync
        def _(sp):
            sp.dma_start(x[:, :, :], x_in).then_inc(x_landed, 16)
            sp.dma_start(col[:, :], cols).then_inc(const_in, 16)
            sp.dma_start(mat[:, :, :], mats).then_inc(const_in, 16)
            for s in range(RAWS):
                sp.dma_start(raw[:, s, :], wst[s]).then_inc(w_landed[s], 16)
            sp.dma_start(trig_sb[:, :, :], trig[0]).then_inc(trig_in, 16)
            sp.dma_start(pm[:, :, :], pmask).then_inc(mask_in, 16)
            sp.dma_start(dm[:, :], dmask).then_inc(mask_in, 16)

            def strip(s, slot):
                sp.wait_ge(l_split, s - RAWS + 1)
                sp.dma_start(raw[:, slot, :], wst[ds(s, 1)].rearrange("a p n -> (a p) n")).then_inc(w_landed[slot], 16)

            def strips(first, end):
                whole = (end - first) // RAWS * RAWS
                if whole:
                    loop(sp, first, whole, lambda s, u, i: strip(s, (first + u) % RAWS))
                for s in range(first + whole, end):
                    strip(s, s % RAWS)

            def cache_load(src, n, j, used):
                if used is not None:
                    sp.wait_ge(c_used, used)
                sp.dma_start(cslot[:, j, :], src[ds(n, 1), j].rearrange("a p n -> (a p) n")).then_inc(c_landed[j], 16)

            strips(RAWS, RAWS + S_MIXOUT)
            for j in range(CL):
                cache_load(kcache, 0, j, None)
            with sp.Fori(1, NB) as n:
                for j in range(CL):
                    cache_load(kcache, n, j, CL * n + (j + 1 - CL))
            with sp.Fori(0, NB) as n:
                for j in range(CL):
                    cache_load(vcache, n, j, CL * n + (CL * NB + j + 1 - CL))
            strips(RAWS + S_MIXOUT, RAWS + S_RETIN)
            sp.wait_ge(strip_used, S_RETIN)
            sp.dma_start(trig_sb[:, :, :], trig[1]).then_inc(trig_in, 16)
            sp.dma_start(rm[:, :, :], rmask).then_inc(rmask_in, 16)
            sp.dma_start(dec[:, :, :, :], qkdec).then_inc(rmask_in, 16)

            def state_load(n, h):
                j = n % 4
                k = 2 * h + n // 4
                if k:
                    sp.wait_ge(s_stored[j], 16 * k)
                sp.dma_start(sslot[:, j, :].rearrange("p (z e) -> p z e", z=2),
                             state[n, h].rearrange("(z p) e -> p z e", p=P)).then_inc(s_landed[j], 16)

            for n in range(4):
                state_load(n, 0)
            strips(RAWS + S_RETIN, RAWS + S_RETOUT)
            for h in range(NHR):
                for n in range(4 if h == 0 else 0, NB):
                    state_load(n, h)
            strips(RAWS + S_RETOUT, N_STRIPS)

        @block.gpsimd
        def _(pool):
            def sum_squares(b):
                for k in range(KT):
                    pool.wait_ge(xsq_done, KT * b + k + 1)
                    if k == 0:
                        nc.gpsimd.tensor_copy(sumsq[:, :], sq[:, 0, :]).then_inc(xacc, 1)
                    else:
                        pool.wait_ge(xacc, KT * b + k)
                        nc.gpsimd.tensor_tensor(sumsq[:, :], sumsq[:, :], sq[:, k % 2, :], ALU.add).then_inc(xacc, 1)

            sum_squares(0)
            pool.wait_ge(rope_out, 2 * 4 * NBR)
            pool.wait_ge(g_dve, 1 + GD_MIX + 21)
            pool.dma_start(k_out, kT[:, :, :]).then_inc(kv_stored, 16)
            pool.dma_start(v_out, vT[:, :, :]).then_inc(kv_stored, 16)
            nc.gpsimd.memset(qbd, 0.0).then_inc(q_zero, 1)
            pool.wait_ge(q_zero, 1)
            for h in range(4):
                nc.gpsimd.tensor_copy(
                    qbd[32 * h:32 * h + 32, :, :].rearrange("p a (c f) -> p a c f", f=4)[:, :, :, h],
                    qT[32 * h:32 * h + 32, :, SEQ:T]).then_inc(q_spread, 1)
            sum_squares(1)
            sum_squares(2)
            pool.wait_ge(strip_used, S_RETIN)
            nc.gpsimd.memset(vpad[:, :, :, :], 0.0).then_inc(r_zero, 1)
            nc.gpsimd.memset(kpad[:, :, :, :], 0.0).then_inc(r_zero, 1)
            for h in range(NHR):
                for z in range(2):
                    pool.wait_ge(r_scopied, 2 * h + z + 1)
                    pool.dma_start(pstate_out[h, z * P:(z + 1) * P, :], ps_sb[z]).then_inc(ps_stored, 16)
                for n in range(NB):
                    pool.wait_ge(r_updated, 2 * (NB * h + n + 1))
                    pool.dma_start(sstate_out[n, h].rearrange("(z p) e -> p z e", p=P),
                                   sslot[:, n % 4, :].rearrange("p (z e) -> p z e", z=2)).then_inc(s_stored[n % 4], 16)
            sum_squares(3)
            pool.wait_ge(x_done, 4 * KT)
            pool.dma_start(x_out, x[:, :, :]).then_inc(fin, 16)
            pool.wait_ge(fin, 16)
            pool.wait_ge(kv_stored, 32)
            pool.wait_ge(ps_stored, 16 * 2 * NHR)
            for j in range(4):
                pool.wait_ge(s_stored[j], 16 * 2 * NHR)

        @block.tensor
        def _(pe):
            def product(s, u, out, hi, lo, start=True, stop=True):
                pe.wait_ge(l_split, s + 1)
                for m in range(2):
                    for k in range(KT):
                        c = slice(k * SC + m * P, k * SC + m * P + P)
                        first, last = start and k == 0, stop and k == KT - 1
                        nc.tensor.matmul(out[:, m, :], wH[:, u % 2, c], hi[:, k, :], start=first, stop=False)
                        nc.tensor.matmul(out[:, m, :], wH[:, u % 2, c], lo[:, k, :], start=False, stop=False)
                        mm = nc.tensor.matmul(out[:, m, :], wL[:, u % 2, c], hi[:, k, :], start=False, stop=last)
                mm.then_inc(strip_used, 1)

            def mean_square(which, of, ready, count):
                pe.wait_ge(ready, count)
                nc.tensor.matmul(MS, which, of, start=True, stop=True).then_inc(ms_done, 1)

            def pre_norm(b):
                mean_square(mean_d, sumsq[:, :], xacc, KT * (b + 1))
                pe.wait_ge(hx_split, KT * (b + 1))

            pe.wait_ge(const_in, 32)
            pre_norm(0)

            def in_mix(s, u, i, j):
                pe.wait_ge(g_dve, j)
                product(s, s if isinstance(s, int) else u, G(u), hH, hL)

            loop(pe, S_Q, N_Q, lambda s, u, i: in_mix(s, u, i, RAWS * i + u))
            loop(pe, S_KV, N_KV, lambda s, u, i: in_mix(s, u, i, RAWS * i + (N_Q + u)))
            in_mix(S_BKV, 0, None, 20)
            pe.wait_ge(kz_done, 1)
            for s in range(2):
                pe.wait_ge(g_dve, 21 + s)
                for z in range(2):
                    mm = nc.tensor.matmul(G(21 + s)[:, z, :], mat[:, 3 + 2 * s + z, :], kz[:, :], start=True, stop=True)
                mm.then_inc(sel_done, 1)
            pe.wait_ge(g_dve, 1 + 23)
            for i in range(7):
                if i >= 2:
                    pe.wait_ge(v_tok, 2 * (i - 1))
                b0 = 2 * (i % 2)
                for c in range(2 if i < 6 else 1):
                    for tb in range(3):
                        w = P if tb < 2 else NS
                        out = banks[0:w, b0 + tb // 2, (tb % 2) * 256 + c * P:(tb % 2) * 256 + c * P + P]
                        mm = nc.tensor.transpose(out, vT[:, 2 * i + c, tb * P:tb * P + w], ident)
                mm.then_inc(v_turned, 1)

            def branches(u):
                return list(range(NG)) if u < NH else [NG]

            def scores(u):
                j = u % NH
                s, r = j // 4, slice(32 * (j % 4), 32 * (j % 4) + 32)
                if u:
                    pe.wait_ge(masked, 2 * u)
                for a, br in enumerate(branches(u)):
                    for z in range(2):
                        t = (2 * br + s) * 2 + z
                        nc.tensor.matmul(S45[:, a * 256:a * 256 + 256], qT[r, t, P:2 * P], kT[r, t, 0:2 * P],
                                         start=z == 0, stop=z == 1)
                for a, br in enumerate(branches(u)):
                    for z in range(2):
                        t = (2 * br + s) * 2 + z
                        mm = nc.tensor.matmul(banks[:, 6, a * P:a * P + P], qT[r, t, 0:P], kT[r, t, 0:P],
                                              start=z == 0, stop=z == 1)
                mm.then_inc(scored, 1)

            def turn_p(u):
                pe.wait_ge(p_norm, 2 * (u + 1))
                if u:
                    pe.wait_ge(pt_copied, u)
                n = len(branches(u))
                for a in range(n):
                    for c, at in enumerate((n * 256 + a * P, a * 256, a * 256 + P)):
                        mm = nc.tensor.transpose(banks[:, a, c * P:c * P + P], p_sb[:, u % 2, at:at + P], ident)
                mm.then_inc(p_turned, 1)

            def pv(u):
                j = u % NH
                pe.wait_ge(pt_copied, u + 1)
                if u % 2 == 0 and u:
                    pe.wait_ge(o_split, u // 2)
                r = slice(64 * (j % 2), 64 * (j % 2) + 64)
                n = len(branches(u))
                for a, br in enumerate(branches(u)):
                    v0 = 4 * br * P + (j * HD if br < NG else j // 4 * HD)
                    nc.tensor.matmul(banks[r, 3, 0:2 * P], vtok[:, 0, v0:v0 + HD], pt_sb[:, a, 0:2 * P],
                                     start=a == 0, stop=False)
                    mm = nc.tensor.matmul(banks[r, 3, P:2 * P], vtok[:, 1, v0:v0 + HD], pt_sb[:, a, 2 * P:3 * P],
                                          start=False, stop=a == n - 1)
                mm.then_inc(pv_done, 1)

            scores(0)
            pe.wait_ge(v_tok, 2 * 7)
            for u in range(NU):
                if u + 1 < NU:
                    scores(u + 1)
                if u:
                    pv(u - 1)
                turn_p(u)
            pv(NU - 1)

            pe.wait_ge(q_spread, 4)
            pe.wait_ge(o_split, NH)
            with pe.Fori(0, NB) as n:
                for j in range(CL):
                    pe.wait_ge(c_landed[j], 16 * n + 16)
                    for c in range(CT):
                        br, off, w = TILES[CT * j + c]
                        for s in range(2):
                            for z in range(2):
                                k0 = c * 512 + (2 * s + z) * P
                                mm = nc.tensor.matmul(
                                    banks[:, 4 + s, ds(16 * n + (br * P + off), w)], cslot[:, j, k0:k0 + P],
                                    qbd[:, (2 * br + s) * 2 + z, ds(16 * n + off, w)], start=z == 0, stop=z == 1)
                    mm.then_inc(c_used, 1)
            for s in range(2):
                for br in range(NBR):
                    for z in range(2):
                        t = (2 * br + s) * 2 + z
                        c = s * P + br * NS
                        mm = nc.tensor.matmul(banks[:, 6, c:c + NS], qbd[:, t, :], kT[:, t, SEQ:T],
                                              start=z == 0, stop=z == 1)
            mm.then_inc(d_scored, 1)
            for s in range(2):
                pe.wait_ge(d_scopied, s + 1)
                for br in range(NBR):
                    mm = nc.tensor.transpose(banks[:, s, br * P:br * P + P], st_sb[:, s, br * P:br * P + P], ident)
                mm.then_inc(d_turned, 1)
            for s in range(2):
                pe.wait_ge(d_norm, 2 * (s + 1))
                for br in range(NBR):
                    at = br * P if br < NG else 480
                    nc.tensor.transpose(banks[:, 2 + s, br * P:br * P + P], sp_sb[:, s, at:at + P], ident)
                for br in range(NBR):
                    at = 384 + br * NS if br < NG else 608
                    mm = nc.tensor.transpose(banks[0:NS, 4 + s, br * P:br * P + P], sp_sb[:, s, at:at + NS], ident)
                mm.then_inc(d_pturned, 1)
            OT = banks[:, 7, :].rearrange("p (m h c e) -> p m h c e", m=2, h=4, e=2)
            pe.wait_ge(d_ptcopied, 4)
            for hp in range(4):
                s, e0 = hp // 2, 2 * (hp % 2)
                for br in range(NBR):
                    mov = ptn_sb[:, s, br * P:br * P + P].rearrange("p (c f) -> p c f", f=4)[:, :, e0:e0 + 2]
                    if br < NG:
                        nc.tensor.matmul(OT[:, 0, hp, :, :], vnew[br][0:NS, hp * P:hp * P + P], mov,
                                         start=hp == 0 and br == 0, stop=False, skip_group_check=True)
                    else:
                        for e in range(2):
                            nc.tensor.matmul(OT[64 * e:64 * e + 64, 1, hp, :, :], vnew[NG][0:NS, s * HD:s * HD + HD], mov,
                                             start=False, stop=False, skip_group_check=True)
            with pe.Fori(0, NB) as n:
                for j in range(CL):
                    pe.wait_ge(c_landed[j], 16 * n + (16 * NB + 16))
                    for c in range(CT):
                        br, off, w = TILES[CT * j + c]
                        for hp in range(4):
                            s, e0 = hp // 2, 2 * (hp % 2)
                            o0 = (256 if br == NG else 0) + hp * 64 + off // 2
                            mov = st_sb[:, s, br * P:br * P + P].rearrange("p (c f) -> p c f", f=4)
                            mm = nc.tensor.matmul(
                                banks[:, 7, ds(8 * n + o0, w // 2)], cslot[:, j, c * 512 + hp * P:c * 512 + hp * P + P],
                                mov[:, ds(4 * n + off // 4, w // 4), e0:e0 + 2],
                                start=False, stop=False, skip_group_check=True)
                    mm.then_inc(c_used, 1)

            pe.wait_ge(o_split, NH + 2)
            for j in range(N_MIXOUT):
                if j >= 2:
                    pe.wait_ge(g_act, j - 1)
                product(S_MIXOUT + j, S_MIXOUT + j, G(j), hH, hL)

            def mlp(first1, first2, gd, ga, base, b):
                pre_norm(b)

                def up(s, u, i):
                    pe.wait_ge(g_dve, RAWS * i + (gd + u))
                    product(s, first1 + u, G(u), hH, hL)

                loop(pe, first1, N_FF, up)
                with pe.Fori(0, 2) as i:
                    for u in range(8):
                        kq = u % 4
                        if kq == 0:
                            pe.wait_ge(g_act, 2 * i + (ga + u // 4 - 1))
                        pe.wait_ge(a_split, base + 4 * (kq + 1))
                        product(8 * i + (first2 + u), first2 + u, G(u // 4), aH[:, 8 * kq:8 * kq + 8, :],
                                aL[:, 8 * kq:8 * kq + 8, :], start=kq == 0, stop=kq == 3)

            mean_square(mean_d, acc[:, 0, :], sq_sum, 4)
            mlp(S_FF1A, S_FF2A, GD_FF1A, 4, 0, 1)
            mean_square(mean_d, acc[:, 0, :], sq_sum, 8)
            pre_norm(2)

            def in_ret(s, u, i):
                pe.wait_ge(g_dve, RAWS * i + (GD_RET + u))
                product(s, S_RETIN + u, G(u), hH, hL)

            loop(pe, S_RETIN, N_RETIN, in_ret)

            pe.wait_ge(gated, 8)
            for h in range(NHR):
                if h:
                    pe.wait_ge(yr_split, h)
                for c in range(4):
                    for tb in range(2):
                        nc.tensor.transpose(banks[:, 6 + tb, c * P:c * P + P], vTr[:, 4 * h + c, tb * P:tb * P + P], ident)
                    nc.tensor.transpose(banks[0:NS, 4, c * P:c * P + P], vTr[:, 4 * h + c, SEQ:T], ident)
                for z in range(2):
                    for tb in range(2):
                        c = tb * DK + z * P
                        mm = nc.tensor.transpose(banks[:, 5, c:c + P], kr[:, 2 * h + z, tb * P:tb * P + P], ident)
                mm.then_inc(r_turned, 1)
                pe.wait_ge(r_padL, 4 * (h + 1))
                pe.wait_ge(r_tok, 4 * (h + 1))
                for half in range(2):
                    for c in range(4):
                        nc.tensor.transpose(banks[:, 6 + half, c * P:c * P + P],
                                            vpad[:, c, 4 * half:4 * half + 4, :].rearrange("p a b -> p (a b)"), ident)
                    for z in range(2):
                        c = half * DK + z * P
                        mm = nc.tensor.transpose(banks[:, 5, c:c + P],
                                                 kpad[:, z, 4 * half:4 * half + 4, :].rearrange("p a b -> p (a b)"), ident)
                mm.then_inc(r_pturned, 1)
                for cols_, kk, qq in ((slice(0, 256), slice(0, P), slice(0, SEQ)),
                                      (slice(256, 384), slice(P, SEQ), slice(P, SEQ)),
                                      (slice(384, 416), slice(SEQ, T), slice(SEQ, T))):
                    for z in range(2):
                        rows = kk.stop - kk.start
                        mm = nc.tensor.matmul(banks[0:rows, 4, cols_], kr[:, 2 * h + z, kk], qr[:, 2 * h + z, qq],
                                              start=z == 0, stop=z == 1)
                mm.then_inc(r_scored, 1)
                pe.wait_ge(r_decayed, 3 * (h + 1))
                for c in range(4):
                    nc.tensor.matmul(banks[:, c, 0:SEQ], vtok_r[:, 0, c * P:c * P + P], at_sb[:, 0:SEQ],
                                     start=True, stop=False)
                    nc.tensor.matmul(banks[:, c, P:SEQ], vtok_r[:, 1, c * P:c * P + P], at_sb[:, 256:384],
                                     start=False, stop=True)
                    mm = nc.tensor.matmul(banks[:, c, SEQ:T], vtok_s[:, c * P:c * P + P], at_sb[0:NS, 384:416],
                                          start=True, stop=True)
                mm.then_inc(r_out, 1)
                pe.wait_ge(r_stack, 2 * (h + 1))
                for z in range(2):
                    for tb in range(2):
                        mm = nc.tensor.matmul(banks[:, 6 + z, :], ktok_r[:, tb, z * P:z * P + P], vtok_r[:, tb, :],
                                              start=tb == 0, stop=tb == 1)
                    mm.then_inc(r_state, 1)
                for n in range(NB):
                    pe.wait_ge(s_landed[n % 4], 16 * (2 * h + n // 4 + 1))
                    for c in range(4):
                        for z in range(2):
                            mm = nc.tensor.matmul(banks[:, 5, c * NS + 4 * n:c * NS + 4 * n + 4],
                                                  sslot[:, n % 4, z * DV + c * P:z * DV + c * P + P],
                                                  qkd[:, 0, 2 * h + z, 4 * n:4 * n + 4], start=z == 0, stop=z == 1)
                    mm.then_inc(r_sread, 1)
                    r = slice(32 * (n % 4), 32 * (n % 4) + 32)
                    for z in range(2):
                        if n == 0:
                            pe.wait_ge(r_scopied, 2 * h + z + 1)
                        else:
                            pe.wait_ge(r_updated, 2 * (NB * h + n - 1) + z + 1)
                        nc.tensor.matmul(banks[:, 6 + z, :], kst[r, n // 4, z * P:z * P + P], vst[r, n // 4, :],
                                         start=True, stop=True).then_inc(r_outer, 1)
                for e in range(2):
                    pe.wait_ge(gn_o, 6 * h + (3 if e == 0 else 5))
                    nc.tensor.matmul(banks[:, 4, 0:T], mean_v, sumsq[:, :], start=True, stop=True).then_inc(gn_mean, 1)

            pe.wait_ge(yr_split, NHR)
            with pe.Fori(0, 2) as i:
                for u in range(4):
                    kh = u % 2
                    if kh == 0:
                        pe.wait_ge(g_act, 2 * i + (8 + u // 2 - 1))
                    product(4 * i + (S_RETOUT + u), S_RETOUT + u, G(u // 2), yH[:, 8 * kh:8 * kh + 8, :],
                            yL[:, 8 * kh:8 * kh + 8, :], start=kh == 0, stop=kh == 1)
            mean_square(mean_d, acc[:, 0, :], sq_sum, 12)
            mlp(S_FF1B, S_FF2B, GD_FF1B, 12, N_FF, 3)
            mean_square(mean_d, acc[:, 0, :], sq_sum, 16)

        @block.scalar
        def _(act):
            def round_strip(s, at, i=0):
                act.wait_ge(w_landed[at % RAWS], 16 * i + 16 * (at // RAWS + 1))
                if at >= SPL - 1:
                    act.wait_ge(strip_used, s - SPL + 1)
                nc.scalar.activation(wH[:, at % SPL, :], raw[:, at % RAWS, :], ACT.Copy).then_inc(h_round, 1)

            def next_strip(s, u, i, first):
                round_strip(s + 1, first + u + 1, i)

            def pre_norm(b, layer, norm):
                for k in range(KT):
                    if b:
                        act.wait_ge(x_done, KT * (b - 1) + k + 1)
                    if k >= 2:
                        act.wait_ge(xacc, KT * b + k - 1)
                    nc.scalar.activation(sq[:, k % 2, :], x[:, k, :], ACT.Square).then_inc(xsq_done, 1)
                    nc.scalar.activation(hH[:, k, :], x[:, k, :], ACT.Copy,
                                         scale=gain(layer, norm, k)).then_inc(hx_round, 1)
                root(2 * b)

            def root(e):
                act.wait_ge(ms_done, e + 1)
                nc.scalar.activation(rms[:, :], MS, ACT.Sqrt, bias=eps).then_inc(rms_done, 1)

            def take_y(e, j, last_strip):
                act.wait_ge(strip_used, last_strip + 1)
                nc.scalar.activation(y[:, 2 * j:2 * j + 2, :], G(j), ACT.Copy).then_inc(y_copied, 1)
                if j >= 2:
                    act.wait_ge(sq_sum, 4 * e + j - 1)
                nc.scalar.activation((sq if j else acc)[:, :, :], G(j), ACT.Square).then_inc(g_act, 1)

            def mlp(first1, first2, gd, base, e):
                def up(s, u, i):
                    next_strip(s, u, i, first1)
                    act.wait_ge(g_dve, RAWS * i + (1 + gd + u + 1))
                    act.wait_ge(a_split, RAWS * i + (base + u))
                    nc.scalar.activation(a_sb[:, :, :], relu_sb[:, u % 2, :, :], ACT.Square).then_inc(relu_sq, 1)
                    act.wait_ge(relu_sq, RAWS * i + (base + u + 1))
                    nc.scalar.activation(aH[:, ds(8 * i + 2 * u, 2), :], a_sb[:, :, :], ACT.Copy).then_inc(a_round, 1)

                loop(act, first1, N_FF, up)
                for u in range(N_FF):
                    if first2 + u + 1 < N_STRIPS:
                        round_strip(first2 + u + 1, first2 + u + 1)
                    if u % 4 == 3:
                        take_y(e, u // 4, first2 + u)
                root(2 * e + 1)

            act.wait_ge(const_in, 32)
            act.wait_ge(x_landed, 16)
            round_strip(0, 0)
            pre_norm(0, 0, 0)
            loop(act, S_Q, N_Q, lambda s, u, i: next_strip(s, u, i, S_Q))
            loop(act, S_KV, N_KV, lambda s, u, i: next_strip(s, u, i, S_KV))
            round_strip(S_MIXOUT, S_MIXOUT)
            act.wait_ge(rope_out, 2 * 4 * NBR)
            for i in range(7):
                act.wait_ge(v_turned, i + 1)
                b0, n = 2 * (i % 2), 256 if i < 6 else 128
                nc.scalar.activation(vtok[:, 0:2, 256 * i:256 * i + n],
                                     banks[:, b0, :].rearrange("p (t c) -> p t c", t=2)[:, :, 0:n],
                                     ACT.Copy).then_inc(v_tok, 1)
                nc.scalar.activation(vnew[i // 2][0:NS, 256 * (i % 2):256 * (i % 2) + n], banks[0:NS, b0 + 1, 0:n],
                                     ACT.Copy).then_inc(v_tok, 1)

            def exps(u):
                n = 3 if u < NH else 1
                act.wait_ge(negmax, u + 1)
                sm = small[:, u % 2, :]
                for b, c in ((0, slice(0, n * 256)), (1, slice(n * 256, n * 384))):
                    nc.scalar.activation(p_sb[:, u % 2, c], p_sb[:, u % 2, c], ACT.Exp, bias=sm[:, 2 + b:3 + b],
                                         scale=SCALE, accum_out=sm[:, 4 + b:5 + b]).then_inc(exp_done, 1)
                nc.scalar.activation(sm[:, 6:8], sm[:, 2:4], ACT.Exp,
                                     bias=col[:, C_SINKP + u:C_SINKP + u + 1]).then_inc(exp_done, 1)

            def copy_pt(u):
                n = 3 if u < NH else 1
                act.wait_ge(p_turned, u + 1)
                if u:
                    act.wait_ge(pv_done, u)
                nc.scalar.activation(pt_sb[:, 0:n, :], banks[:, 0:n, 0:384], ACT.Copy).then_inc(pt_copied, 1)

            def round_o(p):
                act.wait_ge(pv_done, 2 * (p + 1))
                nc.scalar.activation(hH[:, p, 0:SEQ], banks[:, 3, 0:SEQ], ACT.Copy).then_inc(o_round, 1)

            exps(0)
            for u in range(NU):
                if u + 1 < NU:
                    exps(u + 1)
                copy_pt(u)
                if u >= 2 and u % 2 == 0:
                    round_o(u // 2 - 1)
            round_o(NH - 1)

            act.wait_ge(c_used, CL * NB)
            act.wait_ge(o_split, NH)
            for s in range(2):
                nc.scalar.activation(st_sb[:, s, :], banks[:, 4 + s, :], ACT.Copy).then_inc(d_scopied, 1)
            act.wait_ge(d_negmax, 2)
            for s in range(2):
                for m, c in ((0, slice(0, 480)), (1, slice(480, 640))):
                    a = 2 * s + m
                    nc.scalar.activation(sp_sb[:, s, c], sp_sb[:, s, c], ACT.Exp, bias=dsm[:, 8 + a:9 + a], scale=SCALE,
                                         accum_out=dsm[:, 12 + a:13 + a]).then_inc(d_exp, 1)
            nc.scalar.activation(dsm[:, 16:20], dsm[:, 16:20], ACT.Exp).then_inc(d_exp, 1)
            for s in range(2):
                act.wait_ge(d_pturned, s + 1)
                nc.scalar.activation(st_sb[:, s, :], banks[:, 2 + s, :], ACT.Copy).then_inc(d_ptcopied, 1)
                nc.scalar.activation(ptn_sb[:, s, :], banks[0:NS, 4 + s, :], ACT.Copy).then_inc(d_ptcopied, 1)
            act.wait_ge(c_used, 2 * CL * NB)
            for e in range(2):
                r = slice(64 * e, 64 * e + 64)
                nc.scalar.activation(hH[r, :, SEQ:T],
                                     banks[r, 7, :].rearrange("p (a c e) -> p a c e", a=8, e=2)[:, :, :, e],
                                     ACT.Copy).then_inc(o_round, 1)
            for j in range(N_MIXOUT):
                round_strip(S_MIXOUT + j + 1, S_MIXOUT + j + 1)
                take_y(0, j, S_MIXOUT + j)
            root(1)
            pre_norm(1, 0, 2)
            mlp(S_FF1A, S_FF2A, GD_FF1A, 0, 1)
            pre_norm(2, 1, 0)
            loop(act, S_RETIN, 16, lambda s, u, i: next_strip(s, u, i, S_RETIN))

            def gate_exp(s, u, i):
                next_strip(s, u, i, S_RETIN + 16)
                act.wait_ge(g_dve, RAWS * i + (1 + GD_RET + 16 + u + 1))
                nc.scalar.activation(acc[:, :, :], gate[:, ds(8 * i + 2 * u, 2), :], ACT.Exp,
                                     scale=-1.0).then_inc(e_done, 1)

            loop(act, S_RETIN + 16, 8, gate_exp)

            for h in range(NHR):
                if h == 0:
                    act.wait_ge(r_zero, 2)
                    act.wait_ge(r_dec, 2 * NHR)
                    act.wait_ge(gated, 8)
                else:
                    act.wait_ge(r_pturned, h)
                for p in range(2):
                    nc.scalar.activation(
                        kpad[:, :, :, 4 * p:4 * p + 4].bitcast(F32R),
                        qkd[:, 1, 2 * h:2 * h + 2, :].rearrange("p z (n t) -> p z n t", t=NT), ACT.Copy).then_inc(r_padH, 1)
                for p in range(2):
                    nc.scalar.activation(
                        vpad[:, :, :, 8 * p:8 * p + 4].bitcast(F32R),
                        vTr[:, 4 * h:4 * h + 4, SEQ:T].rearrange("p c (n t) -> p c n t", t=NT), ACT.Copy).then_inc(r_padH, 1)
                act.wait_ge(r_turned, h + 1)
                nc.scalar.activation(vtok_r[:, :, :], banks[:, 6:8, :], ACT.Copy).then_inc(r_tok, 1)
                nc.scalar.activation(vtok_s[:, :], banks[0:NS, 4, :], ACT.Copy).then_inc(r_tok, 1)
                for tb in range(2):
                    c = C_KDEC + tb * NHR + h
                    nc.scalar.activation(ktok_r[:, tb, :], banks[:, 5, tb * DK:tb * DK + DK], ACT.Copy,
                                         scale=col[:, c:c + 1]).then_inc(r_tok, 1)
                act.wait_ge(r_pturned, h + 1)
                nc.scalar.activation(vst, banks[:, 6:8, :], ACT.Copy).then_inc(r_stack, 1)
                nc.scalar.activation(kst, banks[:, 5, :].rearrange("p (a c) -> p a c", a=2), ACT.Copy).then_inc(r_stack, 1)
                if h:
                    act.wait_ge(ps_stored, 16 * 2 * h)
                for z in range(2):
                    act.wait_ge(r_state, 2 * h + z + 1)
                    nc.scalar.activation(ps_sb[z], banks[:, 6 + z, :], ACT.Copy).then_inc(r_scopied, 1)
                act.wait_ge(gn_o, 6 * h + 4)
                nc.scalar.activation(o_sb, oc_sb, ACT.Square).then_inc(gn_sq, 1)
                act.wait_ge(gn_mean, 2 * (h + 1))
                nc.scalar.activation(rms[:, :], banks[:, 4, 0:T], ACT.Sqrt, bias=gn_eps).then_inc(gn_rms, 1)
                act.wait_ge(gn_o, 6 * (h + 1))
                nc.scalar.activation(yH[:, 4 * h:4 * h + 4, :], oc_sb, ACT.Copy).then_inc(yr_round, 1)

            for u in range(N_RETOUT):
                round_strip(S_RETOUT + u + 1, S_RETOUT + u + 1)
                if u % 2 == 1:
                    if u == 1:
                        act.wait_ge(ps_stored, 16 * 2 * NHR)
                    take_y(2, u // 2, S_RETOUT + u)
            root(5)
            pre_norm(3, 1, 2)
            for j in range(4):
                act.wait_ge(s_stored[j], 16 * 2 * NHR)
            mlp(S_FF1B, S_FF2B, GD_FF1B, N_FF, 3)

        @block.vector
        def _(dve):
            def split_strip(s, at):
                dve.wait_ge(h_round, s + 1)
                nc.vector.tensor_tensor(wL[:, at % SPL, :], raw[:, at % RAWS, :], wH[:, at % SPL, :].bitcast(F32),
                                        ALU.subtract).then_inc(l_split, 1)

            def inverse(e, to):
                dve.wait_ge(rms_done, e + 1)
                nc.vector.reciprocal(to[:, :], rms[:, :]).then_inc(rs_done, 1)

            def split_x(b, k, layer, norm):
                dve.wait_ge(hx_round, KT * b + k + 1)
                nc.vector.scalar_tensor_tensor(out=hL[:, k, :], in0=x[:, k, :], scalar=gain(layer, norm, k),
                                               in1=hH[:, k, :].bitcast(F32), op0=ALU.mult,
                                               op1=ALU.subtract).then_inc(hx_split, 1)

            def pre_norm(b, layer, norm, part=None):
                inverse(2 * b, rs_pre)
                dve.wait_ge(rs_done, 2 * b + 1)

            def residual(e, layer, norm, b=None, nlayer=0, nnorm=0):
                inverse(2 * e + 1, rs_post)
                dve.wait_ge(rs_done, 2 * e + 2)
                for k in range(KT + 2):
                    if k < KT:
                        if k >= 2:
                            dve.wait_ge(x_done, KT * e + k - 1)
                        nc.vector.scalar_tensor_tensor(out=tmp[:, k % 2, :], in0=y[:, k, :], scalar=gain(layer, norm, k),
                                                       in1=rs_post[:, :], op0=ALU.mult, op1=ALU.mult).then_inc(t_done, 1)
                    if 1 <= k <= KT:
                        dve.wait_ge(t_done, KT * e + k)
                        nc.vector.tensor_tensor(x[:, k - 1, :], x[:, k - 1, :], tmp[:, (k - 1) % 2, :],
                                                ALU.add).then_inc(x_done, 1)
                    if k >= 2 and b is not None:
                        split_x(b, k - 2, nlayer, nnorm)

            def sum_y(e, j, ga):
                dve.wait_ge(g_act, ga + j + 1)
                if j >= 1:
                    if j >= 2:
                        dve.wait_ge(sq_sum, 4 * e + j - 1)
                    nc.vector.tensor_tensor(acc[:, :, :], acc[:, :, :], sq[:, :, :], ALU.add).then_inc(sq_sum, 1)
                if j == 3:
                    dve.wait_ge(sq_sum, 4 * e + 3)
                    nc.vector.tensor_tensor(acc[:, 0, :], acc[:, 0, :], acc[:, 1, :], ALU.add).then_inc(sq_sum, 1)

            def rotate(s, gj, u, rj, out, free):
                if s is not None:
                    dve.wait_ge(strip_used, s + 1)
                dve.wait_ge(rope_out, 2 * rj)
                nc.vector.tensor_tensor(sq[:, :, :], G(u), both(trigR[:, 0, :]), ALU.mult).then_inc(rope_mul, 1)
                nc.vector.tensor_tensor(acc[:, :, :], G(u), both(trigR[:, 1, :]), ALU.mult).then_inc(g_dve, 1)
                dve.wait_ge(rope_mul, rj + 1)
                dve.wait_ge(g_dve, gj + 2)
                nc.vector.tensor_tensor(out(0), sq[:, 0:1, :], acc[:, 1:2, :], ALU.subtract).then_inc(rope_out, 1)
                nc.vector.tensor_tensor(out(1), sq[:, 1:2, :], acc[:, 0:1, :], ALU.add).then_inc(rope_out, 1)

            def mlp(first1, first2, gd, ga, base, e):
                def up(s, u, i):
                    split_strip(s + 1, first1 + u + 1)
                    dve.wait_ge(strip_used, s + 1)
                    dve.wait_ge(relu_sq, RAWS * i + (base + u))
                    nc.vector.scalar_tensor_tensor(out=relu_sb[:, u % 2, :, :], in0=G(u), scalar=0.0,
                                                   in1=both(rs_pre[:, :]), op0=ALU.max, op1=ALU.mult).then_inc(g_dve, 1)
                    dve.wait_ge(a_round, RAWS * i + (base + u + 1))
                    nc.vector.tensor_tensor(aL[:, ds(8 * i + 2 * u, 2), :], a_sb[:, :, :],
                                            aH[:, ds(8 * i + 2 * u, 2), :].bitcast(F32), ALU.subtract).then_inc(a_split, 1)

                loop(dve, first1, N_FF, up)
                for u in range(N_FF):
                    if first2 + u + 1 < N_STRIPS:
                        split_strip(first2 + u + 1, first2 + u + 1)
                    if u % 4 == 3:
                        sum_y(e, u // 4, ga)

            nc.vector.memset(rs_post[:, :], 0.0).then_inc(g_dve, 1)
            split_strip(0, 0)
            dve.wait_ge(const_in, 32)
            for k in range(KT):
                split_x(0, k, 0, 0)
            pre_norm(0, 0, 0)
            dve.wait_ge(trig_in, 16)
            nc.vector.tensor_tensor(trigR[:, :, :], trig_sb[:, :, :], both(rs_pre[:, :]), ALU.mult).then_inc(trigR_done, 1)
            dve.wait_ge(trigR_done, 1)

            def q_strip(s, u, i):
                split_strip(s + 1, S_Q + u + 1)
                rotate(s, RAWS * i + u, u, RAWS * i + u, lambda z: qT[:, ds(8 * i + (2 * u + z), 1), :], 0)

            loop(dve, S_Q, N_Q, q_strip)

            def kv_strip(s, u, i):
                split_strip(s + 1, S_KV + u + 1)
                if u < 2:
                    rotate(s, RAWS * i + (N_Q + u), u, 2 * i + (N_Q + u), lambda z: kT[:, ds(4 * i + (2 * u + z), 1), :], 0)
                else:
                    dve.wait_ge(strip_used, s + 1)
                    nc.vector.tensor_tensor(vT[:, ds(4 * i + 2 * (u - 2), 2), :], G(u), both(rs_pre[:, :]),
                                            ALU.mult).then_inc(g_dve, 1)

            loop(dve, S_KV, N_KV, kv_strip)
            split_strip(S_MIXOUT, S_MIXOUT)
            dve.wait_ge(strip_used, S_BKV + 1)
            nc.vector.tensor_copy(kz[:, :], G(20)[:, 0, :]).then_inc(kz_done, 1)
            nc.vector.tensor_tensor(vT[:, 4 * NG, :], G(20)[:, 1, :], rs_pre[:, :], ALU.mult).then_inc(g_dve, 1)
            for s in range(2):
                dve.wait_ge(sel_done, s + 1)
                rotate(None, 21 + s, 21 + s, 14 + s, lambda z: kT[:, 12 + 2 * s + z:13 + 2 * s + z, :], 0)

            def mask_unit(u):
                n = 3 if u < NH else 1
                br = slice(0, 3) if u < NH else slice(3, 4)
                dve.wait_ge(scored, u + 1)
                if u >= 2:
                    dve.wait_ge(p_turned, u - 1)
                if u == 0:
                    dve.wait_ge(mask_in, 32)
                    dve.wait_ge(kv_stored, 32)
                    dve.wait_ge(v_tok, 14)
                sm = small[:, u % 2, :]
                nc.vector.tensor_tensor_reduce(
                    out=p_sb[:, u % 2, 0:n * 256], in0=S45[:, 0:n * 256], in1=pm[:, br, :].rearrange("p a c -> p (a c)"),
                    scale=1.0, scalar=-3e38, op0=ALU.add, op1=ALU.max, accum_out=sm[:, 0:1]).then_inc(masked, 1)
                nc.vector.tensor_tensor_reduce(
                    out=p_sb[:, u % 2, n * 256:n * 384].rearrange("p (a c) -> p a c", a=n),
                    in0=banks[:, 6, 0:n * P].rearrange("p (a c) -> p a c", a=n), in1=pm[:, br, P:2 * P],
                    scale=1.0, scalar=-3e38, op0=ALU.add, op1=ALU.max, accum_out=sm[:, 1:2]).then_inc(masked, 1)
                dve.wait_ge(masked, 2 * (u + 1))
                nc.vector.tensor_scalar(sm[:, 8:10], sm[:, 0:2], SCALE, col[:, C_SINKP + u:C_SINKP + u + 1],
                                        ALU.mult, ALU.max).then_inc(max_scaled, 1)
                dve.wait_ge(max_scaled, u + 1)
                nc.vector.tensor_scalar(sm[:, 2:4], sm[:, 8:10], -1.0, None, ALU.mult).then_inc(negmax, 1)

            def norm_unit(u):
                n = 3 if u < NH else 1
                sm = small[:, u % 2, :]
                dve.wait_ge(exp_done, 3 * (u + 1))
                nc.vector.tensor_tensor(sm[:, 8:10], sm[:, 4:6], sm[:, 6:8], ALU.add).then_inc(l_done, 1)
                dve.wait_ge(l_done, 2 * u + 1)
                nc.vector.reciprocal(sm[:, 4:6], sm[:, 8:10]).then_inc(l_done, 1)
                dve.wait_ge(l_done, 2 * u + 2)
                for b, c in ((0, slice(0, n * 256)), (1, slice(n * 256, n * 384))):
                    nc.vector.tensor_scalar(p_sb[:, u % 2, c], p_sb[:, u % 2, c], sm[:, 4 + b:5 + b], None,
                                            ALU.mult).then_inc(p_norm, 1)

            def split_o(p):
                dve.wait_ge(o_round, p + 1)
                nc.vector.tensor_tensor(hL[:, p, 0:SEQ], banks[:, 3, 0:SEQ], hH[:, p, 0:SEQ].bitcast(F32),
                                        ALU.subtract).then_inc(o_split, 1)

            mask_unit(0)
            for u in range(NU):
                if u + 1 < NU:
                    mask_unit(u + 1)
                norm_unit(u)
                if u >= 2 and u % 2 == 0:
                    split_o(u // 2 - 1)
            split_o(NH - 1)

            for s in range(2):
                dve.wait_ge(d_turned, s + 1)
                dve.wait_ge(d_scored, 1)
                new = banks[:, 6, s * P:s * P + P]
                for c, src in ((slice(0, 384), banks[:, s, 0:384]), (slice(480, 608), banks[:, s, 384:512]),
                               (slice(384, 480), new[:, 0:96]), (slice(608, 640), new[:, 96:128])):
                    nc.vector.tensor_tensor(sp_sb[:, s, c], src, dm[:, c], ALU.add).then_inc(d_masked, 1)
                dve.wait_ge(d_masked, 4 * (s + 1))
                for m, c in ((0, slice(0, 480)), (1, slice(480, 640))):
                    a = 2 * s + m
                    nc.vector.tensor_reduce(dsm[:, a:a + 1], sp_sb[:, s, c], AX.X, ALU.max).then_inc(d_max, 1)
            dve.wait_ge(d_max, 4)
            nc.vector.scalar_tensor_tensor(out=dsm[:, 4:8], in0=dsm[:, 0:4], scalar=SCALE,
                                           in1=col[:, C_SINKD:C_SINKD + 4], op0=ALU.mult, op1=ALU.max).then_inc(d_max2, 1)
            dve.wait_ge(d_max2, 1)
            nc.vector.tensor_scalar(dsm[:, 8:12], dsm[:, 4:8], -1.0, None, ALU.mult).then_inc(d_negmax, 1)
            nc.vector.tensor_tensor(dsm[:, 16:20], col[:, C_SINKD:C_SINKD + 4], dsm[:, 4:8],
                                    ALU.subtract).then_inc(d_negmax, 1)
            dve.wait_ge(d_exp, 5)
            nc.vector.tensor_tensor(dsm[:, 0:4], dsm[:, 12:16], dsm[:, 16:20], ALU.add).then_inc(d_l, 1)
            dve.wait_ge(d_l, 1)
            nc.vector.reciprocal(dsm[:, 20:24], dsm[:, 0:4]).then_inc(d_l, 1)
            dve.wait_ge(d_l, 2)
            for s in range(2):
                for m, c in ((0, slice(0, 480)), (1, slice(480, 640))):
                    a = 2 * s + m
                    nc.vector.tensor_scalar(sp_sb[:, s, c], sp_sb[:, s, c], dsm[:, 20 + a:21 + a], None,
                                            ALU.mult).then_inc(d_norm, 1)
            for e in range(2):
                dve.wait_ge(o_round, NH + e + 1)
                r = slice(64 * e, 64 * e + 64)
                nc.vector.tensor_tensor(hL[r, :, SEQ:T],
                                        banks[r, 7, :].rearrange("p (a c e) -> p a c e", a=8, e=2)[:, :, :, e],
                                        hH[r, :, SEQ:T].bitcast(F32), ALU.subtract).then_inc(o_split, 1)
            for j in range(N_MIXOUT):
                split_strip(S_MIXOUT + j + 1, S_MIXOUT + j + 1)
                sum_y(0, j, 0)
            residual(0, 0, 1, 1, 0, 2)
            pre_norm(1, 0, 2)
            mlp(S_FF1A, S_FF2A, GD_FF1A, 4, 0, 1)
            residual(1, 0, 3, 2, 1, 0)
            pre_norm(2, 1, 0)
            dve.wait_ge(trig_in, 32)
            nc.vector.tensor_tensor(trigR[:, :, :], trig_sb[:, :, :], both(rs_pre[:, :]), ALU.mult).then_inc(trigR_done, 1)
            dve.wait_ge(trigR_done, 2)

            for t, dst in ((0, qr), (1, kr)):
                for u in range(NHR):
                    s = S_RETIN + 4 * t + u
                    split_strip(s + 1, s + 1)
                    rotate(s, GD_RET + 4 * t + u, u, 16 + 4 * t + u, lambda z: dst[:, 2 * u + z:2 * u + z + 1, :], 0)

            def v_strip(s, u, i):
                split_strip(s + 1, S_RETIN + 8 + u + 1)
                dve.wait_ge(strip_used, s + 1)
                nc.vector.tensor_tensor(vTr[:, ds(8 * i + 2 * u, 2), :], G(u), both(rs_pre[:, :]),
                                        ALU.mult).then_inc(g_dve, 1)

            loop(dve, S_RETIN + 8, 8, v_strip)

            def gate_strip(s, u, i):
                split_strip(s + 1, S_RETIN + 16 + u + 1)
                dve.wait_ge(strip_used, s + 1)
                g = gate[:, ds(8 * i + 2 * u, 2), :]
                nc.vector.tensor_tensor(g, G(u), both(rs_pre[:, :]), ALU.mult).then_inc(g_dve, 1)
                dve.wait_ge(e_done, RAWS * i + (u + 1))
                nc.vector.tensor_scalar(tmp[:, :, :], acc[:, :, :], 1.0, None, ALU.add).then_inc(e_plus, 1)
                dve.wait_ge(e_plus, RAWS * i + (u + 1))
                nc.vector.reciprocal(sq[:, :, :], tmp[:, :, :]).then_inc(e_inv, 1)
                dve.wait_ge(e_inv, RAWS * i + (u + 1))
                nc.vector.tensor_tensor(g, g, sq[:, :, :], ALU.mult).then_inc(gated, 1)

            loop(dve, S_RETIN + 16, 8, gate_strip)
            dve.wait_ge(rmask_in, 32)
            dve.wait_ge(rope_out, 2 * (16 + 8))
            for a, src in ((0, qr), (1, kr)):
                for h in range(NHR):
                    nc.vector.tensor_tensor(qkd[:, a, 2 * h:2 * h + 2, :], src[:, 2 * h:2 * h + 2, SEQ:T],
                                            dec[:, a, h, :].unsqueeze(1).broadcast_to([P, 2, NS]),
                                            ALU.mult).then_inc(r_dec, 1)

            for h in range(NHR):
                c_dec = GAMMA[h] ** NT
                dve.wait_ge(r_padH, 4 * (h + 1))
                if h == 0:
                    dve.wait_ge(r_dec, 2 * NHR)
                for p in range(2):
                    nc.vector.tensor_tensor(kpad[:, :, :, 8 + 4 * p:12 + 4 * p],
                                            qkd[:, 1, 2 * h:2 * h + 2, :].rearrange("p z (n t) -> p z n t", t=NT),
                                            kpad[:, :, :, 4 * p:4 * p + 4], ALU.subtract).then_inc(r_padL, 1)
                for p in range(2):
                    nc.vector.tensor_tensor(vpad[:, :, :, 4 + 8 * p:8 + 8 * p],
                                            vTr[:, 4 * h:4 * h + 4, SEQ:T].rearrange("p c (n t) -> p c n t", t=NT),
                                            vpad[:, :, :, 8 * p:8 * p + 4], ALU.subtract).then_inc(r_padL, 1)
                dve.wait_ge(r_scored, h + 1)
                nc.vector.tensor_tensor(at_sb[:, 0:256], banks[:, 4, 0:256], rm[:, h, 0:256], ALU.mult).then_inc(r_decayed, 1)
                nc.vector.tensor_tensor(at_sb[:, 256:384], banks[:, 4, 256:384], rm[:, h, 0:128],
                                        ALU.mult).then_inc(r_decayed, 1)
                nc.vector.tensor_tensor(at_sb[0:NS, 384:416], banks[0:NS, 4, 384:416], rm[0:NS, h, 256:288],
                                        ALU.mult).then_inc(r_decayed, 1)
                dve.wait_ge(r_out, h + 1)
                nc.vector.tensor_copy(o_sb, banks[:, 0:4, 0:T]).then_inc(gn_o, 1)
                for n in range(NB):
                    for z in range(2):
                        dve.wait_ge(r_outer, 2 * (NB * h + n) + z + 1)
                        c = sslot[:, n % 4, z * DV:z * DV + DV]
                        nc.vector.scalar_tensor_tensor(out=c, in0=c, scalar=c_dec, in1=banks[:, 6 + z, :], op0=ALU.mult,
                                                       op1=ALU.add).then_inc(r_updated, 1)
                dve.wait_ge(r_sread, NB * (h + 1))
                dve.wait_ge(gn_o, 6 * h + 1)
                nc.vector.tensor_tensor(o_sb[:, :, SEQ:T], o_sb[:, :, SEQ:T],
                                        banks[:, 5, 0:4 * NS].rearrange("p (c t) -> p c t", c=4),
                                        ALU.add).then_inc(gn_o, 1)
                dve.wait_ge(gn_o, 6 * h + 2)
                nc.vector.tensor_reduce(sumsq[:, :], o_sb.rearrange("p c t -> p t c"), AX.X, ALU.add).then_inc(gn_o, 1)
                dve.wait_ge(gn_mean, 2 * h + 1)
                nc.vector.tensor_tensor(oc_sb, o_sb, banks[:, 4, 0:T].unsqueeze(1).broadcast_to([P, 4, T]),
                                        ALU.subtract).then_inc(gn_o, 1)
                dve.wait_ge(gn_sq, h + 1)
                nc.vector.tensor_reduce(sumsq[:, :], o_sb.rearrange("p c t -> p t c"), AX.X, ALU.add).then_inc(gn_o, 1)
                dve.wait_ge(gn_rms, h + 1)
                nc.vector.reciprocal(rs_post[:, :], rms[:, :]).then_inc(gn_rs, 1)
                dve.wait_ge(gn_rs, 2 * h + 1)
                nc.vector.tensor_tensor(oc_sb, oc_sb, rs_post[:, :].unsqueeze(1).broadcast_to([P, 4, T]),
                                        ALU.mult).then_inc(gn_rs, 1)
                dve.wait_ge(gn_rs, 2 * h + 2)
                nc.vector.tensor_tensor(oc_sb, oc_sb, gate[:, 4 * h:4 * h + 4, :], ALU.mult).then_inc(gn_o, 1)
                dve.wait_ge(yr_round, h + 1)
                nc.vector.tensor_tensor(yL[:, 4 * h:4 * h + 4, :], oc_sb, yH[:, 4 * h:4 * h + 4, :].bitcast(F32),
                                        ALU.subtract).then_inc(yr_split, 1)

            for u in range(N_RETOUT):
                split_strip(S_RETOUT + u + 1, S_RETOUT + u + 1)
                if u % 2 == 1:
                    sum_y(2, u // 2, 8)
            residual(2, 1, 1, 3, 1, 2)
            pre_norm(3, 1, 2)
            for j in range(4):
                dve.wait_ge(s_stored[j], 16 * 2 * NHR)
            mlp(S_FF1B, S_FF2B, GD_FF1B, 12, N_FF, 3)
            residual(3, 1, 3)


def _strips(w, order):
    blocks = [w[r * D:(r + 1) * D, c * SC:(c + 1) * SC].reshape(KT, P, SC).transpose(1, 0, 2).reshape(P, KT * SC)
              for r, c in order]
    return blocks


def _halves(w):
    return w.reshape(w.shape[0], -1, 4, 2, HALF).transpose(0, 1, 3, 2, 4).reshape(w.shape[0], -1)


def _weights(w_in_mix, w_out_mix, w_in_ret, w_out_ret, w_ff1, w_ff2):
    n = NH * HD
    a = w_in_mix[0][:, :3 * NG * n].reshape(D, NG, 3, n)
    b = w_in_mix[0][:, 3 * NG * n:]
    col1 = [(0, 0), (0, 1)]
    out = []
    for g in range(NG):
        out += _strips(_halves(a[:, g, 0]), col1)
    out += _strips(_halves(b[:, :n]), col1)
    for g in range(NG):
        out += _strips(_halves(a[:, g, 1]), col1) + _strips(a[:, g, 2], col1)
    out += _strips(b[:, n:], [(0, 0)])
    out += _strips(w_out_mix[0], [(0, c) for c in range(4)])

    def mlp(layer):
        return (_strips(w_ff1[layer], [(0, c) for c in range(16)])
                + _strips(w_ff2[layer], [(r, c) for c in range(4) for r in range(4)]))

    out += mlp(0)
    out += _strips(w_in_ret[0], [(0, c) for c in range(24)])
    out += _strips(w_out_ret[0], [(r, c) for c in range(4) for r in range(2)])
    out += mlp(1)
    return np.stack(out)


def _caches(c0, c1, c2, swa):
    a, b, c, d = c0[0], c1[0], c2[0], swa[0]
    b = b.reshape(NB, P, 4, 2, NH, HD)
    c = c.reshape(NB, 64, 16, 2, NH, HD)[:, :, :4].transpose(0, 2, 1, 3, 4, 5).reshape(NB, 2, P, 2, NH, HD)
    d = np.repeat(d, NH // 2, axis=3)
    tiles = np.concatenate([a[:, None], b.transpose(0, 2, 1, 3, 4, 5), c, d[:, None]], axis=1)
    k, v = tiles[:, :, :, 0], tiles[:, :, :, 1]
    k = k.reshape(NB, 8, P, 2, 4, 2, HALF).transpose(0, 1, 4, 6, 3, 5, 2).reshape(NB, 8, P, 512)
    v = v.reshape(NB, 8, P, 512)

    def pack(t):
        return np.ascontiguousarray(t.reshape(NB, 8 // CT, CT, P, 512).transpose(0, 1, 3, 2, 4)
                                    .reshape(NB, 8 // CT, P, CT * 512))

    return pack(k), pack(v)


def _positions():
    return np.concatenate([np.arange(SEQ), np.tile(PAST + np.arange(NT), NB)])


def _trig():
    pos = _positions().astype(np.float32)
    out = []
    for half in (HALF, DK // 2):
        inv = np.float32(10000.0) ** (-np.arange(half, dtype=np.float32) * np.float32(2.0 / (2 * half)))
        ang = pos[None, :] * inv[np.arange(P) % half][:, None]
        out.append(np.stack([np.cos(ang), np.sin(ang)], axis=1))
    return np.stack(out).astype(np.float32)


def _masks():
    p = np.arange(P)[:, None]
    j = np.arange(2 * P)[None, :]
    diff = P + p - j
    rows = [(diff >= 0) & (diff <= w) & (diff % dil == 0) for w, dil in zip(WINS, DILS)]
    rows.append((diff >= 0) & (diff <= 127))
    pm = np.where(np.stack(rows, axis=1), 0.0, NEG).astype(np.float32)
    n, t = p // 16, p // 4 % 4
    j = np.arange(P)[None, :]
    n2, t2 = np.arange(NS)[None, :] // 4, np.arange(NS)[None, :] % 4
    own, upto = (n == n2) & (t == t2), (n == n2) & (t2 <= t)
    ok = np.concatenate([j >= t, np.ones((P, P), bool), j // 64 == t % 2, upto, own, own, j >= t + 1, upto], axis=1)
    dm = np.where(ok, 0.0, NEG).astype(np.float32)
    g = np.array(GAMMA)[None, :, None]
    i = np.arange(SEQ)[None, None, :]
    pp = np.arange(P)[:, None, None]
    big = np.where(i >= pp, g ** np.maximum(i - pp, 0), 0.0) / 16
    ti = np.arange(NS)[None, None, :]
    okk = (pp // 4 == ti // 4) & (pp % 4 <= ti % 4) & (pp < NS)
    sm = np.where(okk, g ** np.maximum(ti % 4 - pp % 4, 0), 0.0) / 16
    rm = np.concatenate([big, sm], axis=2).astype(np.float32)
    t = np.arange(NS) % NT
    gh = np.array(GAMMA)[:, None]
    dec = np.stack([gh ** (t + 1), gh ** (NT - 1 - t) / 16])
    dec = np.broadcast_to(dec[None], (P,) + dec.shape).astype(np.float32)
    return pm, dm, rm, np.ascontiguousarray(dec)


def _columns(gains, sinks):
    col = np.zeros((P, N_COL), np.float32)
    col[:, C_GAIN:C_GAIN + 64] = gains.reshape(8, KT, P).transpose(2, 0, 1).reshape(P, 64)
    col[:, C_SINKP:C_SINKP + 8] = NEG
    col[:, C_SINKP + 8:C_SINKP + 16] = sinks[0][None, :]
    s = sinks[0].reshape(2, 4)
    for a in range(2):
        col[:, C_SINKD + 2 * a] = NEG
        col[:, C_SINKD + 2 * a + 1] = np.tile(s[a], P // 4)
    j = np.arange(SEQ).reshape(2, P)
    for tb in range(2):
        for h in range(NHR):
            col[:, C_KDEC + tb * NHR + h] = GAMMA[h] ** (SEQ - 1 - j[tb]) / 16
    col[:, C_EPS] = EPS
    col[:, C_GNEPS] = GN_EPS
    return col


def _matrices():
    m = np.zeros((P, 7, P), np.float32)
    m[:, 0] = np.eye(P)
    m[:, 1] = 1.0 / D
    m[:, 2] = 1.0 / DV
    for s in range(2):
        for z in range(2):
            for c in range(P):
                m[(2 * s + z) * HALF + c % HALF, 3 + 2 * s + z, c] = 1.0
    return m


def kernel(x_prompt, x_sample, cache_dil_w128, cache_dil_w512, cache_dil_w2048, cache_swa, state_ret,
           norm_gains, w_in_mix, w_out_mix, attn_sinks, w_in_ret, w_out_ret, w_ff1, w_ff2):
    import concourse.bacc as _bacc
    from concourse.bass_utils import run_bass_kernel_spmd as _run

    arr = [np.asarray(a) for a in (x_prompt, x_sample, cache_dil_w128, cache_dil_w512, cache_dil_w2048, cache_swa,
                                   state_ret, norm_gains, w_in_mix, w_out_mix, attn_sinks, w_in_ret, w_out_ret,
                                   w_ff1, w_ff2)]
    xp, xs, c0, c1, c2, swa, st, gains, wim, wom, sinks, wir, wor, wf1, wf2 = arr
    xcat = np.concatenate([xp[0], xs.reshape(NS, D)], axis=0)
    kc, vc = _caches(c0, c1, c2, swa)
    pm, dm, rm, dec = _masks()
    ins = {
        "wst": _weights(wim, wom, wir, wor, wf1, wf2),
        "x_in": np.ascontiguousarray(xcat.T.reshape(KT, P, T).transpose(1, 0, 2)),
        "cols": _columns(gains, sinks), "trig": _trig(), "mats": _matrices(),
        "pmask": pm, "dmask": dm, "rmask": rm, "qkdec": dec, "kcache": kc, "vcache": vc,
        "state": np.ascontiguousarray(st[0]),
    }
    outs = {
        "x_out": (P, KT, T), "k_out": (P, 4 * NBR, T), "v_out": (P, 4 * NG + 1, T),
        "pstate_out": (NHR, DK, DV), "sstate_out": (NB, NHR, DK, DV),
    }
    nc = _bacc.Bacc("TRN2", target_bir_lowering=False, num_devices=1)
    args = [nc.dram_tensor(n, a.shape, mybir.dt.from_np(a.dtype), kind="ExternalInput").ap() for n, a in ins.items()]
    args += [nc.dram_tensor(n, s, F32, kind="ExternalOutput").ap() for n, s in outs.items()]
    build_program(nc, *args)
    r = _run(nc, [ins], core_ids=[0]).results[0]

    xt = np.asarray(r["x_out"]).transpose(2, 1, 0).reshape(T, D)
    k = np.asarray(r["k_out"]).reshape(4, HALF, NBR, 2, 2, T).transpose(5, 2, 3, 0, 4, 1).reshape(T, NBR, NH, HD)
    v = np.asarray(r["v_out"]).transpose(2, 1, 0).reshape(T, (4 * NG + 1) * P)
    va = v[:, :4 * NG * P].reshape(T, NG, NH, HD)
    vb = v[:, 4 * NG * P:].reshape(T, 2, HD)
    rows = []
    for g in range(NG):
        kv = np.stack([k[:, g], va[:, g]], axis=1)
        rows += [kv[SEQ - min(WINS[g], SEQ):SEQ][None, None], kv[SEQ:].reshape(1, NB, NT, 2, NH, HD)]
    kv = np.stack([k[:, NG, ::4], vb], axis=1)
    rows += [kv[SEQ - P:SEQ][None, None], kv[SEQ:].reshape(1, NB, NT, 2, 2, HD)]
    return (xt[:SEQ][None], xt[SEQ:].reshape(NB, NT, D), *[np.ascontiguousarray(a) for a in rows],
            np.asarray(r["pstate_out"])[None, None], np.asarray(r["sstate_out"])[None])
```

```python
from contextlib import ExitStack

import numpy as np

import concourse.bass as bass
from concourse import mybir

F32 = mybir.dt.float32
F32R = mybir.dt.float32r
ALU = mybir.AluOpType
ACT = mybir.ActivationFunctionType
AX = mybir.AxisListType
ds = bass.ds

P = 128
D = 1024
KT = D // P
SEQ = 256
NB, NT = 8, 4
NS = NB * NT
T = SEQ + NS
PAST = 1024
HD = 64
HALF = HD // 2
NH = 8
NG = 3
DILS = (1, 4, 16)
WINS = (128, 512, 2048)
NBR = NG + 1
NHR, DK, DV = 4, 256, 512
DFF = 4 * D
SC = 256
RAWS = 4
SPL = 2
GBUF = 2
EPS = 1e-6
GN_EPS = 1e-5
NEG = -1e30
SCALE = HD ** -0.5
NKT = 8
CD = (NKT - 1) * P
CW = NKT * P
CB = ((1, 0, 512), (2, 512, 256), (0, 768, P), (3, CD, P))
CLOAD = 1024
CL = 4
NG_D = NB // 4
SROW = CW + P
CSLOTS = 8

N_Q, N_KV, N_BKV, N_MIXOUT, N_FF, N_RETIN, N_RETOUT = 8, 12, 1, 4, 16, 24, 8
S_Q = 0
S_KV = S_Q + N_Q
S_BKV = S_KV + N_KV
S_MIXOUT = S_BKV + N_BKV
S_FF1A = S_MIXOUT + N_MIXOUT
S_FF2A = S_FF1A + N_FF
S_RETIN = S_FF2A + N_FF
S_RETOUT = S_RETIN + N_RETIN
S_FF1B = S_RETOUT + N_RETOUT
S_FF2B = S_FF1B + N_FF
N_STRIPS = S_FF2B + N_FF

C_GAIN = 0
C_SINKP = C_GAIN + 64
C_SINKD = C_SINKP + 16
C_KDEC = C_SINKD + 4
C_EPS = C_KDEC + 8
C_GNEPS = C_EPS + 1
C_HEAD = C_GNEPS + 1
N_COL = C_HEAD + 4
GAMMA = [1.0 - 2.0 ** (-5.0 - h) for h in range(NHR)]




def build_program(nc, wst, x_in, cols, trig, mats, pmask, dmask, rmask, qkdec, kcache, vcache, state,
                  x_out, k_out, v_out, pstate_out, sstate_out):
    with ExitStack() as ctx:
        def sem(name):
            return ctx.enter_context(nc.semaphore(name))

        def sb(name, shape, dt=F32, scope=ctx):
            return scope.enter_context(nc.sbuf_tensor(name, shape, dt))

        raw = sb("raw", [P, RAWS, KT * SC])
        wH = sb("wH", [P, SPL, KT * SC], F32R)
        wL = sb("wL", [P, SPL, KT * SC], F32R)
        x = sb("x", [P, KT, T])
        hH = sb("hH", [P, KT, T], F32R)
        hL = sb("hL", [P, KT, T], F32R)
        y = sb("y", [P, KT, T])
        sq = sb("sq", [P, 2, T])
        acc = sb("acc", [P, 2, T])
        sumsq = sb("sumsq", [P, T])
        rms = sb("rms", [P, T])
        rs_post = sb("rs_post", [P, T])
        rs_pre = sb("rs_pre", [P, T])
        tmp = sb("tmp", [P, 2, T])
        trig_sb = sb("trig_sb", [P, 2, T])
        trigR = sb("trigR", [P, 2, T])
        col = sb("col", [P, N_COL])
        mat = sb("mat", [P, 7, P])

        NVT = 4 * NG + 1
        with ExitStack() as mix:
            qT = sb("qT", [P, 4 * NBR, T], F32, mix)
            kT = sb("kT", [P, 4 * NBR, T], F32, mix)
            vtok = sb("vtok", [P, 2, NVT * P], F32, mix)
            vnew = tmp[:, :, :].rearrange("p a t -> p (a t)")[:, 0:NH * HD]
            pm = sb("pm", [P, NBR, 2 * P], F32, mix)
            dm = sb("dm", [P, CW], F32, mix)
            dm_new = trig_sb[:, 0, 0:NG_D * P]
            cache_sb = sb("cache_sb", [P, CSLOTS // 2, CLOAD], F32, mix)
            with ExitStack() as s1:
                vT = sb("vT", [P, NVT, T], F32, s1)
            with ExitStack() as s2:
                p_sb = sb("p_sb", [P, 2, 9 * P], F32, s2)
                pt_sb = sb("pt_sb", [P, 3, 3 * P], F32, s2)
                small = sb("small", [P, 2, 10], F32, s2)
            with ExitStack() as s3:
                st_sb = sb("st_sb", [P, NG_D, SROW], F32, s3)
                nt_sb = sb("nt_sb", [P, NG_D * P], F32, s3)
                dsm = sb("dsm", [P, NG_D, 20], F32, s3)
            sp_sb = y[:, :, :].rearrange("p k t -> p (k t)").rearrange("p (g c) -> p g c", g=NG_D)
            kz = y[:, 0, :]
            HELD = S_MIXOUT + 2
            qm = [raw[:, (HELD + 2 + i) % RAWS, 0:NG * 2 * SEQ].rearrange("p (b z t) -> p b z t", b=NG, z=2) for i in range(2)]
            cslot = [cache_sb[:, i, :] for i in range(4)] + [
                raw[:, (HELD + 2 + i // 2) % RAWS, i % 2 * CLOAD:i % 2 * CLOAD + CLOAD] for i in range(4)]
            qz = [raw[:, s % RAWS, :].rearrange("p (a c) -> p a c", a=8) for s in (HELD, HELD + 1)]
        with ExitStack() as ffs:
            aH = sb("aH", [P, 4 * KT, T], F32R, ffs)
            aL = sb("aL", [P, 4 * KT, T], F32R, ffs)
            relu_sb = sb("relu_sb", [P, 2, 2, T], F32, ffs)
            a_sb = sb("a_sb", [P, 2, T], F32, ffs)
        with ExitStack() as ret:
            with ExitStack() as r1:
                vTr = sb("vTr", [P, 4 * NHR, T], F32, r1)
                gate = sb("gate", [P, 4 * NHR, T], F32, r1)
            with ExitStack() as r2:
                yH = sb("yH", [P, 4 * NHR, T], F32R, r2)
                yL = sb("yL", [P, 4 * NHR, T], F32R, r2)
                qr = sb("qr", [P, 2 * NHR, T], F32, r2)
                kr = sb("kr", [P, 2 * NHR, T], F32, r2)
                sslot = sb("sslot", [P, 4, 2 * DV], F32, r2)
                vtok_r = sb("vtok_r", [P, 2, DV], F32, r2)
                ktok_r = sb("ktok_r", [P, 2, DK], F32, r2)
                vpad = sb("vpad", [P, 4, 8, NS], F32, r2)
                kpad = sb("kpad", [P, 2, 8, NS], F32, r2)
                rm = sb("rm", [P, NHR, T], F32, r2)
                dec = sb("dec", [P, 2, NHR, NS], F32, r2)
            vtok_s = sq[0:NS, :, :].rearrange("p a t -> p (a t)")[:, 0:DV]
            os_sb = sq[:, :, :].rearrange("p a t -> p (a t)")[:, 0:DV]
            at_sb = trig_sb[:, :, :].rearrange("p a t -> p (a t)")[:, 0:13 * NS]
            kd = rs_pre[:, 0:8 * NS].rearrange("p (h c) -> p h c", h=8)
            qpad = trigR
            own_q = trigR[:, :, :].rearrange("p z (n c) -> p z n c", c=NS + NT)[:, :, :, 0:NT]
            kst = hH[:, :, :].rearrange("p k t -> p (k t)")[:, 0:4 * DK].rearrange("p (h a c) -> p h a c", h=2, c=DK)
            vst = hL[:, :, :].rearrange("p k t -> p (k t)")[:, 0:4 * DV].rearrange("p (h a c) -> p h a c", h=2, c=DV)
            o_sb = y[:, 0:4, :]
            oc_sb = y[:, 4:8, :]
            ps_sb = [a[:, :, :].rearrange("p a t -> p (a t)")[:, 0:DV] for a in (tmp, acc)]

        banks = ctx.enter_context(nc.psum_tensor("banks", [P, 8, 512], F32))

        def G(j):
            return banks[:, 2 * (j % 2):2 * (j % 2) + 2, 0:T]

        def both(a):
            return a.unsqueeze(1).broadcast_to([P, 2, T])

        ident, mean_d, mean_v = mat[:, 0, :], mat[:, 1, :], mat[:, 2, :]
        MS = banks[:, 7, 0:T]
        S45 = banks[:, 4:6, :].rearrange("p a c -> p (a c)")
        eps, gn_eps = col[:, C_EPS:C_EPS + 1], col[:, C_GNEPS:C_GNEPS + 1]

        def os_rows(h):
            return slice(32 * (1 + h % 2), 32 * (1 + h % 2) + NS)

        def own_head(g, hp, e):
            r = slice(64 * e, 64 * e + 64)
            src = banks[r, 2 * g:2 * g + 2, hp * P:hp * P + P].rearrange("p m (n s t h) -> p m n s t h", n=4, s=2, t=NT)
            return (lambda dst: dst[r, :, SEQ + 16 * g:SEQ + 16 * g + 16].rearrange(
                        "p (m k) (n t) -> p m k n t", m=2, t=NT)[:, :, hp, :, :],
                    src[:, :, :, hp // 2, :, 2 * (hp % 2) + e])

        def gain(layer, norm, k):
            c = C_GAIN + (4 * layer + norm) * KT + k
            return col[:, c:c + 1]

        cols_in, mats_in, x_landed, trig_in, mask_in, rmask_in = map(
            sem, ("cols_in", "mats_in", "x_landed", "trig_in", "mask_in", "rmask_in"))
        w_landed = [sem(f"w_landed{i}") for i in range(RAWS)]
        h_round, l_split, strip_used = map(sem, ("h_round", "l_split", "strip_used"))
        g_dve, y_copied, g_act = map(sem, ("g_dve", "y_copied", "g_act"))
        hx_round, hx_split = map(sem, ("hx_round", "hx_split"))
        sq_sum, ms_done, rms_done, rs_done = map(sem, ("sq_sum", "ms_done", "rms_done", "rs_done"))
        t_done, x_done, xsq_done, xacc = map(sem, ("t_done", "x_done", "xsq_done", "xacc"))
        rope_mul, rope_out, trigR_done, kz_done, sel_done = map(
            sem, ("rope_mul", "rope_out", "trigR_done", "kz_done", "sel_done"))
        v_turned, v_tok, k_stored, v_stored = map(sem, ("v_turned", "v_tok", "k_stored", "v_stored"))
        scored, q_masked, masked, max_scaled, negmax, exp_done, l_done, p_norm, p_turned, pt_copied, pv_done = map(sem, (
            "scored", "q_masked", "masked", "max_scaled", "negmax", "exp_done", "l_done", "p_norm", "p_turned", "pt_copied",
            "pv_done"))
        o_round, o_split, q_zero, q_spread = map(sem, ("o_round", "o_split", "q_zero", "q_spread"))
        c_landed = [sem(f"c_landed{i}") for i in range(CSLOTS)]
        c_used = sem("c_used")
        d_newT, d_newcopied, d_newrow, d_scored, d_masked, d_max, d_max2, d_negmax, d_exp, d_l, d_norm, d_pturned, d_ptcopied = map(
            sem, ("d_newT", "d_newcopied", "d_newrow", "d_scored", "d_masked", "d_max", "d_max2", "d_negmax", "d_exp", "d_l",
                  "d_norm", "d_pturned", "d_ptcopied"))
        d_out, d_ocopA, d_ocopB, d_oturned = map(sem, ("d_out", "d_ocopA", "d_ocopB", "d_oturned"))
        relu_sq, a_round, a_split = map(sem, ("relu_sq", "a_round", "a_split"))
        fin = sem("fin")
        gated = sem("gated")
        s_landed = [sem(f"s_landed{i}") for i in range(4)]
        s_stored = [sem(f"s_stored{i}") for i in range(4)]
        r_dec, r_zero, r_padH, r_padL, r_turned, r_tok, r_pturned, r_stack = map(
            sem, ("r_dec", "r_zero", "r_padH", "r_padL", "r_turned", "r_tok", "r_pturned", "r_stack"))
        os_copied, os_turned = map(sem, ("os_copied", "os_turned"))
        r_scored, r_decayed, r_state, r_scopied, r_out, r_sread, r_outer, r_updated = map(
            sem, ("r_scored", "r_decayed", "r_state", "r_scopied", "r_out", "r_sread", "r_outer", "r_updated"))
        gn_o, gn_mean, gn_sq, gn_rms, gn_rs, yr_round, yr_split, ps_stored = map(
            sem, ("gn_o", "gn_mean", "gn_sq", "gn_rms", "gn_rs", "yr_round", "yr_split", "ps_stored"))

        block = ctx.enter_context(nc.Block())

        NU = 2 * NH
        GD_MIX, GD_FF1A, GD_RET, GD_FF1B = 0, 23, 39, 63

        def loop(eng, first, count, body, peel=0):
            assert count % RAWS == 0
            for i in range(peel):
                for u in range(RAWS):
                    body(RAWS * i + first + u, u, i)
            if peel < count // RAWS:
                with eng.Fori(peel, count // RAWS) as i:
                    for u in range(RAWS):
                        body(RAWS * i + (first + u), u, i)

        @block.sync
        def _(sp):
            sp.dma_start(col[:, :], cols).then_inc(cols_in, 16)
            sp.dma_start(x[:, :, :], x_in).then_inc(x_landed, 16)
            sp.dma_start(raw[:, 0, :], wst[0]).then_inc(w_landed[0], 16)
            sp.dma_start(mat[:, :, :], mats).then_inc(mats_in, 16)
            for s in range(1, RAWS):
                sp.dma_start(raw[:, s, :], wst[s]).then_inc(w_landed[s], 16)
            sp.dma_start(trig_sb[:, :, :], trig[0]).then_inc(trig_in, 16)
            sp.dma_start(pm[:, :, :], pmask).then_inc(mask_in, 16)
            sp.dma_start(dm[:, :], dmask[:, 0:CW]).then_inc(mask_in, 16)
            sp.wait_ge(trigR_done, 1)
            sp.dma_start(dm_new[:, :], dmask[:, CW:CW + NG_D * P]).then_inc(mask_in, 16)

            def strip(s, slot):
                sp.wait_ge(l_split, s - RAWS + 1)
                sp.dma_start(raw[:, slot, :], wst[ds(s, 1)].rearrange("a p n -> (a p) n")).then_inc(w_landed[slot], 16)

            def strips(first, end):
                whole = (end - first) // RAWS * RAWS
                if whole:
                    loop(sp, first, whole, lambda s, u, i: strip(s, (first + u) % RAWS))
                for s in range(first + whole, end):
                    strip(s, s % RAWS)

            def cache_load(src, n, j, slot, used):
                if used is not None:
                    sp.wait_ge(c_used, used)
                sp.dma_start(cslot[slot], src[ds(n, 1), j].rearrange("a p n -> (a p) n")).then_inc(c_landed[slot], 16)

            strips(RAWS, HELD)
            for slot in range(CSLOTS):
                if slot == CSLOTS // 2:
                    sp.wait_ge(scored, NU)
                cache_load(kcache, slot // CL, slot % CL, slot, None)
            for src, first, before in ((kcache, 1, 0), (vcache, 0, CL * NB)):
                with sp.Fori(first, NB // 2) as m:
                    for slot in range(CSLOTS):
                        cache_load(src, 2 * m + slot // CL, slot % CL, slot, CSLOTS * m + (before + slot + 1 - CSLOTS))
            strips(HELD, HELD + 2)
            sp.wait_ge(c_used, 2 * CL * NB)
            strips(HELD + 2, RAWS + S_RETIN)
            sp.wait_ge(strip_used, S_RETIN)
            sp.dma_start(trig_sb[:, :, :], trig[1]).then_inc(trig_in, 16)
            sp.dma_start(rm[:, :, :], rmask).then_inc(rmask_in, 16)
            sp.dma_start(dec[:, :, :, :], qkdec).then_inc(rmask_in, 16)

            def state_load(n, h):
                j = n % 4
                k = 2 * h + n // 4
                if k:
                    sp.wait_ge(s_stored[j], 16 * k)
                sp.dma_start(sslot[:, j, :].rearrange("p (z e) -> p z e", z=2),
                             state[n, h].rearrange("(z p) e -> p z e", p=P)).then_inc(s_landed[j], 16)

            for n in range(4):
                state_load(n, 0)
            strips(RAWS + S_RETIN, RAWS + S_RETOUT)
            for h in range(NHR):
                for n in range(4 if h == 0 else 0, NB):
                    state_load(n, h)
            strips(RAWS + S_RETOUT, N_STRIPS)

        @block.gpsimd
        def _(pool):
            def sum_squares(b):
                for k in range(KT):
                    pool.wait_ge(xsq_done, KT * b + k + 1)
                    if k == 0:
                        nc.gpsimd.tensor_copy(sumsq[:, :], sq[:, 0, :]).then_inc(xacc, 1)
                    else:
                        pool.wait_ge(xacc, KT * b + k)
                        nc.gpsimd.tensor_tensor(sumsq[:, :], sumsq[:, :], sq[:, k % 2, :], ALU.add).then_inc(xacc, 1)

            sum_squares(0)
            pool.wait_ge(g_dve, GBUF + 21)
            pool.dma_start(v_out, vT[:, :, :]).then_inc(v_stored, 16)
            pool.wait_ge(rope_out, 1 + 2 * 4 * NBR)
            pool.dma_start(k_out, kT[:, :, :]).then_inc(k_stored, 16)
            pool.wait_ge(l_split, S_BKV + 1)
            for a in range(2):
                nc.gpsimd.memset(qz[a], 0.0).then_inc(q_zero, 1)
            pool.wait_ge(q_zero, 2)
            for br in range(NBR):
                for s in range(2):
                    for h in range(4):
                        r = slice(32 * h, 32 * h + 32)
                        t0 = 2 * (2 * (br % 2) + s)
                        nc.gpsimd.tensor_copy(
                            qz[br // 2][r, t0:t0 + 2, :].rearrange("p z (n s t h) -> p z n s t h", n=NB, s=2, t=NT)[
                                :, :, :, s, :, h],
                            qT[r, 4 * br + 2 * s:4 * br + 2 * s + 2, SEQ:T].rearrange(
                                "p z (n t) -> p z n t", t=NT)).then_inc(q_spread, 1)
            sum_squares(1)
            sum_squares(2)
            pool.wait_ge(strip_used, S_RETIN)
            nc.gpsimd.memset(vpad[:, :, :, :], 0.0).then_inc(r_zero, 1)
            nc.gpsimd.memset(kpad[:, :, :, :], 0.0).then_inc(r_zero, 1)
            for h in range(NHR):
                for z in range(2):
                    pool.wait_ge(r_scopied, 2 * h + z + 1)
                    pool.dma_start(pstate_out[h, z * P:(z + 1) * P, :], ps_sb[z]).then_inc(ps_stored, 16)
                for n in range(NB):
                    pool.wait_ge(r_updated, 2 * (NB * h + n + 1))
                    pool.dma_start(sstate_out[n, h].rearrange("(z p) e -> p z e", p=P),
                                   sslot[:, n % 4, :].rearrange("p (z e) -> p z e", z=2)).then_inc(s_stored[n % 4], 16)
            sum_squares(3)
            for k in range(0, KT, 2):
                pool.wait_ge(x_done, 3 * KT + k + 2)
                pool.dma_start(x_out[:, k:k + 2, :], x[:, k:k + 2, :]).then_inc(fin, 16)
            pool.wait_ge(fin, 16 * KT // 2)
            pool.wait_ge(k_stored, 16)
            pool.wait_ge(v_stored, 16)
            pool.wait_ge(ps_stored, 16 * 2 * NHR)
            for j in range(4):
                pool.wait_ge(s_stored[j], 16 * 2 * NHR)

        @block.tensor
        def _(pe):
            def product(s, u, out, hi, lo, start=True, stop=True):
                pe.wait_ge(l_split, s + 1)
                for m in range(2):
                    for k in range(KT):
                        mm = tile_product(u, out, hi, lo, m, k, start, stop)
                mm.then_inc(strip_used, 1)

            def tile_product(u, out, hi, lo, m, k, start=True, stop=True):
                c = slice(k * SC + m * P, k * SC + m * P + P)
                first, last = start and k == 0, stop and k == KT - 1
                nc.tensor.matmul(out[:, m, :], wH[:, u % 2, c], hi[:, k, :], start=first, stop=False)
                nc.tensor.matmul(out[:, m, :], wH[:, u % 2, c], lo[:, k, :], start=False, stop=False)
                return nc.tensor.matmul(out[:, m, :], wL[:, u % 2, c], hi[:, k, :], start=False, stop=last)

            def mean_square(which, of, ready, count):
                pe.wait_ge(ready, count)
                nc.tensor.matmul(MS, which, of, start=True, stop=True).then_inc(ms_done, 1)

            def first_product(b, s, out):
                pe.wait_ge(l_split, s + 1)
                for k in range(KT):
                    pe.wait_ge(hx_split, KT * b + k + 1)
                    for m in range(2):
                        mm = tile_product(s, out, hH, hL, m, k)
                mm.then_inc(strip_used, 1)
                if b == 0:
                    pe.wait_ge(mats_in, 16)
                mean_square(mean_d, sumsq[:, :], xacc, KT * (b + 1))

            def is_first(i, u):
                return isinstance(i, int) and i == 0 and u == 0

            def in_mix(s, u, i, j):
                pe.wait_ge(g_dve, j + GBUF - 1)
                if is_first(i, s - S_Q if isinstance(s, int) else 1):
                    first_product(0, s, G(u))
                else:
                    product(s, s if isinstance(s, int) else u, G(u), hH, hL)

            loop(pe, S_Q, N_Q, lambda s, u, i: in_mix(s, u, i, RAWS * i + u), peel=1)
            loop(pe, S_KV, N_KV, lambda s, u, i: in_mix(s, u, i, RAWS * i + (N_Q + u)))
            in_mix(S_BKV, 0, None, 20)
            pe.wait_ge(kz_done, 1)
            for s in range(2):
                pe.wait_ge(g_dve, GBUF + 20 + s)
                for z in range(2):
                    mm = nc.tensor.matmul(G(21 + s)[:, z, :], mat[:, 3 + 2 * s + z, :], kz[:, :], start=True, stop=True)
                mm.then_inc(sel_done, 1)
            pe.wait_ge(g_dve, GBUF + 21)
            for i in range(7):
                if i >= 2:
                    pe.wait_ge(v_tok, 2 * (i - 1))
                b0 = 4 + 2 * (i % 2)
                for c in range(2 if i < 6 else 1):
                    for tb in range(3):
                        w = P if tb < 2 else NS
                        p0 = 0 if tb < 2 else NS * (i // 2)
                        out = banks[p0:p0 + w, b0 + tb // 2, (tb % 2) * 256 + c * P:(tb % 2) * 256 + c * P + P]
                        v = vT[:, 2 * i + c, tb * P:tb * P + w]
                        if tb < 2:
                            nc.tensor.transpose(out, v, ident)
                        else:
                            mm = nc.tensor.matmul(out, v, ident, start=True, stop=True)
                mm.then_inc(v_turned, 1)

            def branches(u):
                return list(range(NG)) if u < NH else [NG]

            def scores(u):
                s = u % NH // 4
                pe.wait_ge(q_masked, u + 1)
                if u:
                    pe.wait_ge(masked, 2 * u)
                for a, br in enumerate(branches(u)):
                    for z in range(2):
                        t = (2 * br + s) * 2 + z
                        nc.tensor.matmul(S45[:, a * 256:a * 256 + 256], qm[u % 2][:, a, z, P:2 * P], kT[:, t, 0:2 * P],
                                         start=z == 0, stop=z == 1)
                for a, br in enumerate(branches(u)):
                    for z in range(2):
                        t = (2 * br + s) * 2 + z
                        mm = nc.tensor.matmul(banks[:, 6, a * P:a * P + P], qm[u % 2][:, a, z, 0:P], kT[:, t, 0:P],
                                              start=z == 0, stop=z == 1)
                mm.then_inc(scored, 1)

            def turn_p(u):
                pe.wait_ge(p_norm, 2 * (u + 1))
                if u:
                    pe.wait_ge(pt_copied, u)
                n = len(branches(u))
                for a in range(n):
                    for c, at in enumerate((n * 256 + a * P, a * 256, a * 256 + P)):
                        mm = nc.tensor.transpose(banks[:, a, c * P:c * P + P], p_sb[:, u % 2, at:at + P], ident)
                mm.then_inc(p_turned, 1)

            def pv(u):
                j = u % NH
                pe.wait_ge(pt_copied, u + 1)
                if u % 2 == 0 and u:
                    pe.wait_ge(o_split, u // 2)
                r = slice(64 * (j % 2), 64 * (j % 2) + 64)
                n = len(branches(u))
                for a, br in enumerate(branches(u)):
                    v0 = 4 * br * P + (j * HD if br < NG else j // 4 * HD)
                    nc.tensor.matmul(banks[r, 3, 0:2 * P], vtok[:, 0, v0:v0 + HD], pt_sb[:, a, 0:2 * P],
                                     start=a == 0, stop=False)
                    mm = nc.tensor.matmul(banks[r, 3, P:2 * P], vtok[:, 1, v0:v0 + HD], pt_sb[:, a, 2 * P:3 * P],
                                          start=False, stop=a == n - 1)
                mm.then_inc(pv_done, 1)

            pe.wait_ge(v_tok, 2 * 7)
            scores(0)
            for u in range(NU):
                if u + 1 < NU:
                    scores(u + 1)
                if u:
                    pv(u - 1)
                turn_p(u)
            pv(NU - 1)

            def load_at(n, j):
                return (CL * n + j) % CSLOTS, (CL * n + j) // CSLOTS

            pe.wait_ge(q_spread, 8 * NBR)
            pe.wait_ge(o_split, NH)
            for br in range(NBR):
                for t in range(4):
                    mm = nc.tensor.matmul(banks[NS * br:NS * br + NS, 0, 0:NG_D * P], kT[:, 4 * br + t, SEQ:T],
                                          qz[br // 2][:, 4 * (br % 2) + t, :], start=t == 0, stop=t == 3)
            mm.then_inc(d_newT, 1)
            pe.wait_ge(d_newcopied, 1)
            for g in range(NG_D):
                mm = nc.tensor.transpose(banks[:, 0, 256 + g * P:256 + g * P + P], nt_sb[:, g * P:g * P + P], ident)
            mm.then_inc(d_newrow, 1)
            for g in range(NG_D):
                for q in range(4):
                    for j in range(CL):
                        slot, before = load_at(4 * g + q, j)
                        pe.wait_ge(c_landed[slot], 16 * (before + 1))
                        for br, k0, kn in CB:
                            mm = nc.tensor.matmul(
                                banks[32 * q:32 * q + 32, 4 + 2 * g + k0 // 512, k0 % 512:k0 % 512 + kn],
                                qz[br // 2][:, 4 * (br % 2) + j, P * g + 32 * q:P * g + 32 * q + 32], cslot[slot][:, k0:k0 + kn],
                                start=j == 0 and k0 % 512 == 0, stop=j == CL - 1, skip_group_check=True)
                        mm.then_inc(c_used, 1)
            for g in range(NG_D):
                pe.wait_ge(d_norm, 2 * g + 2)
                for i in range(NKT + 1):
                    at = (i * P if i < NKT - 1 else CD + 96 if i == NKT - 1 else CD)
                    w = P if i < NKT else 96
                    mm = nc.tensor.transpose(banks[0:w, 1 + i // 4, i % 4 * P:i % 4 * P + P],
                                             sp_sb[:, g, at:at + w], ident)
                at = SROW - NS
                mm = nc.tensor.matmul(banks[96:P, 3, 0:P], sp_sb[:, g, at:at + NS], ident, start=True, stop=True)
                mm.then_inc(d_pturned, 1)
                pe.wait_ge(d_ptcopied, g + 1)
                for m, r in ((0, slice(0, 96)), (1, slice(96, P))):
                    nc.tensor.matmul(banks[:, 4 + 2 * g + m, :],
                                     st_sb[r, g, CW:SROW], vnew[r, :],
                                     start=True, stop=False, skip_group_check=True)
                for q in range(4):
                    for j in range(CL):
                        slot, before = load_at(NB + 4 * g + q, j)
                        pe.wait_ge(c_landed[slot], 16 * (before + 1))
                        for c in range(2):
                            i = 2 * j + c
                            mm = nc.tensor.matmul(
                                banks[32 * q:32 * q + 32, 4 + 2 * g + i // (NKT - 1), :],
                                st_sb[:, g, i * P + 32 * q:i * P + 32 * q + 32],
                                cslot[slot][:, c * 512:c * 512 + 512], start=False, stop=False, skip_group_check=True)
                        mm.then_inc(c_used, 1)
            for g in range(NG_D):
                pe.wait_ge(d_ocopA, g + 1)
                pe.wait_ge(d_ocopB, g + 1)
                for m in range(2):
                    for hp in range(4):
                        c = m * 512 + hp * P
                        mm = nc.tensor.transpose(banks[:, 2 * g + m, hp * P:hp * P + P], sp_sb[:, g, c:c + P], ident)
                mm.then_inc(d_oturned, 1)

            pe.wait_ge(o_split, NH + 8 * NG_D)
            for j in range(N_MIXOUT):
                if j >= 2:
                    pe.wait_ge(g_act, j - 1)
                product(S_MIXOUT + j, S_MIXOUT + j, G(j), hH, hL)

            def mlp(first1, first2, gd, ga, base, b):
                def up(s, u, i):
                    pe.wait_ge(g_dve, RAWS * i + (GBUF - 1 + gd + u))
                    if is_first(i, u):
                        first_product(b, s, G(u))
                    else:
                        product(s, first1 + u, G(u), hH, hL)

                loop(pe, first1, N_FF, up, peel=1)
                with pe.Fori(0, 2) as i:
                    for u in range(8):
                        kq = u % 4
                        if kq == 0:
                            pe.wait_ge(g_act, 2 * i + (ga + u // 4 - 1))
                        pe.wait_ge(a_split, 1 + base + 4 * (kq + 1))
                        product(8 * i + (first2 + u), first2 + u, G(u // 4), aH[:, 8 * kq:8 * kq + 8, :],
                                aL[:, 8 * kq:8 * kq + 8, :], start=kq == 0, stop=kq == 3)

            mean_square(mean_d, acc[:, 0, :], sq_sum, 4)
            mlp(S_FF1A, S_FF2A, GD_FF1A, 4, 0, 1)
            mean_square(mean_d, acc[:, 0, :], sq_sum, 8)

            def in_ret(s, u, i):
                pe.wait_ge(g_dve, RAWS * i + (GBUF - 1 + GD_RET + u))
                if is_first(i, u):
                    first_product(2, s, G(u))
                else:
                    product(s, S_RETIN + u, G(u), hH, hL)

            loop(pe, S_RETIN, N_RETIN, in_ret, peel=1)

            def turn_head(h):
                for c in range(4):
                    for tb in range(2):
                        nc.tensor.transpose(banks[:, tb, c * P:c * P + P], vTr[:, 4 * h + c, tb * P:tb * P + P], ident)
                    nc.tensor.transpose(banks[0:NS, 3, c * P:c * P + P], vTr[:, 4 * h + c, SEQ:T], ident)
                for z in range(2):
                    for tb in range(2):
                        c = tb * DK + z * P
                        mm = nc.tensor.transpose(banks[:, 2, c:c + P], kr[:, 2 * h + z, tb * P:tb * P + P], ident)
                mm.then_inc(r_turned, 1)

            def turn_samples(h):
                pe.wait_ge(r_padL, 4 * (h + 1))
                pe.wait_ge(r_tok, 4 * (h + 1))
                for half in range(2):
                    for c in range(4):
                        nc.tensor.transpose(banks[:, half, c * P:c * P + P],
                                            vpad[:, c, 4 * half:4 * half + 4, :].rearrange("p a b -> p (a b)"), ident)
                    for z in range(2):
                        c = half * DK + z * P
                        mm = nc.tensor.transpose(banks[:, 2, c:c + P],
                                                 kpad[:, z, 4 * half:4 * half + 4, :].rearrange("p a b -> p (a b)"), ident)
                mm.then_inc(r_pturned, 1)
                for cols_, kk, qq in ((slice(0, 256), slice(0, P), slice(0, SEQ)),
                                      (slice(256, 384), slice(P, SEQ), slice(P, SEQ)),
                                      (slice(384, 416), slice(SEQ, T), slice(SEQ, T))):
                    for z in range(2):
                        rows = kk.stop - kk.start
                        mm = nc.tensor.matmul(banks[0:rows, 3, cols_], kr[:, 2 * h + z, kk], qr[:, 2 * h + z, qq],
                                              start=z == 0, stop=z == 1)
                mm.then_inc(r_scored, 1)

            def prompt_state(h):
                pe.wait_ge(r_stack, 2 * (h + 1))
                for z in range(2):
                    for tb in range(2):
                        mm = nc.tensor.matmul(banks[:, z, :], ktok_r[:, tb, z * P:z * P + P], vtok_r[:, tb, :],
                                              start=tb == 0, stop=tb == 1)
                    mm.then_inc(r_state, 1)

            def outputs(h):
                pe.wait_ge(r_decayed, 3 * (h + 1))
                pe.wait_ge(r_scopied, 2 * (h + 1))
                for c in range(4):
                    nc.tensor.matmul(banks[:, c, 0:SEQ], vtok_r[:, 0, c * P:c * P + P], at_sb[:, 0:SEQ],
                                     start=True, stop=False)
                    nc.tensor.matmul(banks[:, c, P:SEQ], vtok_r[:, 1, c * P:c * P + P], at_sb[:, 256:384],
                                     start=False, stop=True)
                    mm = nc.tensor.matmul(banks[:, c, SEQ:T], vtok_s[:, c * P:c * P + P], at_sb[0:NS, 384:416],
                                          start=True, stop=True)
                mm.then_inc(r_out, 1)

            def states(h, n):
                pe.wait_ge(s_landed[n % 4], 16 * (2 * h + n // 4 + 1))
                if n == 0:
                    pe.wait_ge(r_dec, 6 + h)
                    if h >= 2:
                        pe.wait_ge(os_copied, h - 1)
                for z in range(2):
                    mm = nc.tensor.matmul(banks[os_rows(h), 5, :], qpad[:, z, NS * n:NS * n + NS],
                                          sslot[:, n % 4, z * DV:z * DV + DV], start=n == 0 and z == 0,
                                          stop=n == NB - 1 and z == 1, skip_group_check=True)
                mm.then_inc(r_sread, 1)
                r = slice(32 * (n % 4), 32 * (n % 4) + 32)
                for z in range(2):
                    if h or n:
                        pe.wait_ge(r_updated, 2 * (NB * h + n - 1) + z + 1)
                    nc.tensor.matmul(banks[:, 6 + z, :], kst[r, h % 2, n // 4, z * P:z * P + P], vst[r, h % 2, n // 4, :],
                                     start=True, stop=True).then_inc(r_outer, 1)

            def turn_read(h):
                pe.wait_ge(os_copied, h + 1)
                if h:
                    pe.wait_ge(gn_rms, h)
                r = os_rows(h)
                for c in range(4):
                    mm = nc.tensor.transpose(banks[:, 4, T + c * NS:T + (c + 1) * NS], os_sb[r, c * P:c * P + P], ident[r, r])
                mm.then_inc(os_turned, 1)

            def mean(h, e):
                pe.wait_ge(gn_o, 6 * h + (3 if e == 0 else 5))
                nc.tensor.matmul(banks[:, 4, 0:T], mean_v, sumsq[:, :], start=True, stop=True).then_inc(gn_mean, 1)

            pe.wait_ge(gated, 8)
            turn_head(0)
            turn_samples(0)
            prompt_state(0)
            outputs(0)
            for h in range(NHR):
                for n in range(NB):
                    states(h, n)
                    if h:
                        if n == 0:
                            turn_read(h - 1)
                        if n == 1:
                            mean(h - 1, 0)
                        if n == 2:
                            mean(h - 1, 1)
                    if h + 1 < NHR:
                        if n == 4:
                            pe.wait_ge(gn_o, 6 * h + 1)
                            turn_head(h + 1)
                        if n == 5:
                            turn_samples(h + 1)
                        if n == 6:
                            prompt_state(h + 1)
                        if n == 7:
                            outputs(h + 1)
            turn_read(NHR - 1)
            for e in range(2):
                mean(NHR - 1, e)

            pe.wait_ge(yr_split, NHR)
            with pe.Fori(0, 2) as i:
                for u in range(4):
                    kh = u % 2
                    if kh == 0:
                        pe.wait_ge(g_act, 2 * i + (8 + u // 2 - 1))
                    product(4 * i + (S_RETOUT + u), S_RETOUT + u, G(u // 2), yH[:, 8 * kh:8 * kh + 8, :],
                            yL[:, 8 * kh:8 * kh + 8, :], start=kh == 0, stop=kh == 1)
            mean_square(mean_d, acc[:, 0, :], sq_sum, 12)
            mlp(S_FF1B, S_FF2B, GD_FF1B, 12, N_FF, 3)
            mean_square(mean_d, acc[:, 0, :], sq_sum, 16)

        @block.scalar
        def _(act):
            def round_strip(s, at, i=0):
                act.wait_ge(w_landed[at % RAWS], 16 * i + 16 * (at // RAWS + 1))
                if at >= SPL:
                    act.wait_ge(strip_used, s - SPL + 1)
                nc.scalar.activation(wH[:, at % SPL, :], raw[:, at % RAWS, :], ACT.Copy).then_inc(h_round, 1)

            def next_strip(s, u, i, first):
                round_strip(s + SPL, first + u + SPL, i)

            def round_x(k, layer, norm):
                nc.scalar.activation(hH[:, k, :], x[:, k, :], ACT.Copy, scale=gain(layer, norm, k)).then_inc(hx_round, 1)

            def pre_norm(b, layer, norm):
                for k in range(KT):
                    if b:
                        act.wait_ge(x_done, KT * (b - 1) + k + 1)
                        round_x(k, layer, norm)
                    if k >= 2:
                        act.wait_ge(xacc, KT * b + k - 1)
                    nc.scalar.activation(sq[:, k % 2, :], x[:, k, :], ACT.Square).then_inc(xsq_done, 1)
                root(2 * b)

            def root(e):
                act.wait_ge(ms_done, e + 1)
                nc.scalar.activation(rms[:, :], MS, ACT.Sqrt, bias=eps).then_inc(rms_done, 1)

            def take_y(e, j, last_strip):
                act.wait_ge(strip_used, last_strip + 1)
                nc.scalar.activation(y[:, 2 * j:2 * j + 2, :], G(j), ACT.Copy).then_inc(y_copied, 1)
                if j >= 2:
                    act.wait_ge(sq_sum, 4 * e + j - 1)
                nc.scalar.activation((sq if j else acc)[:, :, :], G(j), ACT.Square).then_inc(g_act, 1)

            def down(e, s, j, last):
                if j is not None and last:
                    take_y(e, j, s)
                if s + SPL < N_STRIPS:
                    round_strip(s + SPL, s + SPL)
                if j is not None and not last:
                    take_y(e, j, s)

            def mlp(first1, first2, gd, base, e):
                def up(s, u, i):
                    next_strip(s, u, i, first1)
                    act.wait_ge(g_dve, RAWS * i + (GBUF + gd + u + 1))
                    act.wait_ge(a_split, RAWS * i + (1 + base + u))
                    nc.scalar.activation(a_sb[:, :, :], relu_sb[:, u % 2, :, :], ACT.Square).then_inc(relu_sq, 1)
                    act.wait_ge(relu_sq, RAWS * i + (1 + base + u + 1))
                    nc.scalar.activation(aH[:, ds(8 * i + 2 * u, 2), :], a_sb[:, :, :], ACT.Copy).then_inc(a_round, 1)

                loop(act, first1, N_FF, up)
                for u in range(N_FF):
                    down(e, first2 + u, u // 4 if u % 4 == 3 else None, u == N_FF - 1)
                root(2 * e + 1)

            act.wait_ge(cols_in, 16)
            act.wait_ge(x_landed, 16)
            nc.scalar.activation(rms[:, 0:1], col[:, 0:1], ACT.Copy).then_inc(relu_sq, 1)
            act.wait_ge(relu_sq, 1)
            for k in range(KT):
                round_x(k, 0, 0)
            for s in range(SPL):
                round_strip(s, s)
            pre_norm(0, 0, 0)
            for s in range(N_Q):
                next_strip(s, s, 0, 0)
            loop(act, S_KV, N_KV, lambda s, u, i: next_strip(s, u, i, S_KV))
            next_strip(S_BKV, 0, 0, S_BKV)
            for i in range(7):
                act.wait_ge(v_turned, i + 1)
                b0, n = 4 + 2 * (i % 2), 256 if i < 6 else 128
                nc.scalar.activation(vtok[:, 0:2, 256 * i:256 * i + n],
                                     banks[:, b0, :].rearrange("p (t c) -> p t c", t=2)[:, :, 0:n],
                                     ACT.Copy).then_inc(v_tok, 1)
                r = slice(NS * (i // 2), NS * (i // 2) + NS)
                if i < 6:
                    nc.scalar.activation(vnew[r, 256 * (i % 2):256 * (i % 2) + 256], banks[r, b0 + 1, 0:n],
                                         ACT.Copy).then_inc(v_tok, 1)
                else:
                    nc.scalar.activation(
                        vnew[r, :].rearrange("p (k f d) -> p k f d", k=2, f=4),
                        banks[r, b0 + 1, 0:n].rearrange("p (k d) -> p k d", k=2).unsqueeze(2).broadcast_to([NS, 2, 4, HD]),
                        ACT.Copy).then_inc(v_tok, 1)

            def exps(u):
                n = 3 if u < NH else 1
                act.wait_ge(negmax, u + 1)
                sm = small[:, u % 2, :]
                for b, c in ((0, slice(0, n * 256)), (1, slice(n * 256, n * 384))):
                    nc.scalar.activation(p_sb[:, u % 2, c], p_sb[:, u % 2, c], ACT.Exp, bias=sm[:, 2 + b:3 + b],
                                         scale=SCALE, accum_out=sm[:, 4 + b:5 + b]).then_inc(exp_done, 1)
                nc.scalar.activation(sm[:, 6:8], sm[:, 2:4], ACT.Exp,
                                     bias=col[:, C_SINKP + u:C_SINKP + u + 1]).then_inc(exp_done, 1)

            def copy_pt(u):
                n = 3 if u < NH else 1
                act.wait_ge(p_turned, u + 1)
                if u:
                    act.wait_ge(pv_done, u)
                nc.scalar.activation(pt_sb[:, 0:n, :], banks[:, 0:n, 0:384], ACT.Copy).then_inc(pt_copied, 1)

            def round_o(p):
                act.wait_ge(pv_done, 2 * (p + 1))
                nc.scalar.activation(hH[:, p, 0:SEQ], banks[:, 3, 0:SEQ], ACT.Copy).then_inc(o_round, 1)

            def pick_act(g):
                act.wait_ge(d_oturned, g + 1)
                for hp in range(4):
                    for e in range(2):
                        dst, src = own_head(g, hp, e)
                        nc.scalar.activation(dst(hH), src, ACT.Copy).then_inc(o_round, 1)

            exps(0)
            for u in range(NU):
                if u + 1 < NU:
                    exps(u + 1)
                copy_pt(u)
                if u >= 2 and u % 2 == 0:
                    round_o(u // 2 - 1)
            round_o(NH - 1)

            act.wait_ge(d_newT, 1)
            nc.scalar.activation(nt_sb[:, :], banks[:, 0, 0:NG_D * P], ACT.Copy).then_inc(d_newcopied, 1)
            for g in range(NG_D):
                act.wait_ge(d_negmax, 2 * (g + 1))
                for m, c in ((0, slice(0, CD + 96)), (1, slice(CD + 96, SROW))):
                    nc.scalar.activation(sp_sb[:, g, c], sp_sb[:, g, c], ACT.Exp, bias=dsm[:, g, 6 + m:7 + m], scale=SCALE,
                                         accum_out=dsm[:, g, 10 + m:11 + m]).then_inc(d_exp, 1)
                nc.scalar.activation(dsm[:, g, 12:14], dsm[:, g, 8:10], ACT.Exp).then_inc(d_exp, 1)
                act.wait_ge(d_pturned, g + 1)
                nc.scalar.activation(st_sb[:, g, :], banks[:, 1:4, :].rearrange("p a c -> p (a c)")[:, 0:SROW],
                                     ACT.Copy).then_inc(d_ptcopied, 1)
            for g in range(NG_D):
                act.wait_ge(c_used, CL * NB + 4 * CL * (g + 1))
                nc.scalar.activation(sp_sb[:, g, 0:512], banks[:, 4 + 2 * g, :], ACT.Copy).then_inc(d_ocopA, 1)
                if g:
                    pick_act(g - 1)
            pick_act(NG_D - 1)
            for j in range(N_MIXOUT):
                down(0, S_MIXOUT + j, j, j == N_MIXOUT - 1)
            root(1)
            pre_norm(1, 0, 2)
            act.wait_ge(k_stored, 16)
            mlp(S_FF1A, S_FF2A, GD_FF1A, 0, 1)
            pre_norm(2, 1, 0)
            loop(act, S_RETIN, 16, lambda s, u, i: next_strip(s, u, i, S_RETIN))

            def gate_silu(s, u, i):
                next_strip(s, u, i, S_RETIN + 16)
                act.wait_ge(g_dve, RAWS * i + (GBUF + GD_RET + 16 + u + 1))
                g = gate[:, ds(8 * i + 2 * u, 2), :]
                nc.scalar.activation(g, g, ACT.Silu).then_inc(gated, 1)

            loop(act, S_RETIN + 16, 8, gate_silu)

            def pad_head(h):
                if h == 0:
                    act.wait_ge(r_zero, 2)
                    act.wait_ge(r_dec, NHR)
                    act.wait_ge(gated, 8)
                else:
                    act.wait_ge(r_pturned, h)
                for p in range(2):
                    nc.scalar.activation(
                        kpad[:, :, :, 4 * p:4 * p + 4].bitcast(F32R),
                        kd[:, 2 * h:2 * h + 2, :].rearrange("p z (n t) -> p z n t", t=NT), ACT.Copy).then_inc(r_padH, 1)
                for p in range(2):
                    nc.scalar.activation(
                        vpad[:, :, :, 8 * p:8 * p + 4].bitcast(F32R),
                        vTr[:, 4 * h:4 * h + 4, SEQ:T].rearrange("p c (n t) -> p c n t", t=NT), ACT.Copy).then_inc(r_padH, 1)

            def copy_turned(h):
                act.wait_ge(r_turned, h + 1)
                nc.scalar.activation(vtok_r[:, :, :], banks[:, 0:2, :], ACT.Copy).then_inc(r_tok, 1)
                nc.scalar.activation(vtok_s[:, :], banks[0:NS, 3, :], ACT.Copy).then_inc(r_tok, 1)
                for tb in range(2):
                    c = C_KDEC + tb * NHR + h
                    nc.scalar.activation(ktok_r[:, tb, :], banks[:, 2, tb * DK:tb * DK + DK], ACT.Copy,
                                         scale=col[:, c:c + 1]).then_inc(r_tok, 1)
                act.wait_ge(r_pturned, h + 1)
                nc.scalar.activation(vst[:, h % 2, :, :], banks[:, 0:2, :], ACT.Copy).then_inc(r_stack, 1)
                nc.scalar.activation(kst[:, h % 2, :, :], banks[:, 2, :].rearrange("p (a c) -> p a c", a=2),
                                     ACT.Copy).then_inc(r_stack, 1)
                if h:
                    act.wait_ge(ps_stored, 16 * 2 * h)
                for z in range(2):
                    act.wait_ge(r_state, 2 * h + z + 1)
                    nc.scalar.activation(ps_sb[z], banks[:, z, :], ACT.Copy).then_inc(r_scopied, 1)

            def norm_head(h):
                act.wait_ge(r_sread, NB * (h + 1))
                nc.scalar.activation(os_sb[os_rows(h), :], banks[os_rows(h), 5, :], ACT.Copy).then_inc(os_copied, 1)
                act.wait_ge(gn_o, 6 * h + 4)
                nc.scalar.activation(o_sb, oc_sb, ACT.Square).then_inc(gn_sq, 1)
                act.wait_ge(gn_mean, 2 * (h + 1))
                nc.scalar.activation(rms[:, :], banks[:, 4, 0:T], ACT.Sqrt, bias=gn_eps).then_inc(gn_rms, 1)
                act.wait_ge(gn_o, 6 * (h + 1))
                nc.scalar.activation(yH[:, 4 * h:4 * h + 4, :], oc_sb, ACT.Copy).then_inc(yr_round, 1)

            pad_head(0)
            copy_turned(0)
            for h in range(NHR):
                if h:
                    norm_head(h - 1)
                if h + 1 < NHR:
                    pad_head(h + 1)
                    copy_turned(h + 1)
            norm_head(NHR - 1)

            for u in range(N_RETOUT):
                if u == 1:
                    act.wait_ge(ps_stored, 16 * 2 * NHR)
                down(2, S_RETOUT + u, u // 2 if u % 2 else None, u == N_RETOUT - 1)
            root(5)
            pre_norm(3, 1, 2)
            for j in range(4):
                act.wait_ge(s_stored[j], 16 * 2 * NHR)
            mlp(S_FF1B, S_FF2B, GD_FF1B, N_FF, 3)

        @block.vector
        def _(dve):
            def split_strip(s, at):
                dve.wait_ge(h_round, s + 1)
                nc.vector.tensor_tensor(wL[:, at % SPL, :], raw[:, at % RAWS, :], wH[:, at % SPL, :].bitcast(F32),
                                        ALU.subtract).then_inc(l_split, 1)

            def inverse(e, to):
                dve.wait_ge(rms_done, e + 1)
                nc.vector.reciprocal(to[:, :], rms[:, :]).then_inc(rs_done, 1)

            def split_x(b, k, layer, norm):
                dve.wait_ge(hx_round, KT * b + k + 1)
                nc.vector.scalar_tensor_tensor(out=hL[:, k, :], in0=x[:, k, :], scalar=gain(layer, norm, k),
                                               in1=hH[:, k, :].bitcast(F32), op0=ALU.mult,
                                               op1=ALU.subtract).then_inc(hx_split, 1)

            def pre_norm(b, layer, norm, part=None):
                inverse(2 * b, rs_pre)
                dve.wait_ge(rs_done, 2 * b + 1)

            def residual(e, layer, norm, b=None, nlayer=0, nnorm=0):
                inverse(2 * e + 1, rs_post)
                dve.wait_ge(rs_done, 2 * e + 2)
                for k in range(KT + 2):
                    if k < KT:
                        if k >= 2:
                            dve.wait_ge(x_done, KT * e + k - 1)
                        nc.vector.scalar_tensor_tensor(out=tmp[:, k % 2, :], in0=y[:, k, :], scalar=gain(layer, norm, k),
                                                       in1=rs_post[:, :], op0=ALU.mult, op1=ALU.mult).then_inc(t_done, 1)
                    if 1 <= k <= KT:
                        dve.wait_ge(t_done, KT * e + k)
                        nc.vector.tensor_tensor(x[:, k - 1, :], x[:, k - 1, :], tmp[:, (k - 1) % 2, :],
                                                ALU.add).then_inc(x_done, 1)
                    if k >= 2 and b is not None:
                        split_x(b, k - 2, nlayer, nnorm)

            def sum_y(e, j, ga):
                dve.wait_ge(g_act, ga + j + 1)
                if j >= 1:
                    if j >= 2:
                        dve.wait_ge(sq_sum, 4 * e + j - 1)
                    nc.vector.tensor_tensor(acc[:, :, :], acc[:, :, :], sq[:, :, :], ALU.add).then_inc(sq_sum, 1)
                if j == 3:
                    dve.wait_ge(sq_sum, 4 * e + 3)
                    nc.vector.tensor_tensor(acc[:, 0, :], acc[:, 0, :], acc[:, 1, :], ALU.add).then_inc(sq_sum, 1)

            def rotate(s, gj, u, rj, out, at=None):
                if s is not None:
                    dve.wait_ge(strip_used, s + 1)
                dve.wait_ge(rope_out, 1 + 2 * rj)
                nc.vector.tensor_tensor(sq[:, :, :], G(u), both(trigR[:, 0, :]), ALU.mult).then_inc(rope_mul, 1)
                nc.vector.tensor_tensor(acc[:, :, :], G(u), both(trigR[:, 1, :]), ALU.mult).then_inc(g_dve, 1)
                if s is not None:
                    split_strip(s + SPL, at + SPL)
                dve.wait_ge(rope_mul, rj + 1)
                dve.wait_ge(g_dve, GBUF + gj + 1)
                nc.vector.tensor_tensor(out(0), sq[:, 0:1, :], acc[:, 1:2, :], ALU.subtract).then_inc(rope_out, 1)
                nc.vector.tensor_tensor(out(1), sq[:, 1:2, :], acc[:, 0:1, :], ALU.add).then_inc(rope_out, 1)

            def down(e, s, j, last, ga):
                if j is not None and last:
                    sum_y(e, j, ga)
                if s + SPL < N_STRIPS:
                    split_strip(s + SPL, s + SPL)
                if j is not None and not last:
                    sum_y(e, j, ga)

            def mlp(first1, first2, gd, ga, base, e):
                def up(s, u, i):
                    dve.wait_ge(strip_used, s + 1)
                    dve.wait_ge(relu_sq, RAWS * i + (1 + base + u))
                    nc.vector.scalar_tensor_tensor(out=relu_sb[:, u % 2, :, :], in0=G(u), scalar=0.0,
                                                   in1=both(rs_pre[:, :]), op0=ALU.max, op1=ALU.mult).then_inc(g_dve, 1)
                    split_strip(s + SPL, first1 + u + SPL)
                    dve.wait_ge(a_round, RAWS * i + (base + u + 1))
                    nc.vector.tensor_tensor(aL[:, ds(8 * i + 2 * u, 2), :], a_sb[:, :, :],
                                            aH[:, ds(8 * i + 2 * u, 2), :].bitcast(F32), ALU.subtract).then_inc(a_split, 1)

                loop(dve, first1, N_FF, up)
                for u in range(N_FF):
                    down(e, first2 + u, u // 4 if u % 4 == 3 else None, u == N_FF - 1, ga)

            nc.vector.memset(rs_post[:, :], 0.0).then_inc(g_dve, GBUF)
            nc.vector.memset(rs_pre[:, :], 0.0).then_inc(rope_out, 1)
            nc.vector.memset(tmp[:, :, :], 0.0).then_inc(a_split, 1)
            for first, count in ((g_dve, GBUF), (rope_out, 1), (a_split, 1)):
                dve.wait_ge(first, count)
            dve.wait_ge(cols_in, 16)
            for k in range(KT):
                split_x(0, k, 0, 0)
            for s in range(SPL):
                split_strip(s, s)
            pre_norm(0, 0, 0)
            dve.wait_ge(trig_in, 16)
            nc.vector.tensor_tensor(trigR[:, :, :], trig_sb[:, :, :], both(rs_pre[:, :]), ALU.mult).then_inc(trigR_done, 1)
            dve.wait_ge(trigR_done, 1)

            def q_strip(s, u, i):
                rotate(s, RAWS * i + u, u, RAWS * i + u, lambda z: qT[:, ds(8 * i + (2 * u + z), 1), :], S_Q + u)

            loop(dve, S_Q, N_Q, q_strip)

            def kv_strip(s, u, i):
                if u < 2:
                    rotate(s, RAWS * i + (N_Q + u), u, 2 * i + (N_Q + u), lambda z: kT[:, ds(4 * i + (2 * u + z), 1), :],
                           S_KV + u)
                else:
                    dve.wait_ge(strip_used, s + 1)
                    nc.vector.tensor_tensor(vT[:, ds(4 * i + 2 * (u - 2), 2), :], G(u), both(rs_pre[:, :]),
                                            ALU.mult).then_inc(g_dve, 1)
                    split_strip(s + SPL, S_KV + u + SPL)

            loop(dve, S_KV, N_KV, kv_strip)
            dve.wait_ge(strip_used, S_BKV + 1)
            nc.vector.tensor_copy(kz[:, :], G(20)[:, 0, :]).then_inc(kz_done, 1)
            nc.vector.tensor_tensor(vT[:, 4 * NG, :], G(20)[:, 1, :], rs_pre[:, :], ALU.mult).then_inc(g_dve, 1)
            split_strip(S_BKV + SPL, S_BKV + SPL)
            for s in range(2):
                dve.wait_ge(sel_done, s + 1)
                rotate(None, 21 + s, 21 + s, 14 + s, lambda z: kT[:, 12 + 2 * s + z:13 + 2 * s + z, :])

            def mask_unit(u):
                n = 3 if u < NH else 1
                br = slice(0, 3) if u < NH else slice(3, 4)
                dve.wait_ge(scored, u + 1)
                if u >= 2:
                    dve.wait_ge(p_turned, u - 1)
                if u == 0:
                    dve.wait_ge(mask_in, 48)
                    dve.wait_ge(v_stored, 16)
                    dve.wait_ge(v_tok, 14)
                sm = small[:, u % 2, :]
                nc.vector.tensor_tensor_reduce(
                    out=p_sb[:, u % 2, 0:n * 256], in0=S45[:, 0:n * 256], in1=pm[:, br, :].rearrange("p a c -> p (a c)"),
                    scale=1.0, scalar=-3e38, op0=ALU.add, op1=ALU.max, accum_out=sm[:, 0:1]).then_inc(masked, 1)
                nc.vector.tensor_tensor_reduce(
                    out=p_sb[:, u % 2, n * 256:n * 384].rearrange("p (a c) -> p a c", a=n),
                    in0=banks[:, 6, 0:n * P].rearrange("p (a c) -> p a c", a=n), in1=pm[:, br, P:2 * P],
                    scale=1.0, scalar=-3e38, op0=ALU.add, op1=ALU.max, accum_out=sm[:, 1:2]).then_inc(masked, 1)
                dve.wait_ge(masked, 2 * (u + 1))
                nc.vector.tensor_scalar(sm[:, 8:10], sm[:, 0:2], SCALE, col[:, C_SINKP + u:C_SINKP + u + 1],
                                        ALU.mult, ALU.max).then_inc(max_scaled, 1)
                dve.wait_ge(max_scaled, u + 1)
                nc.vector.tensor_scalar(sm[:, 2:4], sm[:, 8:10], -1.0, None, ALU.mult).then_inc(negmax, 1)

            def norm_unit(u):
                n = 3 if u < NH else 1
                sm = small[:, u % 2, :]
                dve.wait_ge(exp_done, 3 * (u + 1))
                nc.vector.tensor_tensor(sm[:, 8:10], sm[:, 4:6], sm[:, 6:8], ALU.add).then_inc(l_done, 1)
                dve.wait_ge(l_done, 2 * u + 1)
                nc.vector.reciprocal(sm[:, 4:6], sm[:, 8:10]).then_inc(l_done, 1)
                dve.wait_ge(l_done, 2 * u + 2)
                for b, c in ((0, slice(0, n * 256)), (1, slice(n * 256, n * 384))):
                    nc.vector.tensor_scalar(p_sb[:, u % 2, c], p_sb[:, u % 2, c], sm[:, 4 + b:5 + b], None,
                                            ALU.mult).then_inc(p_norm, 1)

            def split_o(p):
                dve.wait_ge(o_round, p + 1)
                nc.vector.tensor_tensor(hL[:, p, 0:SEQ], banks[:, 3, 0:SEQ], hH[:, p, 0:SEQ].bitcast(F32),
                                        ALU.subtract).then_inc(o_split, 1)

            def mask_q(u):
                j, n = u % NH, 3 if u < NH else 1
                if u == 0:
                    dve.wait_ge(l_split, HELD)
                    dve.wait_ge(rope_out, 1 + 2 * 4 * NBR)
                t0 = 2 * (j // 4) + (0 if u < NH else 4 * NG)
                src = qT[:, t0:t0 + 4 * (n - 1) + 2, 0:SEQ] if n == 1 else qT[:, 0:4 * NG, 0:SEQ].rearrange(
                    "p (b s z) t -> p b s z t", b=NG, s=2)[:, :, j // 4, :, :]
                out = qm[u % 2][:, 0, :, :] if n == 1 else qm[u % 2]
                nc.vector.tensor_scalar(out, src, col[:, C_HEAD + j % 4:C_HEAD + j % 4 + 1], None,
                                        ALU.mult).then_inc(q_masked, 1)

            mask_q(0)
            mask_q(1)
            mask_unit(0)
            mask_q(2)
            for u in range(NU):
                norm_unit(u)
                if u + 1 < NU:
                    mask_unit(u + 1)
                if u + 3 < NU:
                    mask_q(u + 3)
                if u >= 2 and u % 2 == 0:
                    split_o(u // 2 - 1)
            split_o(NH - 1)

            dve.wait_ge(d_newrow, 1)
            for g in range(NG_D):
                dve.wait_ge(c_used, 4 * CL * (g + 1))
                old = banks[:, 4 + 2 * g:6 + 2 * g, :].rearrange("p a c -> p (a c)")
                new, newm = banks[:, 0, 256 + g * P:256 + g * P + P], dm_new[:, g * P:g * P + P]
                for a, (c, src, mask) in enumerate((
                        (slice(0, CD), old[:, 0:CD], dm[:, 0:CD]), (slice(CD + 96, SROW - NS), old[:, CD:CW], dm[:, CD:CW]),
                        (slice(CD, CD + 96), new[:, 0:96], newm[:, 0:96]),
                        (slice(SROW - NS, SROW), new[:, 96:P], newm[:, 96:P]))):
                    nc.vector.tensor_tensor_reduce(out=sp_sb[:, g, c], in0=src, in1=mask, scale=1.0, scalar=-3e38,
                                                   op0=ALU.add, op1=ALU.max, accum_out=dsm[:, g, a:a + 1]).then_inc(d_masked, 1)
                sm = dsm[:, g, :]
                dve.wait_ge(d_masked, 4 * (g + 1))
                nc.vector.tensor_tensor(sm[:, 4:6], sm[:, 0:2], sm[:, 2:4], ALU.max).then_inc(d_max, 1)
                dve.wait_ge(d_max, g + 1)
                nc.vector.scalar_tensor_tensor(out=sm[:, 14:16], in0=sm[:, 4:6], scalar=SCALE,
                                               in1=col[:, C_SINKD:C_SINKD + 2], op0=ALU.mult, op1=ALU.max).then_inc(d_max2, 1)
                dve.wait_ge(d_max2, g + 1)
                nc.vector.tensor_scalar(sm[:, 6:8], sm[:, 14:16], -1.0, None, ALU.mult).then_inc(d_negmax, 1)
                nc.vector.tensor_tensor(sm[:, 8:10], col[:, C_SINKD:C_SINKD + 2], sm[:, 14:16],
                                        ALU.subtract).then_inc(d_negmax, 1)
                dve.wait_ge(d_exp, 3 * (g + 1))
                nc.vector.tensor_tensor(sm[:, 16:18], sm[:, 10:12], sm[:, 12:14], ALU.add).then_inc(d_l, 1)
                dve.wait_ge(d_l, 2 * g + 1)
                nc.vector.reciprocal(sm[:, 18:20], sm[:, 16:18]).then_inc(d_l, 1)
                dve.wait_ge(d_l, 2 * g + 2)
                for m, c in ((0, slice(0, CD + 96)), (1, slice(CD + 96, SROW))):
                    nc.vector.tensor_scalar(sp_sb[:, g, c], sp_sb[:, g, c], sm[:, 18 + m:19 + m], None,
                                            ALU.mult).then_inc(d_norm, 1)

            def pick_dve(g):
                dve.wait_ge(o_round, NH + 8 * (g + 1))
                for hp in range(4):
                    for e in range(2):
                        dst, src = own_head(g, hp, e)
                        nc.vector.tensor_tensor(dst(hL), src, dst(hH).bitcast(F32), ALU.subtract).then_inc(o_split, 1)

            for g in range(NG_D):
                dve.wait_ge(c_used, CL * NB + 4 * CL * (g + 1))
                nc.vector.tensor_copy(sp_sb[:, g, 512:1024], banks[:, 5 + 2 * g, :]).then_inc(d_ocopB, 1)
                if g:
                    pick_dve(g - 1)
            pick_dve(NG_D - 1)
            for j in range(N_MIXOUT):
                down(0, S_MIXOUT + j, j, j == N_MIXOUT - 1, 0)
            residual(0, 0, 1, 1, 0, 2)
            pre_norm(1, 0, 2)
            dve.wait_ge(k_stored, 16)
            dve.wait_ge(k_stored, 16)
            mlp(S_FF1A, S_FF2A, GD_FF1A, 4, 0, 1)
            residual(1, 0, 3, 2, 1, 0)
            pre_norm(2, 1, 0)
            dve.wait_ge(trig_in, 32)
            nc.vector.tensor_tensor(trigR[:, :, :], trig_sb[:, :, :], both(rs_pre[:, :]), ALU.mult).then_inc(trigR_done, 1)
            dve.wait_ge(trigR_done, 2)

            for t, dst in ((0, qr), (1, kr)):
                for u in range(NHR):
                    s = S_RETIN + 4 * t + u
                    rotate(s, GD_RET + 4 * t + u, u, 16 + 4 * t + u, lambda z: dst[:, 2 * u + z:2 * u + z + 1, :], s)

            def v_strip(s, u, i):
                dve.wait_ge(strip_used, s + 1)
                nc.vector.tensor_tensor(vTr[:, ds(8 * i + 2 * u, 2), :], G(u), both(rs_pre[:, :]),
                                        ALU.mult).then_inc(g_dve, 1)
                split_strip(s + SPL, S_RETIN + 8 + u + SPL)

            loop(dve, S_RETIN + 8, 8, v_strip)

            def gate_strip(s, u, i):
                dve.wait_ge(strip_used, s + 1)
                nc.vector.tensor_tensor(gate[:, ds(8 * i + 2 * u, 2), :], G(u), both(rs_pre[:, :]),
                                        ALU.mult).then_inc(g_dve, 1)
                split_strip(s + SPL, S_RETIN + 16 + u + SPL)
            loop(dve, S_RETIN + 16, 8, gate_strip)
            dve.wait_ge(rmask_in, 32)
            dve.wait_ge(g_dve, GBUF + GD_RET + N_RETIN)
            dve.wait_ge(rope_out, 1 + 2 * (16 + 8))
            for h in range(NHR):
                nc.vector.tensor_tensor(kd[:, 2 * h:2 * h + 2, :], kr[:, 2 * h:2 * h + 2, SEQ:T],
                                        dec[:, 1, h, :].unsqueeze(1).broadcast_to([P, 2, NS]), ALU.mult).then_inc(r_dec, 1)
            nc.vector.memset(qpad[:, :, :], 0.0).then_inc(r_dec, 1)

            def query(h):
                if h:
                    dve.wait_ge(r_sread, NB * h)
                dve.wait_ge(r_dec, NHR + 1)
                nc.vector.tensor_tensor(own_q, qr[:, 2 * h:2 * h + 2, SEQ:T].rearrange("p z (n t) -> p z n t", t=NT),
                                        dec[:, 0, h, :].rearrange("p (n t) -> p n t", t=NT).unsqueeze(1).broadcast_to(
                                            [P, 2, NB, NT]), ALU.mult).then_inc(r_dec, 1)

            def pad_low(h):
                dve.wait_ge(r_padH, 4 * (h + 1))
                if h == 0:
                    dve.wait_ge(r_dec, NHR)
                for p in range(2):
                    nc.vector.tensor_tensor(kpad[:, :, :, 8 + 4 * p:12 + 4 * p],
                                            kd[:, 2 * h:2 * h + 2, :].rearrange("p z (n t) -> p z n t", t=NT),
                                            kpad[:, :, :, 4 * p:4 * p + 4], ALU.subtract).then_inc(r_padL, 1)
                for p in range(2):
                    nc.vector.tensor_tensor(vpad[:, :, :, 4 + 8 * p:8 + 8 * p],
                                            vTr[:, 4 * h:4 * h + 4, SEQ:T].rearrange("p c (n t) -> p c n t", t=NT),
                                            vpad[:, :, :, 8 * p:8 * p + 4], ALU.subtract).then_inc(r_padL, 1)

            def decay(h):
                dve.wait_ge(r_scored, h + 1)
                nc.vector.tensor_tensor(at_sb[:, 0:256], banks[:, 3, 0:256], rm[:, h, 0:256], ALU.mult).then_inc(r_decayed, 1)
                nc.vector.tensor_tensor(at_sb[:, 256:384], banks[:, 3, 256:384], rm[:, h, 0:128],
                                        ALU.mult).then_inc(r_decayed, 1)
                nc.vector.tensor_tensor(at_sb[0:NS, 384:416], banks[0:NS, 3, 384:416], rm[0:NS, h, 256:288],
                                        ALU.mult).then_inc(r_decayed, 1)

            def copy_o(h):
                dve.wait_ge(r_out, h + 1)
                nc.vector.tensor_copy(o_sb, banks[:, 0:4, 0:T]).then_inc(gn_o, 1)

            def update(h, n):
                for z in range(2):
                    dve.wait_ge(r_outer, 2 * (NB * h + n) + z + 1)
                    c = sslot[:, n % 4, z * DV:z * DV + DV]
                    nc.vector.scalar_tensor_tensor(out=c, in0=c, scalar=GAMMA[h] ** NT, in1=banks[:, 6 + z, :],
                                                   op0=ALU.mult, op1=ALU.add).then_inc(r_updated, 1)

            def add_read(h):
                dve.wait_ge(os_turned, h + 1)
                dve.wait_ge(gn_o, 6 * h + 1)
                nc.vector.tensor_tensor(o_sb[:, :, SEQ:T], o_sb[:, :, SEQ:T],
                                        banks[:, 4, T:T + 4 * NS].rearrange("p (c t) -> p c t", c=4),
                                        ALU.add).then_inc(gn_o, 1)
                dve.wait_ge(gn_o, 6 * h + 2)
                nc.vector.tensor_reduce(sumsq[:, :], o_sb.rearrange("p c t -> p t c"), AX.X, ALU.add).then_inc(gn_o, 1)

            def centre(h):
                dve.wait_ge(gn_mean, 2 * h + 1)
                nc.vector.tensor_tensor(oc_sb, o_sb, banks[:, 4, 0:T].unsqueeze(1).broadcast_to([P, 4, T]),
                                        ALU.subtract).then_inc(gn_o, 1)

            def square_sum(h):
                dve.wait_ge(gn_sq, h + 1)
                nc.vector.tensor_reduce(sumsq[:, :], o_sb.rearrange("p c t -> p t c"), AX.X, ALU.add).then_inc(gn_o, 1)

            def scale_gate(h):
                dve.wait_ge(gn_rms, h + 1)
                nc.vector.reciprocal(rs_post[:, :], rms[:, :]).then_inc(gn_rs, 1)
                dve.wait_ge(gn_rs, 2 * h + 1)
                nc.vector.tensor_tensor(oc_sb, oc_sb, rs_post[:, :].unsqueeze(1).broadcast_to([P, 4, T]),
                                        ALU.mult).then_inc(gn_rs, 1)
                dve.wait_ge(gn_rs, 2 * h + 2)
                nc.vector.tensor_tensor(oc_sb, oc_sb, gate[:, 4 * h:4 * h + 4, :], ALU.mult).then_inc(gn_o, 1)

            def split_y(h):
                dve.wait_ge(yr_round, h + 1)
                nc.vector.tensor_tensor(yL[:, 4 * h:4 * h + 4, :], oc_sb, yH[:, 4 * h:4 * h + 4, :].bitcast(F32),
                                        ALU.subtract).then_inc(yr_split, 1)

            norm_steps = (add_read, centre, square_sum, scale_gate, split_y)
            pad_low(0)
            decay(0)
            query(0)
            for h in range(NHR):
                for n in range(NB):
                    update(h, n)
                    if h and n < 4:
                        norm_steps[n](h - 1)
                    if n == 4:
                        if h:
                            split_y(h - 1)
                        copy_o(h)
                        if h + 1 < NHR:
                            pad_low(h + 1)
                    if n == 6 and h + 1 < NHR:
                        decay(h + 1)
                if h + 1 < NHR:
                    query(h + 1)
            for step in norm_steps:
                step(NHR - 1)

            for u in range(N_RETOUT):
                down(2, S_RETOUT + u, u // 2 if u % 2 else None, u == N_RETOUT - 1, 8)
            residual(2, 1, 1, 3, 1, 2)
            pre_norm(3, 1, 2)
            for j in range(4):
                dve.wait_ge(s_stored[j], 16 * 2 * NHR)
            mlp(S_FF1B, S_FF2B, GD_FF1B, 12, N_FF, 3)
            residual(3, 1, 3)


def _strips(w, order):
    blocks = [w[r * D:(r + 1) * D, c * SC:(c + 1) * SC].reshape(KT, P, SC).transpose(1, 0, 2).reshape(P, KT * SC)
              for r, c in order]
    return blocks


def _halves(w):
    return w.reshape(w.shape[0], -1, 4, 2, HALF).transpose(0, 1, 3, 2, 4).reshape(w.shape[0], -1)


def _weights(w_in_mix, w_out_mix, w_in_ret, w_out_ret, w_ff1, w_ff2):
    n = NH * HD
    a = w_in_mix[0][:, :3 * NG * n].reshape(D, NG, 3, n)
    b = w_in_mix[0][:, 3 * NG * n:]
    col1 = [(0, 0), (0, 1)]
    out = []
    for g in range(NG):
        out += _strips(_halves(a[:, g, 0]), col1)
    out += _strips(_halves(b[:, :n]), col1)
    for g in range(NG):
        out += _strips(_halves(a[:, g, 1]), col1) + _strips(a[:, g, 2], col1)
    out += _strips(b[:, n:], [(0, 0)])
    out += _strips(w_out_mix[0], [(0, c) for c in range(4)])

    def mlp(layer):
        return (_strips(w_ff1[layer], [(0, c) for c in range(16)])
                + _strips(w_ff2[layer], [(r, c) for c in range(4) for r in range(4)]))

    out += mlp(0)
    out += _strips(w_in_ret[0], [(0, c) for c in range(24)])
    out += _strips(w_out_ret[0], [(r, c) for c in range(4) for r in range(2)])
    out += mlp(1)
    return np.stack(out)


def _caches(c0, c1, c2, swa):
    a, b, c, d = c0[0], c1[0], c2[0], swa[0]
    b = b.reshape(NB, P, 4, 2, NH, HD)
    c = c.reshape(NB, 64, 16, 2, NH, HD)[:, :, :4].transpose(0, 2, 1, 3, 4, 5).reshape(NB, 2, P, 2, NH, HD)
    d = np.repeat(d, NH // 2, axis=3)
    tiles = np.concatenate([b.transpose(0, 2, 1, 3, 4, 5), c, a[:, None], d[:, None]], axis=1)
    k, v = tiles[:, :, :, 0], tiles[:, :, :, 1]
    k = k.reshape(NB, NKT * P, 2, 4, 2, HALF).transpose(0, 2, 4, 3, 5, 1).reshape(NB, CL, P, CLOAD)
    v = v.reshape(NB, CL, 2, P, 512).transpose(0, 1, 3, 2, 4).reshape(NB, CL, P, CLOAD)
    return np.ascontiguousarray(k), np.ascontiguousarray(v)


def _positions():
    return np.concatenate([np.arange(SEQ), np.tile(PAST + np.arange(NT), NB)])


def _trig():
    pos = _positions().astype(np.float32)
    out = []
    for half in (HALF, DK // 2):
        inv = np.float32(10000.0) ** (-np.arange(half, dtype=np.float32) * np.float32(2.0 / (2 * half)))
        ang = pos[None, :] * inv[np.arange(P) % half][:, None]
        out.append(np.stack([np.cos(ang), np.sin(ang)], axis=1))
    return np.stack(out).astype(np.float32)


def _masks():
    p = np.arange(P)[:, None]
    j = np.arange(2 * P)[None, :]
    diff = P + p - j
    rows = [(diff >= 0) & (diff <= w) & (diff % dil == 0) for w, dil in zip(WINS, DILS)]
    rows.append((diff >= 0) & (diff <= 127))
    pm = np.where(np.stack(rows, axis=1), 0.0, NEG).astype(np.float32)
    t = p // 4 % 4
    j = np.arange(P)[None, :]
    n2, t2 = np.arange(NS)[None, :] // 4, np.arange(NS)[None, :] % 4
    ok = [np.broadcast_to(t == r, (P, P)) for r in range(4)]
    ok += [t == 2 * r + j // 64 for r in range(2)] + [j >= t, j >= t + 1]
    for g in range(NG_D):
        n = 4 * g + p // 32
        own, upto = (n == n2) & (t == t2), (n == n2) & (t2 <= t)
        ok += [upto, own, own, upto]
    ok = np.concatenate(ok, axis=1)
    dm = np.where(ok, 0.0, NEG).astype(np.float32)
    g = np.array(GAMMA)[None, :, None]
    i = np.arange(SEQ)[None, None, :]
    pp = np.arange(P)[:, None, None]
    big = np.where(i >= pp, g ** np.maximum(i - pp, 0), 0.0) / 16
    ti = np.arange(NS)[None, None, :]
    okk = (pp // 4 == ti // 4) & (pp % 4 <= ti % 4) & (pp < NS)
    sm = np.where(okk, g ** np.maximum(ti % 4 - pp % 4, 0), 0.0) / 16
    rm = np.concatenate([big, sm], axis=2).astype(np.float32)
    t = np.arange(NS) % NT
    gh = np.array(GAMMA)[:, None]
    dec = np.stack([gh ** (t + 1), gh ** (NT - 1 - t) / 16])
    dec = np.broadcast_to(dec[None], (P,) + dec.shape).astype(np.float32)
    return pm, dm, rm, np.ascontiguousarray(dec)


def _columns(gains, sinks):
    col = np.zeros((P, N_COL), np.float32)
    col[:, C_GAIN:C_GAIN + 64] = gains.reshape(8, KT, P).transpose(2, 0, 1).reshape(P, 64)
    col[:, C_SINKP:C_SINKP + 8] = NEG
    col[:, C_SINKP + 8:C_SINKP + 16] = sinks[0][None, :]
    p = np.arange(P)
    col[:, C_SINKD] = NEG
    col[:, C_SINKD + 1] = sinks[0][p // 16 % 2 * 4 + p % 4]
    j = np.arange(SEQ).reshape(2, P)
    for tb in range(2):
        for h in range(NHR):
            col[:, C_KDEC + tb * NHR + h] = GAMMA[h] ** (SEQ - 1 - j[tb]) / 16
    col[:, C_EPS] = EPS
    col[:, C_GNEPS] = GN_EPS
    col[p, C_HEAD + p // 32] = 1.0
    return col


def _matrices():
    m = np.zeros((P, 7, P), np.float32)
    m[:, 0] = np.eye(P)
    m[:, 1] = 1.0 / D
    m[:, 2] = 1.0 / DV
    for s in range(2):
        for z in range(2):
            for c in range(P):
                m[(2 * s + z) * HALF + c % HALF, 3 + 2 * s + z, c] = 1.0
    return m


def kernel(x_prompt, x_sample, cache_dil_w128, cache_dil_w512, cache_dil_w2048, cache_swa, state_ret,
           norm_gains, w_in_mix, w_out_mix, attn_sinks, w_in_ret, w_out_ret, w_ff1, w_ff2):
    import concourse.bacc as _bacc
    from concourse.bass_utils import run_bass_kernel_spmd as _run

    arr = [np.asarray(a) for a in (x_prompt, x_sample, cache_dil_w128, cache_dil_w512, cache_dil_w2048, cache_swa,
                                   state_ret, norm_gains, w_in_mix, w_out_mix, attn_sinks, w_in_ret, w_out_ret,
                                   w_ff1, w_ff2)]
    xp, xs, c0, c1, c2, swa, st, gains, wim, wom, sinks, wir, wor, wf1, wf2 = arr
    xcat = np.concatenate([xp[0], xs.reshape(NS, D)], axis=0)
    kc, vc = _caches(c0, c1, c2, swa)
    pm, dm, rm, dec = _masks()
    ins = {
        "wst": _weights(wim, wom, wir, wor, wf1, wf2),
        "x_in": np.ascontiguousarray(xcat.T.reshape(KT, P, T).transpose(1, 0, 2)),
        "cols": _columns(gains, sinks), "trig": _trig(), "mats": _matrices(),
        "pmask": pm, "dmask": dm, "rmask": rm, "qkdec": dec, "kcache": kc, "vcache": vc,
        "state": np.ascontiguousarray(st[0]),
    }
    outs = {
        "x_out": (P, KT, T), "k_out": (P, 4 * NBR, T), "v_out": (P, 4 * NG + 1, T),
        "pstate_out": (NHR, DK, DV), "sstate_out": (NB, NHR, DK, DV),
    }
    nc = _bacc.Bacc("TRN2", target_bir_lowering=False, num_devices=1)
    args = [nc.dram_tensor(n, a.shape, mybir.dt.from_np(a.dtype), kind="ExternalInput").ap() for n, a in ins.items()]
    args += [nc.dram_tensor(n, s, F32, kind="ExternalOutput").ap() for n, s in outs.items()]
    build_program(nc, *args)
    r = _run(nc, [ins], core_ids=[0]).results[0]

    xt = np.asarray(r["x_out"]).transpose(2, 1, 0).reshape(T, D)
    k = np.asarray(r["k_out"]).reshape(4, HALF, NBR, 2, 2, T).transpose(5, 2, 3, 0, 4, 1).reshape(T, NBR, NH, HD)
    v = np.asarray(r["v_out"]).transpose(2, 1, 0).reshape(T, (4 * NG + 1) * P)
    va = v[:, :4 * NG * P].reshape(T, NG, NH, HD)
    vb = v[:, 4 * NG * P:].reshape(T, 2, HD)
    rows = []
    for g in range(NG):
        kv = np.stack([k[:, g], va[:, g]], axis=1)
        rows += [kv[SEQ - min(WINS[g], SEQ):SEQ][None, None], kv[SEQ:].reshape(1, NB, NT, 2, NH, HD)]
    kv = np.stack([k[:, NG, ::4], vb], axis=1)
    rows += [kv[SEQ - P:SEQ][None, None], kv[SEQ:].reshape(1, NB, NT, 2, 2, HD)]
    return (xt[:SEQ][None], xt[SEQ:].reshape(NB, NT, D), *[np.ascontiguousarray(a) for a in rows],
            np.asarray(r["pstate_out"])[None, None], np.asarray(r["sstate_out"])[None])
```

```python
from contextlib import ExitStack

import numpy as np

import concourse.bass as bass
from concourse import mybir

F32 = mybir.dt.float32
F32R = mybir.dt.float32r
ALU = mybir.AluOpType
ACT = mybir.ActivationFunctionType
ds = bass.ds

P = 128
D = 1024
KT = D // P
SEQ = 256
NB, NT = 8, 4
NS = NB * NT
T = SEQ + NS
PAST = 1024
HD = 64
HALF = HD // 2
NH = 8
NG = 3
DILS = (1, 4, 16)
WINS = (128, 512, 2048)
NBR = NG + 1
NHR, DK, DV = 4, 256, 512
DFF = 4 * D
SC = 256
RAWS = 4
SPL = 2
HALF_STRIP = KT * SC // 2
GBUF = 2
EPS = 1e-6
GN_EPS = 1e-5
NEG = -1e30
SCALE = HD ** -0.5
NKT = 8
CD = (NKT - 1) * P
CW = NKT * P
CB = ((1, 0, 512), (2, 512, 256), (0, 768, P), (3, CD, P))
CLOAD = 1024
CL = 4
NG_D = NB // 4
SROW = CW + P
CSLOTS = 8

N_Q, N_KV, N_BKV, N_MIXOUT, N_FF, N_RETIN, N_RETOUT = 8, 12, 1, 4, 16, 24, 8
S_Q = 0
S_KV = S_Q + N_Q
S_BKV = S_KV + N_KV
S_MIXOUT = S_BKV + N_BKV
S_FF1A = S_MIXOUT + N_MIXOUT
S_FF2A = S_FF1A + N_FF
S_RETIN = S_FF2A + N_FF
S_RETOUT = S_RETIN + N_RETIN
S_FF1B = S_RETOUT + N_RETOUT
S_FF2B = S_FF1B + N_FF
N_STRIPS = S_FF2B + N_FF

C_GAIN = 0
C_SINKP = C_GAIN + 64
C_SINKD = C_SINKP + 16
C_KDEC = C_SINKD + 4
C_EPS = C_KDEC + 8
C_GNEPS = C_EPS + 1
C_HEAD = C_GNEPS + 1
N_COL = C_HEAD + 4
GAMMA = [1.0 - 2.0 ** (-5.0 - h) for h in range(NHR)]




def build_program(nc, wst, x_in, cols, trig, mats, pmask, dmask, rmask, qkdec, kcache, vcache, state,
                  x_out, k_out, v_out, pstate_out, sstate_out):
    with ExitStack() as ctx:
        def sem(name):
            return ctx.enter_context(nc.semaphore(name))

        def sb(name, shape, dt=F32, scope=ctx):
            return scope.enter_context(nc.sbuf_tensor(name, shape, dt))

        raw = sb("raw", [P, RAWS, KT * SC])
        wH = sb("wH", [P, SPL, KT * SC], F32R)
        wL = sb("wL", [P, SPL, KT * SC], F32R)
        x = sb("x", [P, KT, T])
        hH = sb("hH", [P, KT, T], F32R)
        hL = sb("hL", [P, KT, T], F32R)
        y = sb("y", [P, KT, T])
        sq = sb("sq", [P, 2, T])
        acc = sb("acc", [P, 2, T])
        sumsq = sb("sumsq", [P, T])
        rms = sb("rms", [P, T])
        rs_post = sb("rs_post", [P, T])
        rs_pre = sb("rs_pre", [P, T])
        tmp = sb("tmp", [P, 2, T])
        trig_sb = sb("trig_sb", [P, 2, T])
        trigR = sb("trigR", [P, 2, T])
        col = sb("col", [P, N_COL])
        scratch = sb("scratch", [P, 1])
        mat = sb("mat", [P, 7, P])

        NVT = 4 * NG + 1
        with ExitStack() as mix:
            qT = sb("qT", [P, 4 * NBR, T], F32, mix)
            kT = sb("kT", [P, 4 * NBR, T], F32, mix)
            vtok = sb("vtok", [P, 2, NVT * P], F32, mix)
            vnew = tmp[:, :, :].rearrange("p a t -> p (a t)")[:, 0:NH * HD]
            pm = sb("pm", [P, NBR, 2 * P], F32, mix)
            dm = sb("dm", [P, CW], F32, mix)
            dm_new = trig_sb[:, 0, 0:NG_D * P]
            cache_sb = sb("cache_sb", [P, CSLOTS // 2, CLOAD], F32, mix)
            with ExitStack() as s1:
                vT = sb("vT", [P, NVT, T], F32, s1)
            with ExitStack() as s2:
                p_sb = sb("p_sb", [P, 2, 9 * P], F32, s2)
                pt_sb = sb("pt_sb", [P, 3, 3 * P], F32, s2)
                small = sb("small", [P, 2, 10], F32, s2)
            with ExitStack() as s3:
                st_sb = sb("st_sb", [P, NG_D, SROW], F32, s3)
                nt_sb = sb("nt_sb", [P, NG_D * P], F32, s3)
                dsm = sb("dsm", [P, NG_D, 20], F32, s3)
            sp_sb = y[:, :, :].rearrange("p k t -> p (k t)").rearrange("p (g c) -> p g c", g=NG_D)
            kz = y[:, 0, :]
            HELD = S_MIXOUT + 2
            qm = [raw[:, (HELD + 2 + i) % RAWS, 0:NG * 2 * SEQ].rearrange("p (b z t) -> p b z t", b=NG, z=2) for i in range(2)]
            cslot = [cache_sb[:, i, :] for i in range(4)] + [
                raw[:, (HELD + 2 + i // 2) % RAWS, i % 2 * CLOAD:i % 2 * CLOAD + CLOAD] for i in range(4)]
            qz = [raw[:, s % RAWS, :].rearrange("p (a c) -> p a c", a=8) for s in (HELD, HELD + 1)]
        with ExitStack() as ffs:
            aH = sb("aH", [P, 4 * KT, T], F32R, ffs)
            aL = sb("aL", [P, 4 * KT, T], F32R, ffs)
            relu_sb = sb("relu_sb", [P, 2, 2, T], F32, ffs)
            a_sb = sb("a_sb", [P, 2, T], F32, ffs)
        with ExitStack() as ret:
            with ExitStack() as r1:
                vTr = sb("vTr", [P, 4 * NHR, T], F32, r1)
                gate = sb("gate", [P, 4 * NHR, T], F32, r1)
            with ExitStack() as r2:
                yH = sb("yH", [P, 4 * NHR, T], F32R, r2)
                yL = sb("yL", [P, 4 * NHR, T], F32R, r2)
                qr = sb("qr", [P, 2 * NHR, T], F32, r2)
                kr = sb("kr", [P, 2 * NHR, T], F32, r2)
                sslot = sb("sslot", [P, 4, 2 * DV], F32, r2)
                vtok_r = sb("vtok_r", [P, 2, DV], F32, r2)
                ktok_r = sb("ktok_r", [P, 2, DK], F32, r2)
                vpad = sb("vpad", [P, 4, 8, NS], F32, r2)
                kpad = sb("kpad", [P, 2, 8, NS], F32, r2)
                rm = sb("rm", [P, NHR, T], F32, r2)
                dec = sb("dec", [P, 2, NHR, NS], F32, r2)
            vtok_s = sq[0:NS, :, :].rearrange("p a t -> p (a t)")[:, 0:DV]
            os_sb = sq[:, :, :].rearrange("p a t -> p (a t)")[:, 0:DV]
            at_sb = trig_sb[:, :, :].rearrange("p a t -> p (a t)")[:, 0:13 * NS]
            kd = sumsq[:, 0:8 * NS].rearrange("p (h c) -> p h c", h=8)
            qpad = trigR
            own_q = trigR[:, :, :].rearrange("p z (n c) -> p z n c", c=NS + NT)[:, :, :, 0:NT]
            kst = hH[:, :, :].rearrange("p k t -> p (k t)")[:, 0:4 * DK].rearrange("p (h a c) -> p h a c", h=2, c=DK)
            vst = hL[:, :, :].rearrange("p k t -> p (k t)")[:, 0:4 * DV].rearrange("p (h a c) -> p h a c", h=2, c=DV)
            o_sb = y[:, 0:4, :]
            oc_sb = y[:, 4:8, :]
            ps_sb = [a[:, :, :].rearrange("p a t -> p (a t)")[:, 0:DV] for a in (tmp, acc)]

        banks = ctx.enter_context(nc.psum_tensor("banks", [P, 8, 512], F32))

        def G(j):
            return banks[:, 2 * (j % 2):2 * (j % 2) + 2, 0:T]

        def both(a):
            return a.unsqueeze(1).broadcast_to([P, 2, T])

        ident, mean_d, mean_v = mat[:, 0, :], mat[:, 1, :], mat[:, 2, :]
        MS = banks[:, 7, 0:T]
        S45 = banks[:, 4:6, :].rearrange("p a c -> p (a c)")
        eps, gn_eps = col[:, C_EPS:C_EPS + 1], col[:, C_GNEPS:C_GNEPS + 1]

        def late(u):
            return S45 if u < NH else banks[:, 7, 0:256]

        def early(u):
            return banks[:, 6, :] if u < NH else banks[:, 7, 256:384]

        def turned(h):
            return 4 if h == 0 else 0

        def os_rows(h):
            return slice(32 * (1 + h % 2), 32 * (1 + h % 2) + NS)

        def own_head(g, hp, e):
            r = slice(64 * e, 64 * e + 64)
            src = banks[r, 2 * g:2 * g + 2, hp * P:hp * P + P].rearrange("p m (n s t h) -> p m n s t h", n=4, s=2, t=NT)
            return (lambda dst: dst[r, :, SEQ + 16 * g:SEQ + 16 * g + 16].rearrange(
                        "p (m k) (n t) -> p m k n t", m=2, t=NT)[:, :, hp, :, :],
                    src[:, :, :, hp // 2, :, 2 * (hp % 2) + e])

        def gain(layer, norm, k):
            c = C_GAIN + (4 * layer + norm) * KT + k
            return col[:, c:c + 1]

        cols_in, mats_in, x_landed, trig_in, mask_in, rmask_in = map(
            sem, ("cols_in", "mats_in", "x_landed", "trig_in", "mask_in", "rmask_in"))
        w_landed = [sem(f"w_landed{i}") for i in range(RAWS)]
        h_round, l_split, strip_used = map(sem, ("h_round", "l_split", "strip_used"))
        g_dve, y_copied, g_act = map(sem, ("g_dve", "y_copied", "g_act"))
        hx_round, hx_split = map(sem, ("hx_round", "hx_split"))
        sq_sum, ms_done, rms_done, rs_done = map(sem, ("sq_sum", "ms_done", "rms_done", "rs_done"))
        t_done, x_done, xsq_done, xacc = map(sem, ("t_done", "x_done", "xsq_done", "xacc"))
        rope_mul, rope_out, trigR_done, kz_done, sel_done = map(
            sem, ("rope_mul", "rope_out", "trigR_done", "kz_done", "sel_done"))
        v_turned, v_tok, k_stored, v_stored = map(sem, ("v_turned", "v_tok", "k_stored", "v_stored"))
        scored, q_masked, masked, max_scaled, negmax, exp_done, l_done, p_norm, p_turned, pt_copied, pv_done = map(sem, (
            "scored", "q_masked", "masked", "max_scaled", "negmax", "exp_done", "l_done", "p_norm", "p_turned", "pt_copied",
            "pv_done"))
        o_round, o_split, q_zero, q_spread = map(sem, ("o_round", "o_split", "q_zero", "q_spread"))
        c_landed = [sem(f"c_landed{i}") for i in range(CSLOTS)]
        c_used = sem("c_used")
        d_newT, d_newcopied, d_newrow, d_masked, d_max, d_max2, d_negmax, d_exp, d_l, d_norm, d_pturned, d_ptcopied = map(
            sem, ("d_newT", "d_newcopied", "d_newrow", "d_masked", "d_max", "d_max2", "d_negmax", "d_exp", "d_l",
                  "d_norm", "d_pturned", "d_ptcopied"))
        d_ocopA, d_ocopB, d_oturned = map(sem, ("d_ocopA", "d_ocopB", "d_oturned"))
        relu_sq, a_round, a_split = map(sem, ("relu_sq", "a_round", "a_split"))
        fin = sem("fin")
        half_round, half_split = sem("half_round"), sem("half_split")
        gated, sqrt_loaded = sem("gated"), sem("sqrt_loaded")
        s_landed = [sem(f"s_landed{i}") for i in range(4)]
        s_stored = [sem(f"s_stored{i}") for i in range(4)]
        r_dec, r_zero, r_padH, r_padL, r_turned, r_tok, r_pturned, r_stack = map(
            sem, ("r_dec", "r_zero", "r_padH", "r_padL", "r_turned", "r_tok", "r_pturned", "r_stack"))
        os_copied, os_turned, o_copied = map(sem, ("os_copied", "os_turned", "o_copied"))
        r_scored, r_decayed, r_state, r_scopied, r_out, r_sread, r_outer, r_updated = map(
            sem, ("r_scored", "r_decayed", "r_state", "r_scopied", "r_out", "r_sread", "r_outer", "r_updated"))
        gn_o, gn_mean, gn_sq, gn_rms, gn_rs, yr_round, yr_split, ps_stored = map(
            sem, ("gn_o", "gn_mean", "gn_sq", "gn_rms", "gn_rs", "yr_round", "yr_split", "ps_stored"))

        block = ctx.enter_context(nc.Block())

        RET_GROUP = {2: 0, 3: 1, 5: 2, 7: 3}
        NU = 2 * NH
        GD_FF1A, GD_RET, GD_FF1B = 23, 39, 63

        def loop(eng, first, count, body, peel=0):
            assert count % RAWS == 0
            for i in range(peel):
                for u in range(RAWS):
                    body(RAWS * i + first + u, u, i)
            if peel < count // RAWS:
                with eng.Fori(peel, count // RAWS) as i:
                    for u in range(RAWS):
                        body(RAWS * i + (first + u), u, i)

        @block.sync
        def _(sp):
            sp.dma_start(col[:, :], cols).then_inc(cols_in, 16)
            sp.dma_start(x[:, :, :], x_in).then_inc(x_landed, 16)
            sp.dma_start(raw[:, 0, :], wst[0]).then_inc(w_landed[0], 16)
            sp.dma_start(mat[:, :, :], mats).then_inc(mats_in, 16)
            for s in range(1, RAWS):
                sp.dma_start(raw[:, s, :], wst[s]).then_inc(w_landed[s], 16)
            sp.dma_start(trig_sb[:, :, :], trig[0]).then_inc(trig_in, 16)
            sp.dma_start(pm[:, :, :], pmask).then_inc(mask_in, 16)
            sp.dma_start(dm[:, :], dmask[:, 0:CW]).then_inc(mask_in, 16)
            sp.wait_ge(trigR_done, 1)
            sp.dma_start(dm_new[:, :], dmask[:, CW:CW + NG_D * P]).then_inc(mask_in, 16)

            def strip(s, slot):
                sp.wait_ge(l_split, s - RAWS + 1)
                sp.dma_start(raw[:, slot, :], wst[ds(s, 1)].rearrange("a p n -> (a p) n")).then_inc(w_landed[slot], 16)

            def strips(first, end):
                whole = (end - first) // RAWS * RAWS
                if whole:
                    loop(sp, first, whole, lambda s, u, i: strip(s, (first + u) % RAWS))
                for s in range(first + whole, end):
                    strip(s, s % RAWS)

            def cache_load(src, n, j, slot, used):
                if used is not None:
                    sp.wait_ge(c_used, used)
                sp.dma_start(cslot[slot], src[ds(n, 1), j].rearrange("a p n -> (a p) n")).then_inc(c_landed[slot], 16)

            strips(RAWS, HELD)
            for j in range(CL):
                cache_load(kcache, 0, j, j, None)
            with sp.Fori(1, 4) as n:
                for j in range(CL):
                    cache_load(kcache, n, j, j, CL * n + (j + 1 - CL))
            for j in range(CL):
                cache_load(kcache, 4, j, j, CL * 4 + j + 1 - CL)
            sp.wait_ge(scored, NU)
            for j in range(CL):
                cache_load(kcache, 5, j, CL + j, None)
            for src, first, before in ((kcache, 3, 0), (vcache, 0, CL * NB)):
                with sp.Fori(first, NB // 2) as m:
                    for slot in range(CSLOTS):
                        cache_load(src, 2 * m + slot // CL, slot % CL, slot, CSLOTS * m + (before + slot + 1 - CSLOTS))
            strips(HELD, HELD + 2)
            sp.wait_ge(c_used, 2 * CL * NB)
            strips(HELD + 2, RAWS + S_RETIN)
            sp.wait_ge(strip_used, S_RETIN)
            sp.dma_start(trig_sb[:, :, :], trig[1]).then_inc(trig_in, 16)
            sp.dma_start(rm[:, :, :], rmask).then_inc(rmask_in, 16)
            sp.dma_start(dec[:, :, :, :], qkdec).then_inc(rmask_in, 16)

            def state_load(n, h):
                j = n % 4
                k = 2 * h + n // 4
                if k:
                    sp.wait_ge(s_stored[j], 16 * k)
                sp.dma_start(sslot[:, j, :].rearrange("p (z e) -> p z e", z=2),
                             state[n, h].rearrange("(z p) e -> p z e", p=P)).then_inc(s_landed[j], 16)

            for n in range(4):
                state_load(n, 0)
            strips(RAWS + S_RETIN, RAWS + S_RETOUT)
            for h in range(NHR):
                for n in range(4 if h == 0 else 0, NB):
                    state_load(n, h)
            strips(RAWS + S_RETOUT, N_STRIPS)

        @block.gpsimd
        def _(pool):
            def sum_squares(b):
                for k in range(KT):
                    pool.wait_ge(xsq_done, KT * b + k + 1)
                    if k == 0:
                        nc.gpsimd.tensor_copy(sumsq[:, :], sq[:, 0, :]).then_inc(xacc, 1)
                    else:
                        pool.wait_ge(xacc, KT * b + k)
                        nc.gpsimd.tensor_tensor(sumsq[:, :], sumsq[:, :], sq[:, k % 2, :], ALU.add).then_inc(xacc, 1)

            sum_squares(0)
            pool.wait_ge(g_dve, GBUF + 21)
            pool.dma_start(v_out, vT[:, :, :]).then_inc(v_stored, 16)
            pool.wait_ge(rope_out, 1 + 2 * 4 * NBR)
            pool.dma_start(k_out, kT[:, :, :]).then_inc(k_stored, 16)
            pool.wait_ge(l_split, S_BKV + 1)
            for a in range(2):
                nc.gpsimd.memset(qz[a], 0.0).then_inc(q_zero, 1)
            pool.wait_ge(q_zero, 2)
            for br in range(NBR):
                for s in range(2):
                    for h in range(4):
                        r = slice(32 * h, 32 * h + 32)
                        t0 = 2 * (2 * (br % 2) + s)
                        nc.gpsimd.tensor_copy(
                            qz[br // 2][r, t0:t0 + 2, :].rearrange("p z (n s t h) -> p z n s t h", n=NB, s=2, t=NT)[
                                :, :, :, s, :, h],
                            qT[r, 4 * br + 2 * s:4 * br + 2 * s + 2, SEQ:T].rearrange(
                                "p z (n t) -> p z n t", t=NT)).then_inc(q_spread, 1)
            sum_squares(1)
            sum_squares(2)
            pool.wait_ge(strip_used, S_RETIN)
            nc.gpsimd.memset(vpad[:, :, :, :], 0.0).then_inc(r_zero, 1)
            nc.gpsimd.memset(kpad[:, :, :, :], 0.0).then_inc(r_zero, 1)
            for h in range(NHR):
                for z in range(2):
                    pool.wait_ge(r_scopied, 2 * h + z + 1)
                    pool.dma_start(pstate_out[h, z * P:(z + 1) * P, :], ps_sb[z]).then_inc(ps_stored, 16)
                for n in range(NB):
                    pool.wait_ge(r_updated, 2 * (NB * h + n + 1))
                    pool.dma_start(sstate_out[n, h].rearrange("(z p) e -> p z e", p=P),
                                   sslot[:, n % 4, :].rearrange("p (z e) -> p z e", z=2)).then_inc(s_stored[n % 4], 16)
            sum_squares(3)
            for k in range(0, KT, 2):
                pool.wait_ge(x_done, 3 * KT + k + 2)
                pool.dma_start(x_out[:, k:k + 2, :], x[:, k:k + 2, :]).then_inc(fin, 16)
            pool.wait_ge(fin, 16 * KT // 2)
            pool.wait_ge(k_stored, 16)
            pool.wait_ge(v_stored, 16)
            pool.wait_ge(ps_stored, 16 * 2 * NHR)
            for j in range(4):
                pool.wait_ge(s_stored[j], 16 * 2 * NHR)

        @block.tensor
        def _(pe):
            def product(s, u, out, hi, lo, start=True, stop=True):
                pe.wait_ge(l_split, s + 1)
                for m in range(2):
                    for k in range(KT):
                        mm = tile_product(u, out, hi, lo, m, k, start, stop)
                mm.then_inc(strip_used, 1)

            def tile_product(u, out, hi, lo, m, k, start=True, stop=True):
                c = slice(k * SC + m * P, k * SC + m * P + P)
                first, last = start and k == 0, stop and k == KT - 1
                nc.tensor.matmul(out[:, m, :], wH[:, u % 2, c], hi[:, k, :], start=first, stop=False)
                nc.tensor.matmul(out[:, m, :], wH[:, u % 2, c], lo[:, k, :], start=False, stop=False)
                return nc.tensor.matmul(out[:, m, :], wL[:, u % 2, c], hi[:, k, :], start=False, stop=last)

            def mean_square(which, of, ready, count):
                pe.wait_ge(ready, count)
                nc.tensor.matmul(MS, which, of, start=True, stop=True).then_inc(ms_done, 1)

            def first_product(b, s, out):
                if b == 0:
                    pe.wait_ge(half_split, 1)
                else:
                    pe.wait_ge(l_split, s + 1)
                for k in range(KT):
                    if b == 0 and k == KT // 2:
                        pe.wait_ge(l_split, 1)
                    pe.wait_ge(hx_split, KT * b + k + 1)
                    for m in range(2):
                        mm = tile_product(s, out, hH, hL, m, k)
                mm.then_inc(strip_used, 1)
                if b == 0:
                    pe.wait_ge(mats_in, 16)
                mean_square(mean_d, sumsq[:, :], xacc, KT * (b + 1))

            def is_first(i, u):
                return isinstance(i, int) and i == 0 and u == 0

            def in_mix(s, u, i, j):
                pe.wait_ge(g_dve, j + GBUF - 1)
                if is_first(i, s - S_Q if isinstance(s, int) else 1):
                    first_product(0, s, G(u))
                else:
                    product(s, s if isinstance(s, int) else u, G(u), hH, hL)

            loop(pe, S_Q, N_Q, lambda s, u, i: in_mix(s, u, i, RAWS * i + u), peel=1)
            loop(pe, S_KV, N_KV, lambda s, u, i: in_mix(s, u, i, RAWS * i + (N_Q + u)))
            in_mix(S_BKV, 0, None, 20)
            pe.wait_ge(kz_done, 1)
            for s in range(2):
                pe.wait_ge(g_dve, GBUF + 20 + s)
                for z in range(2):
                    mm = nc.tensor.matmul(G(21 + s)[:, z, :], mat[:, 3 + 2 * s + z, :], kz[:, :], start=True, stop=True)
                mm.then_inc(sel_done, 1)
            pe.wait_ge(g_dve, GBUF + 21)
            for i in range(7):
                if i >= 2:
                    pe.wait_ge(v_tok, 2 * (i - 1))
                b0 = 4 + 2 * (i % 2)
                for c in range(2 if i < 6 else 1):
                    for tb in range(3):
                        w = P if tb < 2 else NS
                        p0 = 0 if tb < 2 else NS * (i // 2)
                        out = banks[p0:p0 + w, b0 + tb // 2, (tb % 2) * 256 + c * P:(tb % 2) * 256 + c * P + P]
                        v = vT[:, 2 * i + c, tb * P:tb * P + w]
                        if tb < 2:
                            nc.tensor.transpose(out, v, ident)
                        else:
                            mm = nc.tensor.matmul(out, v, ident, start=True, stop=True)
                mm.then_inc(v_turned, 1)

            def branches(u):
                return list(range(NG)) if u < NH else [NG]

            def scores(u):
                s = u % NH // 4
                pe.wait_ge(q_masked, u + 1)
                if u:
                    pe.wait_ge(masked, 2 * u)
                for a, br in enumerate(branches(u)):
                    for z in range(2):
                        t = (2 * br + s) * 2 + z
                        nc.tensor.matmul(late(u)[:, a * 256:a * 256 + 256], qm[u % 2][:, a, z, P:2 * P], kT[:, t, 0:2 * P],
                                         start=z == 0, stop=z == 1)
                for a, br in enumerate(branches(u)):
                    for z in range(2):
                        t = (2 * br + s) * 2 + z
                        mm = nc.tensor.matmul(early(u)[:, a * P:a * P + P], qm[u % 2][:, a, z, 0:P], kT[:, t, 0:P],
                                              start=z == 0, stop=z == 1)
                mm.then_inc(scored, 1)

            def turn_p(u):
                pe.wait_ge(p_norm, 2 * (u + 1))
                if u:
                    pe.wait_ge(pt_copied, u)
                n = len(branches(u))
                for a in range(n):
                    for c, at in enumerate((n * 256 + a * P, a * 256, a * 256 + P)):
                        mm = nc.tensor.transpose(banks[:, a, c * P:c * P + P], p_sb[:, u % 2, at:at + P], ident)
                mm.then_inc(p_turned, 1)

            def pv(u):
                j = u % NH
                pe.wait_ge(pt_copied, u + 1)
                if u % 2 == 0 and u:
                    pe.wait_ge(o_split, u // 2)
                r = slice(64 * (j % 2), 64 * (j % 2) + 64)
                n = len(branches(u))
                for a, br in enumerate(branches(u)):
                    v0 = 4 * br * P + (j * HD if br < NG else j // 4 * HD)
                    nc.tensor.matmul(banks[r, 3, 0:2 * P], vtok[:, 0, v0:v0 + HD], pt_sb[:, a, 0:2 * P],
                                     start=a == 0, stop=False)
                    mm = nc.tensor.matmul(banks[r, 3, P:2 * P], vtok[:, 1, v0:v0 + HD], pt_sb[:, a, 2 * P:3 * P],
                                          start=False, stop=a == n - 1)
                mm.then_inc(pv_done, 1)

            def load_at(i):
                if i < 4 * CL:
                    return i % CL, i // CL
                slot = (i - 4 * CL) % CSLOTS
                return slot, (i - 4 * CL) // CSLOTS + (4 if slot < CL else 0)

            def cached_scores(i):
                n, j = i // CL, i % CL
                g, q = n // 4, n % 4
                slot, before = load_at(i)
                pe.wait_ge(c_landed[slot], 16 * (before + 1))
                for br, k0, kn in CB:
                    mm = nc.tensor.matmul(
                        banks[32 * q:32 * q + 32, 4 + 2 * g + k0 // 512, k0 % 512:k0 % 512 + kn],
                        qz[br // 2][:, 4 * (br % 2) + j, P * g + 32 * q:P * g + 32 * q + 32], cslot[slot][:, k0:k0 + kn],
                        start=j == 0 and k0 % 512 == 0, stop=j == CL - 1, skip_group_check=True)
                mm.then_inc(c_used, 1)

            pe.wait_ge(v_tok, 2 * 7)
            scores(0)
            for u in range(NU):
                if u + 1 < NU:
                    scores(u + 1)
                if u:
                    pv(u - 1)
                turn_p(u)
                if u >= NH:
                    if u == NH:
                        pe.wait_ge(q_spread, 8 * NBR)
                        pe.wait_ge(masked, 2 * NH)
                    for i in range(2 * (u - NH), 2 * (u - NH) + 2):
                        cached_scores(i)
            pv(NU - 1)

            pe.wait_ge(o_split, NH)
            for br in range(NBR):
                for t in range(4):
                    mm = nc.tensor.matmul(banks[NS * br:NS * br + NS, 0, 0:NG_D * P], kT[:, 4 * br + t, SEQ:T],
                                          qz[br // 2][:, 4 * (br % 2) + t, :], start=t == 0, stop=t == 3)
            mm.then_inc(d_newT, 1)
            pe.wait_ge(d_newcopied, 1)
            for g in range(NG_D):
                mm = nc.tensor.transpose(banks[:, 0, 256 + g * P:256 + g * P + P], nt_sb[:, g * P:g * P + P], ident)
            mm.then_inc(d_newrow, 1)
            for i in range(CL * 4, CL * NB):
                cached_scores(i)
            for g in range(NG_D):
                pe.wait_ge(d_norm, 2 * g + 2)
                for i in range(NKT + 1):
                    at = (i * P if i < NKT - 1 else CD + 96 if i == NKT - 1 else CD)
                    w = P if i < NKT else 96
                    mm = nc.tensor.transpose(banks[0:w, 1 + i // 4, i % 4 * P:i % 4 * P + P],
                                             sp_sb[:, g, at:at + w], ident)
                at = SROW - NS
                mm = nc.tensor.matmul(banks[96:P, 3, 0:P], sp_sb[:, g, at:at + NS], ident, start=True, stop=True)
                mm.then_inc(d_pturned, 1)
                pe.wait_ge(d_ptcopied, g + 1)
                for m, r in ((0, slice(0, 96)), (1, slice(96, P))):
                    nc.tensor.matmul(banks[:, 4 + 2 * g + m, :],
                                     st_sb[r, g, CW:SROW], vnew[r, :],
                                     start=True, stop=False, skip_group_check=True)
                for q in range(4):
                    for j in range(CL):
                        slot, before = load_at(CL * (NB + 4 * g + q) + j)
                        pe.wait_ge(c_landed[slot], 16 * (before + 1))
                        for c in range(2):
                            i = 2 * j + c
                            mm = nc.tensor.matmul(
                                banks[32 * q:32 * q + 32, 4 + 2 * g + i // (NKT - 1), :],
                                st_sb[:, g, i * P + 32 * q:i * P + 32 * q + 32],
                                cslot[slot][:, c * 512:c * 512 + 512], start=False, stop=False, skip_group_check=True)
                        mm.then_inc(c_used, 1)
            for g in range(NG_D):
                pe.wait_ge(d_ocopA, g + 1)
                pe.wait_ge(d_ocopB, g + 1)
                for m in range(2):
                    for hp in range(4):
                        c = m * 512 + hp * P
                        mm = nc.tensor.transpose(banks[:, 2 * g + m, hp * P:hp * P + P], sp_sb[:, g, c:c + P], ident)
                mm.then_inc(d_oturned, 1)

            pe.wait_ge(o_split, NH + 8 * NG_D)
            for j in range(N_MIXOUT):
                if j >= 2:
                    pe.wait_ge(g_act, j - 1)
                product(S_MIXOUT + j, S_MIXOUT + j, G(j), hH, hL)

            def mlp(first1, first2, gd, ga, base, b):
                def up(s, u, i):
                    pe.wait_ge(g_dve, RAWS * i + (GBUF - 1 + gd + u))
                    if is_first(i, u):
                        first_product(b, s, G(u))
                    else:
                        product(s, first1 + u, G(u), hH, hL)

                loop(pe, first1, N_FF, up, peel=1)
                with pe.Fori(0, 2) as i:
                    for u in range(8):
                        kq = u % 4
                        if kq == 0:
                            pe.wait_ge(g_act, 2 * i + (ga + u // 4 - 1))
                        pe.wait_ge(a_split, 1 + base + 4 * (kq + 1))
                        product(8 * i + (first2 + u), first2 + u, G(u // 4), aH[:, 8 * kq:8 * kq + 8, :],
                                aL[:, 8 * kq:8 * kq + 8, :], start=kq == 0, stop=kq == 3)

            mean_square(mean_d, acc[:, 0, :], sq_sum, 4)
            mlp(S_FF1A, S_FF2A, GD_FF1A, 4, 0, 1)
            mean_square(mean_d, acc[:, 0, :], sq_sum, 8)

            def in_ret(s, u, i):
                pe.wait_ge(g_dve, RAWS * i + (GBUF - 1 + GD_RET + u))
                if is_first(i, u):
                    first_product(2, s, G(u))
                else:
                    product(s, S_RETIN + u, G(u), hH, hL)

            loop(pe, S_RETIN, N_RETIN - 8, in_ret, peel=1)

            def turn_head(h):
                for c in range(4):
                    for tb in range(2):
                        nc.tensor.transpose(banks[:, turned(h) + tb, c * P:c * P + P],
                                            vTr[:, 4 * h + c, tb * P:tb * P + P], ident)
                    nc.tensor.transpose(banks[0:NS, turned(h) + 3, c * P:c * P + P], vTr[:, 4 * h + c, SEQ:T], ident)
                for z in range(2):
                    for tb in range(2):
                        c = tb * DK + z * P
                        mm = nc.tensor.transpose(banks[:, turned(h) + 2, c:c + P], kr[:, 2 * h + z, tb * P:tb * P + P], ident)
                mm.then_inc(r_turned, 1)

            def turn_samples(h):
                pe.wait_ge(r_padL, 4 * (h + 1))
                pe.wait_ge(r_tok, 4 * (h + 1))
                if h == 0:
                    pe.wait_ge(r_scopied, 2)
                for half in range(2):
                    for c in range(4):
                        nc.tensor.transpose(banks[:, turned(h) + half, c * P:c * P + P],
                                            vpad[:, c, 4 * half:4 * half + 4, :].rearrange("p a b -> p (a b)"), ident)
                    for z in range(2):
                        c = half * DK + z * P
                        mm = nc.tensor.transpose(banks[:, turned(h) + 2, c:c + P],
                                                 kpad[:, z, 4 * half:4 * half + 4, :].rearrange("p a b -> p (a b)"), ident)
                mm.then_inc(r_pturned, 1)

            def head_scores(h):
                pe.wait_ge(r_tok, 4 * (h + 1))
                for cols_, kk, qq in ((slice(0, 256), slice(0, P), slice(0, SEQ)),
                                      (slice(256, 384), slice(P, SEQ), slice(P, SEQ)),
                                      (slice(384, 416), slice(SEQ, T), slice(SEQ, T))):
                    for z in range(2):
                        rows = kk.stop - kk.start
                        mm = nc.tensor.matmul(banks[0:rows, turned(h) + 3, cols_], kr[:, 2 * h + z, kk], qr[:, 2 * h + z, qq],
                                              start=z == 0, stop=z == 1)
                mm.then_inc(r_scored, 1)

            def prompt_state(h):
                if h:
                    pe.wait_ge(r_stack, 2 * (h + 1))
                for z in range(2):
                    for tb in range(2):
                        mm = nc.tensor.matmul(banks[:, turned(h) + z, :], ktok_r[:, tb, z * P:z * P + P], vtok_r[:, tb, :],
                                              start=tb == 0, stop=tb == 1)
                    mm.then_inc(r_state, 1)

            def outputs(h):
                pe.wait_ge(r_decayed, 3 * (h + 1))
                pe.wait_ge(r_scopied, 2 * (h + 1))
                for c in range(4):
                    nc.tensor.matmul(banks[:, c, 0:SEQ], vtok_r[:, 0, c * P:c * P + P], at_sb[:, 0:SEQ],
                                     start=True, stop=False)
                    nc.tensor.matmul(banks[:, c, P:SEQ], vtok_r[:, 1, c * P:c * P + P], at_sb[:, 256:384],
                                     start=False, stop=True)
                    mm = nc.tensor.matmul(banks[:, c, SEQ:T], vtok_s[:, c * P:c * P + P], at_sb[0:NS, 384:416],
                                          start=True, stop=True)
                mm.then_inc(r_out, 1)

            def states(h, n):
                pe.wait_ge(s_landed[n % 4], 16 * (2 * h + n // 4 + 1))
                if n == 0:
                    pe.wait_ge(r_dec, 6 + h)
                    if h >= 2:
                        pe.wait_ge(os_copied, h - 1)
                for z in range(2):
                    mm = nc.tensor.matmul(banks[os_rows(h), 5, :], qpad[:, z, NS * n:NS * n + NS],
                                          sslot[:, n % 4, z * DV:z * DV + DV], start=n == 0 and z == 0,
                                          stop=n == NB - 1 and z == 1, skip_group_check=True)
                mm.then_inc(r_sread, 1)
                r = slice(32 * (n % 4), 32 * (n % 4) + 32)
                for z in range(2):
                    if h or n:
                        pe.wait_ge(r_updated, 2 * (NB * h + n - 1) + z + 1)
                    nc.tensor.matmul(banks[:, 6 + z, :], kst[r, h % 2, n // 4, z * P:z * P + P], vst[r, h % 2, n // 4, :],
                                     start=True, stop=True).then_inc(r_outer, 1)

            def turn_read(h):
                pe.wait_ge(os_copied, h + 1)
                if h:
                    pe.wait_ge(gn_rms, h)
                r = os_rows(h)
                for c in range(4):
                    mm = nc.tensor.transpose(banks[:, 4, T + c * NS:T + (c + 1) * NS], os_sb[r, c * P:c * P + P], ident[r, r])
                mm.then_inc(os_turned, 1)

            def mean(h, e):
                pe.wait_ge(*((gn_o, 3 * h + 1) if e == 0 else (gn_sq, h + 1)))
                for c in range(4):
                    mm = nc.tensor.matmul(banks[:, 4, 0:T], mean_v, o_sb[:, c, :], start=c == 0, stop=c == 3)
                mm.then_inc(gn_mean, 1)

            def gate_product(s, u, i):
                in_ret(s, u, i + 4)
                if RAWS * i + u == 1:
                    turn_head(0)
                if RAWS * i + u == 3:
                    head_scores(0)
                    prompt_state(0)
                if RAWS * i + u == 7:
                    turn_samples(0)

            loop(pe, S_RETIN + 16, 8, gate_product, peel=2)
            pe.wait_ge(g_dve, GBUF + GD_RET + N_RETIN)
            outputs(0)
            pe.wait_ge(r_stack, 2)
            for h in range(NHR):
                for n in range(NB):
                    states(h, n)
                    if h:
                        if n == 0:
                            turn_read(h - 1)
                        if n == 1:
                            mean(h - 1, 0)
                        if n == 2:
                            mean(h - 1, 1)
                    if h + 1 < NHR:
                        if n == 3:
                            pe.wait_ge(o_copied, h + 1)
                            turn_head(h + 1)
                        if n == 5:
                            turn_samples(h + 1)
                            head_scores(h + 1)
                        if n == 6:
                            prompt_state(h + 1)
                        if n == 7:
                            outputs(h + 1)
            def out_half(s, u, j, kh, half=None):
                hi, lo = yH[:, 8 * kh:8 * kh + 8, :], yL[:, 8 * kh:8 * kh + 8, :]
                if half is None:
                    return product(s, u, G(j), hi, lo, start=kh == 0, stop=kh == 1)
                pe.wait_ge(l_split, s + 1)
                for k in range(KT):
                    mm = tile_product(u, G(j), hi, lo, half, k, start=kh == 0, stop=kh == 1)
                if half == 1:
                    mm.then_inc(strip_used, 1)

            turn_read(NHR - 1)
            pe.wait_ge(yr_split, 2)
            out_half(S_RETOUT, S_RETOUT, 0, 0, half=0)
            mean(NHR - 1, 0)
            out_half(S_RETOUT, S_RETOUT, 0, 0, half=1)
            mean(NHR - 1, 1)
            out_half(S_RETOUT + 1, S_RETOUT + 1, 1, 0)
            pe.wait_ge(yr_split, NHR)
            for u in range(2, N_RETOUT):
                j = u - 2 if u < 4 else u // 2
                kh = 1 if u < 4 else u % 2
                if kh == 0:
                    pe.wait_ge(g_act, 8 + j - 1)
                out_half(S_RETOUT + u, S_RETOUT + u, j, kh)
            mean_square(mean_d, acc[:, 0, :], sq_sum, 12)
            mlp(S_FF1B, S_FF2B, GD_FF1B, 12, N_FF, 3)
            mean_square(mean_d, acc[:, 0, :], sq_sum, 16)

        @block.scalar
        def _(act):
            def round_strip(s, at, i=0):
                act.wait_ge(w_landed[at % RAWS], 16 * i + 16 * (at // RAWS + 1))
                if at >= SPL:
                    act.wait_ge(strip_used, s - SPL + 1)
                nc.scalar.activation(wH[:, at % SPL, :], raw[:, at % RAWS, :], ACT.Copy).then_inc(h_round, 1)

            def next_strip(s, u, i, first):
                round_strip(s + SPL, first + u + SPL, i)

            def round_x(k, layer, norm):
                nc.scalar.activation(hH[:, k, :], x[:, k, :], ACT.Copy, scale=gain(layer, norm, k)).then_inc(hx_round, 1)

            def pre_norm(b, layer, norm):
                for k in range(KT):
                    if b:
                        act.wait_ge(x_done, KT * (b - 1) + k + 1)
                        round_x(k, layer, norm)
                    elif k == KT // 2:
                        round_strip(1, 1)
                    if k >= 2:
                        act.wait_ge(xacc, KT * b + k - 1)
                    nc.scalar.activation(sq[:, k % 2, :], x[:, k, :], ACT.Square).then_inc(xsq_done, 1)
                root(2 * b)

            def load_sqrt(i):
                if i:
                    act.wait_ge(sqrt_loaded, i)
                nc.scalar.activation(scratch[:, :], rs_post[:, 0:1], ACT.Sqrt).then_inc(sqrt_loaded, 1)

            def root(e):
                act.wait_ge(ms_done, e + 1)
                nc.scalar.activation(rms[:, :], MS, ACT.Sqrt, bias=eps).then_inc(rms_done, 1)

            def take_y(e, j, last_strip):
                act.wait_ge(strip_used, last_strip + 1)
                nc.scalar.activation(y[:, 2 * j:2 * j + 2, :], G(j), ACT.Copy).then_inc(y_copied, 1)
                if j >= 2:
                    act.wait_ge(sq_sum, 4 * e + j - 1)
                nc.scalar.activation((sq if j else acc)[:, :, :], G(j), ACT.Square).then_inc(g_act, 1)

            def down(e, s, j, last):
                if j is not None and last:
                    take_y(e, j, s)
                if s + SPL < N_STRIPS:
                    round_strip(s + SPL, s + SPL)
                if j is not None and not last:
                    take_y(e, j, s)

            def mlp(first1, first2, gd, base, e):
                def up(s, u, i):
                    next_strip(s, u, i, first1)
                    act.wait_ge(g_dve, RAWS * i + (GBUF + gd + u + 1))
                    act.wait_ge(a_split, RAWS * i + (1 + base + u))
                    nc.scalar.activation(a_sb[:, :, :], relu_sb[:, u % 2, :, :], ACT.Square).then_inc(relu_sq, 1)
                    act.wait_ge(relu_sq, RAWS * i + (1 + base + u + 1))
                    nc.scalar.activation(aH[:, ds(8 * i + 2 * u, 2), :], a_sb[:, :, :], ACT.Copy).then_inc(a_round, 1)

                loop(act, first1, N_FF, up)
                for u in range(N_FF):
                    down(e, first2 + u, u // 4 if u % 4 == 3 else None, u == N_FF - 1)
                root(2 * e + 1)

            act.wait_ge(g_dve, GBUF)
            load_sqrt(0)
            act.wait_ge(cols_in, 16)
            act.wait_ge(x_landed, 16)
            nc.scalar.activation(rms[:, 0:1], col[:, 0:1], ACT.Copy).then_inc(relu_sq, 1)
            act.wait_ge(relu_sq, 1)
            for k in range(KT):
                round_x(k, 0, 0)
            act.wait_ge(w_landed[0], 16)
            for sem_, c in ((half_round, slice(0, HALF_STRIP)), (h_round, slice(HALF_STRIP, KT * SC))):
                nc.scalar.activation(wH[:, 0, c], raw[:, 0, c], ACT.Copy).then_inc(sem_, 1)
            pre_norm(0, 0, 0)
            for s in range(N_Q):
                next_strip(s, s, 0, 0)
            loop(act, S_KV, N_KV, lambda s, u, i: next_strip(s, u, i, S_KV))
            next_strip(S_BKV, 0, 0, S_BKV)
            for i in range(7):
                act.wait_ge(v_turned, i + 1)
                b0, n = 4 + 2 * (i % 2), 256 if i < 6 else 128
                nc.scalar.activation(vtok[:, 0:2, 256 * i:256 * i + n],
                                     banks[:, b0, :].rearrange("p (t c) -> p t c", t=2)[:, :, 0:n],
                                     ACT.Copy).then_inc(v_tok, 1)
                r = slice(NS * (i // 2), NS * (i // 2) + NS)
                if i < 6:
                    nc.scalar.activation(vnew[r, 256 * (i % 2):256 * (i % 2) + 256], banks[r, b0 + 1, 0:n],
                                         ACT.Copy).then_inc(v_tok, 1)
                else:
                    nc.scalar.activation(
                        vnew[r, :].rearrange("p (k f d) -> p k f d", k=2, f=4),
                        banks[r, b0 + 1, 0:n].rearrange("p (k d) -> p k d", k=2).unsqueeze(2).broadcast_to([NS, 2, 4, HD]),
                        ACT.Copy).then_inc(v_tok, 1)

            def exps(u):
                n = 3 if u < NH else 1
                act.wait_ge(negmax, u + 1)
                sm = small[:, u % 2, :]
                for b, c in ((0, slice(0, n * 256)), (1, slice(n * 256, n * 384))):
                    nc.scalar.activation(p_sb[:, u % 2, c], p_sb[:, u % 2, c], ACT.Exp, bias=sm[:, 2 + b:3 + b],
                                         scale=SCALE, accum_out=sm[:, 4 + b:5 + b]).then_inc(exp_done, 1)
                nc.scalar.activation(sm[:, 6:8], sm[:, 2:4], ACT.Exp,
                                     bias=col[:, C_SINKP + u:C_SINKP + u + 1]).then_inc(exp_done, 1)

            def copy_pt(u):
                n = 3 if u < NH else 1
                act.wait_ge(p_turned, u + 1)
                if u:
                    act.wait_ge(pv_done, u)
                nc.scalar.activation(pt_sb[:, 0:n, :], banks[:, 0:n, 0:384], ACT.Copy).then_inc(pt_copied, 1)

            def round_o(p):
                act.wait_ge(pv_done, 2 * (p + 1))
                nc.scalar.activation(hH[:, p, 0:SEQ], banks[:, 3, 0:SEQ], ACT.Copy).then_inc(o_round, 1)

            def pick_act(g):
                act.wait_ge(d_oturned, g + 1)
                for hp in range(4):
                    for e in range(2):
                        dst, src = own_head(g, hp, e)
                        nc.scalar.activation(dst(hH), src, ACT.Copy).then_inc(o_round, 1)

            exps(0)
            for u in range(NU):
                if u + 1 < NU:
                    exps(u + 1)
                copy_pt(u)
                if u >= 2 and u % 2 == 0:
                    round_o(u // 2 - 1)
            round_o(NH - 1)

            act.wait_ge(d_newT, 1)
            nc.scalar.activation(nt_sb[:, :], banks[:, 0, 0:NG_D * P], ACT.Copy).then_inc(d_newcopied, 1)
            for g in range(NG_D):
                act.wait_ge(d_negmax, 2 * (g + 1))
                for m, c in ((0, slice(0, CD + 96)), (1, slice(CD + 96, SROW))):
                    nc.scalar.activation(sp_sb[:, g, c], sp_sb[:, g, c], ACT.Exp, bias=dsm[:, g, 6 + m:7 + m], scale=SCALE,
                                         accum_out=dsm[:, g, 10 + m:11 + m]).then_inc(d_exp, 1)
                nc.scalar.activation(dsm[:, g, 12:14], dsm[:, g, 8:10], ACT.Exp).then_inc(d_exp, 1)
                act.wait_ge(d_pturned, g + 1)
                nc.scalar.activation(st_sb[:, g, :], banks[:, 1:4, :].rearrange("p a c -> p (a c)")[:, 0:SROW],
                                     ACT.Copy).then_inc(d_ptcopied, 1)
            for g in range(NG_D):
                act.wait_ge(c_used, CL * NB + 4 * CL * (g + 1))
                nc.scalar.activation(sp_sb[:, g, 0:512], banks[:, 4 + 2 * g, :], ACT.Copy).then_inc(d_ocopA, 1)
                if g:
                    pick_act(g - 1)
            pick_act(NG_D - 1)
            for j in range(N_MIXOUT):
                if j == 0:
                    load_sqrt(1)
                down(0, S_MIXOUT + j, j, j == N_MIXOUT - 1)
            root(1)
            pre_norm(1, 0, 2)
            act.wait_ge(k_stored, 16)
            mlp(S_FF1A, S_FF2A, GD_FF1A, 0, 1)
            pre_norm(2, 1, 0)
            loop(act, S_RETIN, 16, lambda s, u, i: next_strip(s, u, i, S_RETIN))

            def pad_head(h):
                if h == 0:
                    act.wait_ge(r_zero, 2)
                    act.wait_ge(r_dec, NHR)
                else:
                    act.wait_ge(r_pturned, h)
                for p in range(2):
                    nc.scalar.activation(
                        kpad[:, :, :, 4 * p:4 * p + 4].bitcast(F32R),
                        kd[:, 2 * h:2 * h + 2, :].rearrange("p z (n t) -> p z n t", t=NT), ACT.Copy).then_inc(r_padH, 1)
                for p in range(2):
                    nc.scalar.activation(
                        vpad[:, :, :, 8 * p:8 * p + 4].bitcast(F32R),
                        vTr[:, 4 * h:4 * h + 4, SEQ:T].rearrange("p c (n t) -> p c n t", t=NT), ACT.Copy).then_inc(r_padH, 1)

            def gate_silu(s, u, i):
                next_strip(s, u, i, S_RETIN + 16)
                act.wait_ge(g_dve, RAWS * i + (GBUF + GD_RET + 16 + u + 1))
                g = gate[:, ds(8 * i + 2 * u, 2), :]
                nc.scalar.activation(g, g, ACT.Silu).then_inc(gated, 1)

            def copy_turned(h):
                b = turned(h)
                act.wait_ge(r_turned, h + 1)
                if h == 0:
                    act.wait_ge(rope_out, 1 + 2 * (16 + 8))
                nc.scalar.activation(vtok_r[:, :, :], banks[:, b:b + 2, :], ACT.Copy).then_inc(r_tok, 1)
                nc.scalar.activation(vtok_s[:, :], banks[0:NS, b + 3, :], ACT.Copy).then_inc(r_tok, 1)
                for tb in range(2):
                    c = C_KDEC + tb * NHR + h
                    nc.scalar.activation(ktok_r[:, tb, :], banks[:, b + 2, tb * DK:tb * DK + DK], ACT.Copy,
                                         scale=col[:, c:c + 1]).then_inc(r_tok, 1)

            def copy_stack(h):
                b = turned(h)
                act.wait_ge(r_pturned, h + 1)
                nc.scalar.activation(vst[:, h % 2, :, :], banks[:, b:b + 2, :], ACT.Copy).then_inc(r_stack, 1)
                nc.scalar.activation(kst[:, h % 2, :, :], banks[:, b + 2, :].rearrange("p (a c) -> p a c", a=2),
                                     ACT.Copy).then_inc(r_stack, 1)

            def copy_state(h):
                if h:
                    act.wait_ge(ps_stored, 16 * 2 * h)
                for z in range(2):
                    act.wait_ge(r_state, 2 * h + z + 1)
                    nc.scalar.activation(ps_sb[z], banks[:, turned(h) + z, :], ACT.Copy).then_inc(r_scopied, 1)

            def gate_step(s, u, i):
                gate_silu(s, u, i)
                if RAWS * i + u == 2:
                    copy_turned(0)
                if RAWS * i + u == 4:
                    copy_state(0)
                if RAWS * i + u == 5:
                    pad_head(0)

            loop(act, S_RETIN + 16, 8, gate_step, peel=2)

            def norm_head(h):
                act.wait_ge(r_sread, NB * (h + 1))
                nc.scalar.activation(os_sb[os_rows(h), :], banks[os_rows(h), 5, :], ACT.Copy).then_inc(os_copied, 1)
                act.wait_ge(gn_o, 3 * h + 2)
                nc.scalar.activation(o_sb, oc_sb, ACT.Square).then_inc(gn_sq, 1)
                act.wait_ge(gn_mean, 2 * (h + 1))
                nc.scalar.activation(rms[:, :], banks[:, 4, 0:T], ACT.Sqrt, bias=gn_eps).then_inc(gn_rms, 1)

            def round_y(h):
                act.wait_ge(gn_o, 3 * (h + 1))
                nc.scalar.activation(yH[:, 4 * h:4 * h + 4, :], oc_sb, ACT.Copy).then_inc(yr_round, 1)

            def copy_o(h):
                act.wait_ge(r_out, h + 1)
                nc.scalar.activation(o_sb, banks[:, 0:4, 0:T], ACT.Copy).then_inc(o_copied, 1)

            act.wait_ge(strip_used, S_RETOUT)
            act.wait_ge(gated, 8)
            copy_stack(0)
            copy_o(0)
            for h in range(NHR):
                if h:
                    norm_head(h - 1)
                    copy_o(h)
                if h + 1 < NHR:
                    pad_head(h + 1)
                if h:
                    round_y(h - 1)
                if h + 1 < NHR:
                    copy_turned(h + 1)
                    copy_stack(h + 1)
                    copy_state(h + 1)
            norm_head(NHR - 1)
            round_strip(S_RETOUT + SPL, S_RETOUT + SPL)
            round_y(NHR - 1)

            for u in range(N_RETOUT):
                if u == 2:
                    act.wait_ge(ps_stored, 16 * 2 * NHR)
                if u:
                    down(2, S_RETOUT + u, RET_GROUP.get(u), u == N_RETOUT - 1)
            root(5)
            pre_norm(3, 1, 2)
            for j in range(4):
                act.wait_ge(s_stored[j], 16 * 2 * NHR)
            mlp(S_FF1B, S_FF2B, GD_FF1B, N_FF, 3)

        @block.vector
        def _(dve):
            def split_strip(s, at):
                dve.wait_ge(h_round, s + 1)
                nc.vector.tensor_tensor(wL[:, at % SPL, :], raw[:, at % RAWS, :], wH[:, at % SPL, :].bitcast(F32),
                                        ALU.subtract).then_inc(l_split, 1)

            def inverse(e, to):
                dve.wait_ge(rms_done, e + 1)
                nc.vector.reciprocal(to[:, :], rms[:, :]).then_inc(rs_done, 1)

            def split_x(b, k, layer, norm):
                dve.wait_ge(hx_round, KT * b + k + 1)
                nc.vector.scalar_tensor_tensor(out=hL[:, k, :], in0=x[:, k, :], scalar=gain(layer, norm, k),
                                               in1=hH[:, k, :].bitcast(F32), op0=ALU.mult,
                                               op1=ALU.subtract).then_inc(hx_split, 1)

            def pre_norm(b, layer, norm, part=None):
                inverse(2 * b, rs_pre)
                dve.wait_ge(rs_done, 2 * b + 1)

            def residual(e, layer, norm, s=None, b=None, nlayer=0, nnorm=0):
                inverse(2 * e + 1, rs_post)
                dve.wait_ge(rs_done, 2 * e + 2)
                for k in range(KT + 2):
                    if k < KT:
                        if k >= 2:
                            dve.wait_ge(x_done, KT * e + k - 1)
                        nc.vector.scalar_tensor_tensor(out=tmp[:, k % 2, :], in0=y[:, k, :], scalar=gain(layer, norm, k),
                                                       in1=rs_post[:, :], op0=ALU.mult, op1=ALU.mult).then_inc(t_done, 1)
                    if 1 <= k <= KT:
                        dve.wait_ge(t_done, KT * e + k)
                        nc.vector.tensor_tensor(x[:, k - 1, :], x[:, k - 1, :], tmp[:, (k - 1) % 2, :],
                                                ALU.add).then_inc(x_done, 1)
                    if k >= 2 and b is not None:
                        split_x(b, k - 2, nlayer, nnorm)
                if s is not None:
                    split_strip(s + SPL, s + SPL)

            def sum_y(e, j, ga):
                dve.wait_ge(g_act, ga + j + 1)
                if j >= 1:
                    if j >= 2:
                        dve.wait_ge(sq_sum, 4 * e + j - 1)
                    nc.vector.tensor_tensor(acc[:, :, :], acc[:, :, :], sq[:, :, :], ALU.add).then_inc(sq_sum, 1)
                if j == 3:
                    dve.wait_ge(sq_sum, 4 * e + 3)
                    nc.vector.tensor_tensor(acc[:, 0, :], acc[:, 0, :], acc[:, 1, :], ALU.add).then_inc(sq_sum, 1)

            def rotate(s, gj, u, rj, out, at=None):
                if s is not None:
                    dve.wait_ge(strip_used, s + 1)
                dve.wait_ge(rope_out, 1 + 2 * rj)
                nc.vector.tensor_tensor(sq[:, :, :], G(u), both(trigR[:, 0, :]), ALU.mult).then_inc(rope_mul, 1)
                nc.vector.tensor_tensor(acc[:, :, :], G(u), both(trigR[:, 1, :]), ALU.mult).then_inc(g_dve, 1)
                if s is not None:
                    split_strip(s + SPL, at + SPL)
                dve.wait_ge(rope_mul, rj + 1)
                dve.wait_ge(g_dve, GBUF + gj + 1)
                nc.vector.tensor_tensor(out(0), sq[:, 0:1, :], acc[:, 1:2, :], ALU.subtract).then_inc(rope_out, 1)
                nc.vector.tensor_tensor(out(1), sq[:, 1:2, :], acc[:, 0:1, :], ALU.add).then_inc(rope_out, 1)

            def down(e, s, j, last, ga):
                if s + SPL < N_STRIPS and not last:
                    split_strip(s + SPL, s + SPL)
                if j is not None:
                    sum_y(e, j, ga)

            def mlp(first1, first2, gd, ga, base, e):
                def up(s, u, i):
                    dve.wait_ge(strip_used, s + 1)
                    dve.wait_ge(relu_sq, RAWS * i + (1 + base + u))
                    nc.vector.scalar_tensor_tensor(out=relu_sb[:, u % 2, :, :], in0=G(u), scalar=0.0,
                                                   in1=both(rs_pre[:, :]), op0=ALU.max, op1=ALU.mult).then_inc(g_dve, 1)
                    split_strip(s + SPL, first1 + u + SPL)
                    dve.wait_ge(a_round, RAWS * i + (base + u + 1))
                    nc.vector.tensor_tensor(aL[:, ds(8 * i + 2 * u, 2), :], a_sb[:, :, :],
                                            aH[:, ds(8 * i + 2 * u, 2), :].bitcast(F32), ALU.subtract).then_inc(a_split, 1)

                loop(dve, first1, N_FF, up)
                for u in range(N_FF):
                    down(e, first2 + u, u // 4 if u % 4 == 3 else None, u == N_FF - 1, ga)

            nc.vector.memset(rs_post[:, :], 0.0).then_inc(g_dve, GBUF)
            nc.vector.memset(rs_pre[:, :], 0.0).then_inc(rope_out, 1)
            nc.vector.memset(tmp[:, :, :], 0.0).then_inc(a_split, 1)
            for first, count in ((g_dve, GBUF), (rope_out, 1), (a_split, 1)):
                dve.wait_ge(first, count)
            dve.wait_ge(cols_in, 16)
            for k in range(KT):
                split_x(0, k, 0, 0)
            for ready, c, done in ((half_round, slice(0, HALF_STRIP), half_split), (h_round, slice(HALF_STRIP, KT * SC), l_split)):
                dve.wait_ge(ready, 1)
                nc.vector.tensor_tensor(wL[:, 0, c], raw[:, 0, c], wH[:, 0, c].bitcast(F32), ALU.subtract).then_inc(done, 1)
            split_strip(1, 1)
            pre_norm(0, 0, 0)
            dve.wait_ge(trig_in, 16)
            nc.vector.tensor_tensor(trigR[:, :, :], trig_sb[:, :, :], both(rs_pre[:, :]), ALU.mult).then_inc(trigR_done, 1)
            dve.wait_ge(trigR_done, 1)

            def q_strip(s, u, i):
                rotate(s, RAWS * i + u, u, RAWS * i + u, lambda z: qT[:, ds(8 * i + (2 * u + z), 1), :], S_Q + u)

            loop(dve, S_Q, N_Q, q_strip)

            def kv_strip(s, u, i):
                if u < 2:
                    rotate(s, RAWS * i + (N_Q + u), u, 2 * i + (N_Q + u), lambda z: kT[:, ds(4 * i + (2 * u + z), 1), :],
                           S_KV + u)
                else:
                    dve.wait_ge(strip_used, s + 1)
                    nc.vector.tensor_tensor(vT[:, ds(4 * i + 2 * (u - 2), 2), :], G(u), both(rs_pre[:, :]),
                                            ALU.mult).then_inc(g_dve, 1)
                    split_strip(s + SPL, S_KV + u + SPL)

            loop(dve, S_KV, N_KV, kv_strip)
            dve.wait_ge(strip_used, S_BKV + 1)
            nc.vector.tensor_copy(kz[:, :], G(20)[:, 0, :]).then_inc(kz_done, 1)
            nc.vector.tensor_tensor(vT[:, 4 * NG, :], G(20)[:, 1, :], rs_pre[:, :], ALU.mult).then_inc(g_dve, 1)
            split_strip(S_BKV + SPL, S_BKV + SPL)

            def mask_q(u):
                j, n = u % NH, 3 if u < NH else 1
                if u == 0:
                    dve.wait_ge(l_split, HELD)
                    dve.wait_ge(rope_out, 1 + 2 * (N_Q + 2 * NG))
                if u == 1:
                    dve.wait_ge(rope_out, 1 + 2 * 4 * NBR)
                t0 = 2 * (j // 4) + (0 if u < NH else 4 * NG)
                src = qT[:, t0:t0 + 4 * (n - 1) + 2, 0:SEQ] if n == 1 else qT[:, 0:4 * NG, 0:SEQ].rearrange(
                    "p (b s z) t -> p b s z t", b=NG, s=2)[:, :, j // 4, :, :]
                out = qm[u % 2][:, 0, :, :] if n == 1 else qm[u % 2]
                nc.vector.tensor_scalar(out, src, col[:, C_HEAD + j % 4:C_HEAD + j % 4 + 1], None,
                                        ALU.mult).then_inc(q_masked, 1)

            mask_q(0)
            for s in range(2):
                dve.wait_ge(sel_done, s + 1)
                rotate(None, 21 + s, 21 + s, 14 + s, lambda z: kT[:, 12 + 2 * s + z:13 + 2 * s + z, :])

            def mask_unit(u):
                n = 3 if u < NH else 1
                br = slice(0, 3) if u < NH else slice(3, 4)
                dve.wait_ge(scored, u + 1)
                if u >= 2:
                    dve.wait_ge(p_turned, u - 1)
                if u == 0:
                    dve.wait_ge(mask_in, 48)
                    dve.wait_ge(v_stored, 16)
                    dve.wait_ge(v_tok, 14)
                sm = small[:, u % 2, :]
                nc.vector.tensor_tensor_reduce(
                    out=p_sb[:, u % 2, 0:n * 256], in0=late(u)[:, 0:n * 256], in1=pm[:, br, :].rearrange("p a c -> p (a c)"),
                    scale=1.0, scalar=-3e38, op0=ALU.add, op1=ALU.max, accum_out=sm[:, 0:1]).then_inc(masked, 1)
                nc.vector.tensor_tensor_reduce(
                    out=p_sb[:, u % 2, n * 256:n * 384].rearrange("p (a c) -> p a c", a=n),
                    in0=early(u)[:, 0:n * P].rearrange("p (a c) -> p a c", a=n), in1=pm[:, br, P:2 * P],
                    scale=1.0, scalar=-3e38, op0=ALU.add, op1=ALU.max, accum_out=sm[:, 1:2]).then_inc(masked, 1)
                dve.wait_ge(masked, 2 * (u + 1))
                nc.vector.tensor_scalar(sm[:, 8:10], sm[:, 0:2], SCALE, col[:, C_SINKP + u:C_SINKP + u + 1],
                                        ALU.mult, ALU.max).then_inc(max_scaled, 1)
                dve.wait_ge(max_scaled, u + 1)
                nc.vector.tensor_scalar(sm[:, 2:4], sm[:, 8:10], -1.0, None, ALU.mult).then_inc(negmax, 1)

            def norm_unit(u):
                n = 3 if u < NH else 1
                sm = small[:, u % 2, :]
                dve.wait_ge(exp_done, 3 * (u + 1))
                nc.vector.tensor_tensor(sm[:, 8:10], sm[:, 4:6], sm[:, 6:8], ALU.add).then_inc(l_done, 1)
                dve.wait_ge(l_done, 2 * u + 1)
                nc.vector.reciprocal(sm[:, 4:6], sm[:, 8:10]).then_inc(l_done, 1)
                dve.wait_ge(l_done, 2 * u + 2)
                for b, c in ((0, slice(0, n * 256)), (1, slice(n * 256, n * 384))):
                    nc.vector.tensor_scalar(p_sb[:, u % 2, c], p_sb[:, u % 2, c], sm[:, 4 + b:5 + b], None,
                                            ALU.mult).then_inc(p_norm, 1)

            def split_o(p):
                dve.wait_ge(o_round, p + 1)
                nc.vector.tensor_tensor(hL[:, p, 0:SEQ], banks[:, 3, 0:SEQ], hH[:, p, 0:SEQ].bitcast(F32),
                                        ALU.subtract).then_inc(o_split, 1)

            mask_q(1)
            mask_unit(0)
            mask_q(2)
            for u in range(NU):
                norm_unit(u)
                if u + 1 < NU:
                    mask_unit(u + 1)
                if u + 3 < NU:
                    mask_q(u + 3)
                if u >= 2 and u % 2 == 0:
                    split_o(u // 2 - 1)
            split_o(NH - 1)

            dve.wait_ge(d_newrow, 1)
            for g in range(NG_D):
                dve.wait_ge(c_used, 4 * CL * (g + 1))
                old = banks[:, 4 + 2 * g:6 + 2 * g, :].rearrange("p a c -> p (a c)")
                new, newm = banks[:, 0, 256 + g * P:256 + g * P + P], dm_new[:, g * P:g * P + P]
                for a, (c, src, mask) in enumerate((
                        (slice(0, CD), old[:, 0:CD], dm[:, 0:CD]), (slice(CD + 96, SROW - NS), old[:, CD:CW], dm[:, CD:CW]),
                        (slice(CD, CD + 96), new[:, 0:96], newm[:, 0:96]),
                        (slice(SROW - NS, SROW), new[:, 96:P], newm[:, 96:P]))):
                    nc.vector.tensor_tensor_reduce(out=sp_sb[:, g, c], in0=src, in1=mask, scale=1.0, scalar=-3e38,
                                                   op0=ALU.add, op1=ALU.max, accum_out=dsm[:, g, a:a + 1]).then_inc(d_masked, 1)
                sm = dsm[:, g, :]
                dve.wait_ge(d_masked, 4 * (g + 1))
                nc.vector.tensor_tensor(sm[:, 4:6], sm[:, 0:2], sm[:, 2:4], ALU.max).then_inc(d_max, 1)
                dve.wait_ge(d_max, g + 1)
                nc.vector.scalar_tensor_tensor(out=sm[:, 14:16], in0=sm[:, 4:6], scalar=SCALE,
                                               in1=col[:, C_SINKD:C_SINKD + 2], op0=ALU.mult, op1=ALU.max).then_inc(d_max2, 1)
                dve.wait_ge(d_max2, g + 1)
                nc.vector.tensor_scalar(sm[:, 6:8], sm[:, 14:16], -1.0, None, ALU.mult).then_inc(d_negmax, 1)
                nc.vector.tensor_tensor(sm[:, 8:10], col[:, C_SINKD:C_SINKD + 2], sm[:, 14:16],
                                        ALU.subtract).then_inc(d_negmax, 1)
                dve.wait_ge(d_exp, 3 * (g + 1))
                nc.vector.tensor_tensor(sm[:, 16:18], sm[:, 10:12], sm[:, 12:14], ALU.add).then_inc(d_l, 1)
                dve.wait_ge(d_l, 2 * g + 1)
                nc.vector.reciprocal(sm[:, 18:20], sm[:, 16:18]).then_inc(d_l, 1)
                dve.wait_ge(d_l, 2 * g + 2)
                for m, c in ((0, slice(0, CD + 96)), (1, slice(CD + 96, SROW))):
                    nc.vector.tensor_scalar(sp_sb[:, g, c], sp_sb[:, g, c], sm[:, 18 + m:19 + m], None,
                                            ALU.mult).then_inc(d_norm, 1)

            def pick_dve(g):
                dve.wait_ge(o_round, NH + 8 * (g + 1))
                for hp in range(4):
                    for e in range(2):
                        dst, src = own_head(g, hp, e)
                        nc.vector.tensor_tensor(dst(hL), src, dst(hH).bitcast(F32), ALU.subtract).then_inc(o_split, 1)

            for g in range(NG_D):
                dve.wait_ge(c_used, CL * NB + 4 * CL * (g + 1))
                nc.vector.tensor_copy(sp_sb[:, g, 512:1024], banks[:, 5 + 2 * g, :]).then_inc(d_ocopB, 1)
                if g:
                    pick_dve(g - 1)
            pick_dve(NG_D - 1)
            for j in range(N_MIXOUT):
                down(0, S_MIXOUT + j, j, j == N_MIXOUT - 1, 0)
            residual(0, 0, 1, S_FF1A - 1, 1, 0, 2)
            pre_norm(1, 0, 2)
            dve.wait_ge(k_stored, 16)
            dve.wait_ge(k_stored, 16)
            mlp(S_FF1A, S_FF2A, GD_FF1A, 4, 0, 1)
            residual(1, 0, 3, S_RETIN - 1, 2, 1, 0)
            pre_norm(2, 1, 0)
            dve.wait_ge(trig_in, 32)
            nc.vector.tensor_tensor(trigR[:, :, :], trig_sb[:, :, :], both(rs_pre[:, :]), ALU.mult).then_inc(trigR_done, 1)
            dve.wait_ge(trigR_done, 2)

            for t, dst in ((0, qr), (1, kr)):
                for u in range(NHR):
                    s = S_RETIN + 4 * t + u
                    rotate(s, GD_RET + 4 * t + u, u, 16 + 4 * t + u, lambda z: dst[:, 2 * u + z:2 * u + z + 1, :], s)

            def v_strip(s, u, i):
                dve.wait_ge(strip_used, s + 1)
                nc.vector.tensor_tensor(vTr[:, ds(8 * i + 2 * u, 2), :], G(u), both(rs_pre[:, :]),
                                        ALU.mult).then_inc(g_dve, 1)
                split_strip(s + SPL, S_RETIN + 8 + u + SPL)

            loop(dve, S_RETIN + 8, 8, v_strip)

            dve.wait_ge(rmask_in, 32)
            dve.wait_ge(rope_out, 1 + 2 * (16 + 8))
            for h in range(NHR):
                nc.vector.tensor_tensor(kd[:, 2 * h:2 * h + 2, :], kr[:, 2 * h:2 * h + 2, SEQ:T],
                                        dec[:, 1, h, :].unsqueeze(1).broadcast_to([P, 2, NS]), ALU.mult).then_inc(r_dec, 1)
            nc.vector.memset(qpad[:, :, :], 0.0).then_inc(r_dec, 1)

            def query(h):
                if h:
                    dve.wait_ge(r_sread, NB * h)
                dve.wait_ge(r_dec, NHR + 1)
                nc.vector.tensor_tensor(own_q, qr[:, 2 * h:2 * h + 2, SEQ:T].rearrange("p z (n t) -> p z n t", t=NT),
                                        dec[:, 0, h, :].rearrange("p (n t) -> p n t", t=NT).unsqueeze(1).broadcast_to(
                                            [P, 2, NB, NT]), ALU.mult).then_inc(r_dec, 1)

            query(0)

            def pad_low(h):
                dve.wait_ge(r_padH, 4 * (h + 1))
                if h == 0:
                    dve.wait_ge(r_dec, NHR)
                for p in range(2):
                    nc.vector.tensor_tensor(kpad[:, :, :, 8 + 4 * p:12 + 4 * p],
                                            kd[:, 2 * h:2 * h + 2, :].rearrange("p z (n t) -> p z n t", t=NT),
                                            kpad[:, :, :, 4 * p:4 * p + 4], ALU.subtract).then_inc(r_padL, 1)
                for p in range(2):
                    nc.vector.tensor_tensor(vpad[:, :, :, 4 + 8 * p:8 + 8 * p],
                                            vTr[:, 4 * h:4 * h + 4, SEQ:T].rearrange("p c (n t) -> p c n t", t=NT),
                                            vpad[:, :, :, 8 * p:8 * p + 4], ALU.subtract).then_inc(r_padL, 1)

            def gate_strip(s, u, i):
                dve.wait_ge(strip_used, s + 1)
                nc.vector.tensor_tensor(gate[:, ds(8 * i + 2 * u, 2), :], G(u), both(rs_pre[:, :]),
                                        ALU.mult).then_inc(g_dve, 1)
                split_strip(s + SPL, S_RETIN + 16 + u + SPL)
            def decay(h):
                b = turned(h) + 3
                dve.wait_ge(r_scored, h + 1)
                if h == 0:
                    dve.wait_ge(rmask_in, 32)
                nc.vector.tensor_tensor(at_sb[:, 0:256], banks[:, b, 0:256], rm[:, h, 0:256], ALU.mult).then_inc(r_decayed, 1)
                nc.vector.tensor_tensor(at_sb[:, 256:384], banks[:, b, 256:384], rm[:, h, 0:128],
                                        ALU.mult).then_inc(r_decayed, 1)
                nc.vector.tensor_tensor(at_sb[0:NS, 384:416], banks[0:NS, b, 384:416], rm[0:NS, h, 256:288],
                                        ALU.mult).then_inc(r_decayed, 1)

            def gate_step(s, u, i):
                gate_strip(s, u, i)
                if RAWS * i + u == 4:
                    decay(0)
                if RAWS * i + u == 6:
                    pad_low(0)

            loop(dve, S_RETIN + 16, 8, gate_step, peel=2)
            def update(h, n):
                for z in range(2):
                    dve.wait_ge(r_outer, 2 * (NB * h + n) + z + 1)
                    c = sslot[:, n % 4, z * DV:z * DV + DV]
                    nc.vector.scalar_tensor_tensor(out=c, in0=c, scalar=GAMMA[h] ** NT, in1=banks[:, 6 + z, :],
                                                   op0=ALU.mult, op1=ALU.add).then_inc(r_updated, 1)

            def add_read(h):
                dve.wait_ge(os_turned, h + 1)
                dve.wait_ge(o_copied, h + 1)
                nc.vector.tensor_tensor(o_sb[:, :, SEQ:T], o_sb[:, :, SEQ:T],
                                        banks[:, 4, T:T + 4 * NS].rearrange("p (c t) -> p c t", c=4),
                                        ALU.add).then_inc(gn_o, 1)

            def centre(h):
                dve.wait_ge(gn_mean, 2 * h + 1)
                nc.vector.tensor_tensor(oc_sb, o_sb, banks[:, 4, 0:T].unsqueeze(1).broadcast_to([P, 4, T]),
                                        ALU.subtract).then_inc(gn_o, 1)

            def scale(h):
                dve.wait_ge(gn_rms, h + 1)
                nc.vector.reciprocal(rs_post[:, :], rms[:, :]).then_inc(gn_rs, 1)
                dve.wait_ge(gn_rs, 2 * h + 1)
                nc.vector.tensor_tensor(oc_sb, oc_sb, rs_post[:, :].unsqueeze(1).broadcast_to([P, 4, T]),
                                        ALU.mult).then_inc(gn_rs, 1)

            def times_gate(h):
                dve.wait_ge(gn_rs, 2 * h + 2)
                nc.vector.tensor_tensor(oc_sb, oc_sb, gate[:, 4 * h:4 * h + 4, :], ALU.mult).then_inc(gn_o, 1)

            def split_y(h):
                dve.wait_ge(yr_round, h + 1)
                nc.vector.tensor_tensor(yL[:, 4 * h:4 * h + 4, :], oc_sb, yH[:, 4 * h:4 * h + 4, :].bitcast(F32),
                                        ALU.subtract).then_inc(yr_split, 1)

            norm_steps = {0: add_read, 1: centre, 3: scale, 4: times_gate, 5: split_y}
            next_steps = {2: pad_low, 6: decay}
            for h in range(NHR):
                for n in range(NB):
                    update(h, n)
                    if h and n in norm_steps:
                        norm_steps[n](h - 1)
                    if h + 1 < NHR and n in next_steps:
                        next_steps[n](h + 1)
                if h + 1 < NHR:
                    query(h + 1)
            for step in norm_steps.values():
                step(NHR - 1)

            for u in range(N_RETOUT):
                down(2, S_RETOUT + u, RET_GROUP.get(u), u == N_RETOUT - 1, 8)
            residual(2, 1, 1, S_FF1B - 1, 3, 1, 2)
            pre_norm(3, 1, 2)
            for j in range(4):
                dve.wait_ge(s_stored[j], 16 * 2 * NHR)
            mlp(S_FF1B, S_FF2B, GD_FF1B, 12, N_FF, 3)
            residual(3, 1, 3)


def _strips(w, order):
    blocks = [w[r * D:(r + 1) * D, c * SC:(c + 1) * SC].reshape(KT, P, SC).transpose(1, 0, 2).reshape(P, KT * SC)
              for r, c in order]
    return blocks


def _halves(w):
    return w.reshape(w.shape[0], -1, 4, 2, HALF).transpose(0, 1, 3, 2, 4).reshape(w.shape[0], -1)


def _weights(w_in_mix, w_out_mix, w_in_ret, w_out_ret, w_ff1, w_ff2):
    n = NH * HD
    a = w_in_mix[0][:, :3 * NG * n].reshape(D, NG, 3, n)
    b = w_in_mix[0][:, 3 * NG * n:]
    col1 = [(0, 0), (0, 1)]
    out = []
    for g in range(NG):
        out += _strips(_halves(a[:, g, 0]), col1)
    out += _strips(_halves(b[:, :n]), col1)
    for g in range(NG):
        out += _strips(_halves(a[:, g, 1]), col1) + _strips(a[:, g, 2], col1)
    out += _strips(b[:, n:], [(0, 0)])
    out += _strips(w_out_mix[0], [(0, c) for c in range(4)])

    def mlp(layer):
        return (_strips(w_ff1[layer], [(0, c) for c in range(16)])
                + _strips(w_ff2[layer], [(r, c) for c in range(4) for r in range(4)]))

    out += mlp(0)
    out += _strips(w_in_ret[0], [(0, c) for c in range(24)])
    out += _strips(w_out_ret[0], [(0, 0), (0, 1), (1, 0), (1, 1), (0, 2), (1, 2), (0, 3), (1, 3)])
    out += mlp(1)
    return np.stack(out)


def _caches(c0, c1, c2, swa):
    a, b, c, d = c0[0], c1[0], c2[0], swa[0]
    b = b.reshape(NB, P, 4, 2, NH, HD)
    c = c.reshape(NB, 64, 16, 2, NH, HD)[:, :, :4].transpose(0, 2, 1, 3, 4, 5).reshape(NB, 2, P, 2, NH, HD)
    d = np.repeat(d, NH // 2, axis=3)
    tiles = np.concatenate([b.transpose(0, 2, 1, 3, 4, 5), c, a[:, None], d[:, None]], axis=1)
    k, v = tiles[:, :, :, 0], tiles[:, :, :, 1]
    k = k.reshape(NB, NKT * P, 2, 4, 2, HALF).transpose(0, 2, 4, 3, 5, 1).reshape(NB, CL, P, CLOAD)
    v = v.reshape(NB, CL, 2, P, 512).transpose(0, 1, 3, 2, 4).reshape(NB, CL, P, CLOAD)
    return np.ascontiguousarray(k), np.ascontiguousarray(v)


def _positions():
    return np.concatenate([np.arange(SEQ), np.tile(PAST + np.arange(NT), NB)])


def _trig():
    pos = _positions().astype(np.float32)
    out = []
    for half in (HALF, DK // 2):
        inv = np.float32(10000.0) ** (-np.arange(half, dtype=np.float32) * np.float32(2.0 / (2 * half)))
        ang = pos[None, :] * inv[np.arange(P) % half][:, None]
        out.append(np.stack([np.cos(ang), np.sin(ang)], axis=1))
    return np.stack(out).astype(np.float32)


def _masks():
    p = np.arange(P)[:, None]
    j = np.arange(2 * P)[None, :]
    diff = P + p - j
    rows = [(diff >= 0) & (diff <= w) & (diff % dil == 0) for w, dil in zip(WINS, DILS)]
    rows.append((diff >= 0) & (diff <= 127))
    pm = np.where(np.stack(rows, axis=1), 0.0, NEG).astype(np.float32)
    t = p // 4 % 4
    j = np.arange(P)[None, :]
    n2, t2 = np.arange(NS)[None, :] // 4, np.arange(NS)[None, :] % 4
    ok = [np.broadcast_to(t == r, (P, P)) for r in range(4)]
    ok += [t == 2 * r + j // 64 for r in range(2)] + [j >= t, j >= t + 1]
    for g in range(NG_D):
        n = 4 * g + p // 32
        own, upto = (n == n2) & (t == t2), (n == n2) & (t2 <= t)
        ok += [upto, own, own, upto]
    ok = np.concatenate(ok, axis=1)
    dm = np.where(ok, 0.0, NEG).astype(np.float32)
    g = np.array(GAMMA)[None, :, None]
    i = np.arange(SEQ)[None, None, :]
    pp = np.arange(P)[:, None, None]
    big = np.where(i >= pp, g ** np.maximum(i - pp, 0), 0.0) / 16
    ti = np.arange(NS)[None, None, :]
    okk = (pp // 4 == ti // 4) & (pp % 4 <= ti % 4) & (pp < NS)
    sm = np.where(okk, g ** np.maximum(ti % 4 - pp % 4, 0), 0.0) / 16
    rm = np.concatenate([big, sm], axis=2).astype(np.float32)
    t = np.arange(NS) % NT
    gh = np.array(GAMMA)[:, None]
    dec = np.stack([gh ** (t + 1), gh ** (NT - 1 - t) / 16])
    dec = np.broadcast_to(dec[None], (P,) + dec.shape).astype(np.float32)
    return pm, dm, rm, np.ascontiguousarray(dec)


def _columns(gains, sinks):
    col = np.zeros((P, N_COL), np.float32)
    col[:, C_GAIN:C_GAIN + 64] = gains.reshape(8, KT, P).transpose(2, 0, 1).reshape(P, 64)
    col[:, C_SINKP:C_SINKP + 8] = NEG
    col[:, C_SINKP + 8:C_SINKP + 16] = sinks[0][None, :]
    p = np.arange(P)
    col[:, C_SINKD] = NEG
    col[:, C_SINKD + 1] = sinks[0][p // 16 % 2 * 4 + p % 4]
    j = np.arange(SEQ).reshape(2, P)
    for tb in range(2):
        for h in range(NHR):
            col[:, C_KDEC + tb * NHR + h] = GAMMA[h] ** (SEQ - 1 - j[tb]) / 16
    col[:, C_EPS] = EPS
    col[:, C_GNEPS] = GN_EPS
    col[p, C_HEAD + p // 32] = 1.0
    return col


def _matrices():
    m = np.zeros((P, 7, P), np.float32)
    m[:, 0] = np.eye(P)
    m[:, 1] = 1.0 / D
    m[:, 2] = 1.0 / DV
    for s in range(2):
        for z in range(2):
            for c in range(P):
                m[(2 * s + z) * HALF + c % HALF, 3 + 2 * s + z, c] = 1.0
    return m


def kernel(x_prompt, x_sample, cache_dil_w128, cache_dil_w512, cache_dil_w2048, cache_swa, state_ret,
           norm_gains, w_in_mix, w_out_mix, attn_sinks, w_in_ret, w_out_ret, w_ff1, w_ff2):
    import concourse.bacc as _bacc
    from concourse.bass_utils import run_bass_kernel_spmd as _run

    arr = [np.asarray(a) for a in (x_prompt, x_sample, cache_dil_w128, cache_dil_w512, cache_dil_w2048, cache_swa,
                                   state_ret, norm_gains, w_in_mix, w_out_mix, attn_sinks, w_in_ret, w_out_ret,
                                   w_ff1, w_ff2)]
    xp, xs, c0, c1, c2, swa, st, gains, wim, wom, sinks, wir, wor, wf1, wf2 = arr
    xcat = np.concatenate([xp[0], xs.reshape(NS, D)], axis=0)
    kc, vc = _caches(c0, c1, c2, swa)
    pm, dm, rm, dec = _masks()
    ins = {
        "wst": _weights(wim, wom, wir, wor, wf1, wf2),
        "x_in": np.ascontiguousarray(xcat.T.reshape(KT, P, T).transpose(1, 0, 2)),
        "cols": _columns(gains, sinks), "trig": _trig(), "mats": _matrices(),
        "pmask": pm, "dmask": dm, "rmask": rm, "qkdec": dec, "kcache": kc, "vcache": vc,
        "state": np.ascontiguousarray(st[0]),
    }
    outs = {
        "x_out": (P, KT, T), "k_out": (P, 4 * NBR, T), "v_out": (P, 4 * NG + 1, T),
        "pstate_out": (NHR, DK, DV), "sstate_out": (NB, NHR, DK, DV),
    }
    nc = _bacc.Bacc("TRN2", target_bir_lowering=False, num_devices=1)
    args = [nc.dram_tensor(n, a.shape, mybir.dt.from_np(a.dtype), kind="ExternalInput").ap() for n, a in ins.items()]
    args += [nc.dram_tensor(n, s, F32, kind="ExternalOutput").ap() for n, s in outs.items()]
    build_program(nc, *args)
    r = _run(nc, [ins], core_ids=[0]).results[0]

    xt = np.asarray(r["x_out"]).transpose(2, 1, 0).reshape(T, D)
    k = np.asarray(r["k_out"]).reshape(4, HALF, NBR, 2, 2, T).transpose(5, 2, 3, 0, 4, 1).reshape(T, NBR, NH, HD)
    v = np.asarray(r["v_out"]).transpose(2, 1, 0).reshape(T, (4 * NG + 1) * P)
    va = v[:, :4 * NG * P].reshape(T, NG, NH, HD)
    vb = v[:, 4 * NG * P:].reshape(T, 2, HD)
    rows = []
    for g in range(NG):
        kv = np.stack([k[:, g], va[:, g]], axis=1)
        rows += [kv[SEQ - min(WINS[g], SEQ):SEQ][None, None], kv[SEQ:].reshape(1, NB, NT, 2, NH, HD)]
    kv = np.stack([k[:, NG, ::4], vb], axis=1)
    rows += [kv[SEQ - P:SEQ][None, None], kv[SEQ:].reshape(1, NB, NT, 2, 2, HD)]
    return (xt[:SEQ][None], xt[SEQ:].reshape(NB, NT, D), *[np.ascontiguousarray(a) for a in rows],
            np.asarray(r["pstate_out"])[None, None], np.asarray(r["sstate_out"])[None])
```
